# Optimizing a Trainium2 kernel written in Bass

```python
import math
import jax, jax.numpy as jnp
from jax import lax
import numpy as np

D_MODEL = 1024
BATCH = 1
SEQ = 512
DEPTH = 2
DEC_BATCH = 8
DEC_SEQ = 1
PAST_LEN = 1024
PAGE_SIZE = 128

N_A_LAYERS = (DEPTH + 1) // 2
N_C_LAYERS = DEPTH // 2
EPS = 1e-6
CONV_W = 4
CHUNK = 64
Q_BLOCK = 128
GDN_HEADS = 4
GDN_DK = 128
GDN_DV = 128
GDN_QK = GDN_HEADS * GDN_DK
GDN_VW = GDN_HEADS * GDN_DV
GDN_CONV_CH = 2 * GDN_QK + GDN_VW
SSM_HEADS = 8
SSM_P = 64
SSM_N = 128
SSM_GROUPS = 2
SSM_INNER = SSM_HEADS * SSM_P
SSM_BC = SSM_GROUPS * SSM_N
SSM_CONV_CH = SSM_INNER + 2 * SSM_BC
IN_A_WIDTHS = (GDN_CONV_CH, GDN_VW, GDN_HEADS, GDN_HEADS, SSM_INNER, SSM_CONV_CH, SSM_HEADS)
IN_A = sum(IN_A_WIDTHS)
MIX_A = GDN_VW + SSM_INNER
MLA_HEADS = 16
Q_LORA = 512
KV_LORA = 256
QK_NOPE = 64
QK_ROPE = 32
QK_HEAD = QK_NOPE + QK_ROPE
V_HEAD = 64
MLA_IN = Q_LORA + KV_LORA + QK_ROPE
MLA_ROW = KV_LORA + QK_ROPE + MLA_HEADS
ROPE_THETA = 10000.0
D_FF = -(-8 * D_MODEL // (3 * 256)) * 256

kernel_name = 'hybrid_gdn_ssd_mla_decoder_step'

def rms_norm(x, g):
    xf = x.astype(jnp.float32)
    y = xf * lax.rsqrt(jnp.mean(xf * xf, axis=-1, keepdims=True) + EPS)
    return (y * g.astype(jnp.float32)).astype(x.dtype)

def l2_normalize(x):
    xf = x.astype(jnp.float32)
    return xf * lax.rsqrt(jnp.sum(xf * xf, axis=-1, keepdims=True) + EPS)

def rope(x, pos):
    half = x.shape[-1] // 2
    inv_freq = ROPE_THETA ** (-jnp.arange(half, dtype=jnp.float32) / half)
    ang = pos[:, None] * inv_freq[None, :]
    shape = (1, pos.shape[0]) + (1,) * (x.ndim - 3) + (half,)
    cos, sin = jnp.cos(ang).reshape(shape), jnp.sin(ang).reshape(shape)
    x1, x2 = x[..., :half], x[..., half:]
    return jnp.concatenate([x1 * cos - x2 * sin, x2 * cos + x1 * sin], axis=-1)

def causal_conv(x, prev, w):
    T = x.shape[1]
    xp = jnp.concatenate([prev.astype(x.dtype), x], axis=1)
    y = sum(w[i] * xp[:, i:i + T] for i in range(CONV_W))
    return y, xp[:, xp.shape[1] - (CONV_W - 1):]

def to_chunks(a, chunk):
    B, T = a.shape[:2]
    return jnp.moveaxis(a.reshape((B, T // chunk, chunk) + a.shape[2:]), 1, 0)

def from_chunks(a):
    n, B, C = a.shape[:3]
    return jnp.moveaxis(a, 0, 1).reshape((B, n * C) + a.shape[3:])

def gated_delta_chunked(q, k, v, g, beta, S0, chunk):
    f32 = jnp.float32
    incl = jnp.tril(jnp.ones((chunk, chunk), bool))
    strict = jnp.tril(jnp.ones((chunk, chunk), bool), -1)
    eye = jnp.eye(chunk, dtype=f32)
    dv = v.shape[-1]

    def step(S, inp):
        qi, ki, vi, gi, bi = (jnp.swapaxes(a.astype(f32), 1, 2) for a in inp)
        cum = jnp.cumsum(gi, axis=-1)
        decay = jnp.exp(jnp.where(incl, cum[..., :, None] - cum[..., None, :], -jnp.inf))
        kb = ki * bi[..., None]
        lower = jnp.where(strict, jnp.einsum('bhid,bhjd->bhij', kb, ki) * decay, 0.0)
        rhs = jnp.concatenate([vi * bi[..., None], kb * jnp.exp(cum)[..., None]], axis=-1)
        sol = lax.linalg.triangular_solve(eye + lower, rhs, left_side=True, lower=True,
                                          unit_diagonal=True)
        u, w = sol[..., :dv], sol[..., dv:]
        v_new = u - w @ S
        attn = jnp.einsum('bhid,bhjd->bhij', qi, ki) * decay
        o = (qi * jnp.exp(cum)[..., None]) @ S + attn @ v_new
        last = cum[..., -1:]
        S = S * jnp.exp(last)[..., None] + jnp.einsum(
            'bhjd,bhjv->bhdv', ki * jnp.exp(last - cum)[..., None], v_new)
        return S, jnp.swapaxes(o, 1, 2)

    S, o = lax.scan(step, S0.astype(f32), tuple(to_chunks(a, chunk) for a in (q, k, v, g, beta)))
    return from_chunks(o), S

def ssd_chunked(x, dt, A, Bh, Ch, h0, chunk):
    f32 = jnp.float32
    incl = jnp.tril(jnp.ones((chunk, chunk), bool))
    la = dt * A
    xdt = x.astype(f32) * dt[..., None]

    def step(h, inp):
        xi, lai, bi, ci = inp
        cum = jnp.cumsum(lai, axis=1)
        cum_h = jnp.swapaxes(cum, 1, 2)
        seg = jnp.exp(jnp.where(incl, cum_h[..., :, None] - cum_h[..., None, :], -jnp.inf))
        scores = jnp.einsum('bihn,bjhn->bhij', ci, bi) * seg
        y = (jnp.einsum('bhij,bjhp->bihp', scores, xi)
             + jnp.einsum('bihn,bhpn->bihp', ci, h) * jnp.exp(cum)[..., None])
        last = cum[:, -1:]
        h = h * jnp.exp(last[:, 0])[..., None, None] + jnp.einsum(
            'bjhn,bjhp->bhpn', bi * jnp.exp(last - cum)[..., None], xi)
        return h, y

    h, y = lax.scan(step, h0.astype(f32),
                    tuple(to_chunks(a, chunk) for a in (xdt, la, Bh.astype(f32), Ch.astype(f32))))
    return from_chunks(y), h

def hybrid_layer(x, S0, gconv0, h0, sconv0, chunk, norm_g, w_in, conv_gdn_w, gdn_A_log,
                 gdn_dt_bias, gdn_norm, conv_ssm_w, conv_ssm_b, ssm_A_log, ssm_dt_bias, ssm_D,
                 ssm_norm, w_out):
    B, T, _ = x.shape
    f32 = jnp.float32
    proj = rms_norm(x, norm_g) @ w_in
    g_qkv, g_z, g_a, g_b, s_z, s_xbc, s_dt = jnp.split(
        proj, np.cumsum(IN_A_WIDTHS)[:-1].tolist(), axis=-1)
    qkv, gdn_conv = causal_conv(g_qkv, gconv0, conv_gdn_w)
    q, k, v = jnp.split(jax.nn.silu(qkv), [GDN_QK, 2 * GDN_QK], axis=-1)
    q = l2_normalize(q.reshape(B, T, GDN_HEADS, GDN_DK)) * GDN_DK ** -0.5
    k = l2_normalize(k.reshape(B, T, GDN_HEADS, GDN_DK))
    v = v.reshape(B, T, GDN_HEADS, GDN_DV)
    beta = jax.nn.sigmoid(g_b.astype(f32))
    g = -jnp.exp(gdn_A_log.astype(f32)) * jax.nn.softplus(g_a.astype(f32) + gdn_dt_bias)
    o, S = gated_delta_chunked(q, k, v, g, beta, S0, chunk)
    o = rms_norm(o, gdn_norm) * jax.nn.silu(g_z.reshape(B, T, GDN_HEADS, GDN_DV).astype(f32))
    xbc, ssm_conv = causal_conv(s_xbc, sconv0, conv_ssm_w)
    xs, bm, cm = jnp.split(jax.nn.silu(xbc + conv_ssm_b), [SSM_INNER, SSM_INNER + SSM_BC], axis=-1)
    xs = xs.reshape(B, T, SSM_HEADS, SSM_P)
    rep = SSM_HEADS // SSM_GROUPS
    bh = jnp.repeat(bm.reshape(B, T, SSM_GROUPS, SSM_N), rep, axis=2)
    ch = jnp.repeat(cm.reshape(B, T, SSM_GROUPS, SSM_N), rep, axis=2)
    dt = jax.nn.softplus(s_dt.astype(f32) + ssm_dt_bias)
    y, h = ssd_chunked(xs, dt, -jnp.exp(ssm_A_log.astype(f32)), bh, ch, h0, chunk)
    y = (y + ssm_D[:, None] * xs).reshape(B, T, SSM_INNER) * jax.nn.silu(s_z.astype(f32))
    y = rms_norm(y.reshape(B, T, SSM_GROUPS, SSM_INNER // SSM_GROUPS),
                 ssm_norm.reshape(SSM_GROUPS, -1)).reshape(B, T, SSM_INNER)
    mix = jnp.concatenate([o.reshape(B, T, GDN_VW), y], axis=-1).astype(x.dtype) @ w_out
    return x + mix, (S, gdn_conv, h, ssm_conv)

def causal_block_attention(q, k, v):
    B, T, H, Dq = q.shape
    nb = T // Q_BLOCK
    q_blocks = jnp.moveaxis(q.reshape(B, nb, Q_BLOCK, H, Dq), 1, 0)
    k_pos = jnp.arange(T)
    scale = Dq ** -0.5

    def attend(args):
        qb, start = args
        s = jnp.einsum('bqhd,bkhd->bhqk', qb, k).astype(jnp.float32) * scale
        q_pos = start + jnp.arange(Q_BLOCK)
        s = jnp.where(k_pos[None, :] <= q_pos[:, None], s, -jnp.inf)
        return jnp.einsum('bhqk,bkhd->bqhd', jax.nn.softmax(s, axis=-1), v)

    o = lax.map(attend, (q_blocks, jnp.arange(nb) * Q_BLOCK))
    return jnp.moveaxis(o, 0, 1).reshape(B, T, H, v.shape[-1])

def latent_scores(qa, q_rope, rows):
    c, kr, inv_r = jnp.split(rows, [KV_LORA, KV_LORA + QK_ROPE], axis=-1)
    s = (jnp.einsum('bthc,bsc->bhts', qa, c).astype(jnp.float32)
         + jnp.einsum('bthr,bsr->bhts', q_rope, kr).astype(jnp.float32))
    return s * jnp.swapaxes(inv_r, 1, 2)[:, :, None, :].astype(jnp.float32) * QK_HEAD ** -0.5

def mla_layer(x, pos, past, norm_g, w_in, q_a_norm, kv_a_norm, w_uq, w_uk, w_uv, q_norm, k_norm,
              w_out):
    B, T, _ = x.shape
    f32 = jnp.float32
    cq, ckv, kr = jnp.split(rms_norm(x, norm_g) @ w_in, [Q_LORA, Q_LORA + KV_LORA], axis=-1)
    q = rms_norm((rms_norm(cq, q_a_norm) @ w_uq).reshape(B, T, MLA_HEADS, QK_HEAD), q_norm)
    q_nope, q_rope = q[..., :QK_NOPE], rope(q[..., QK_NOPE:], pos)
    c = rms_norm(ckv, kv_a_norm)
    k_nope = jnp.einsum('btc,chd->bthd', c, w_uk)
    krf = kr.astype(f32)
    ssq = jnp.sum(jnp.square(k_nope.astype(f32)), axis=-1) + jnp.sum(krf * krf, axis=-1)[..., None]
    inv_r = lax.rsqrt(ssq / QK_HEAD + EPS)
    kr_rot = rope(kr * k_norm[QK_NOPE:], pos)
    rows = jnp.concatenate([c, kr_rot, inv_r.astype(c.dtype)], axis=-1)
    if past is None:
        k = jnp.concatenate([k_nope * k_norm[:QK_NOPE],
                             jnp.broadcast_to(kr_rot[:, :, None, :], (B, T, MLA_HEADS, QK_ROPE))],
                            axis=-1) * inv_r[..., None]
        v = jnp.einsum('btc,chv->bthv', c, w_uv)
        o = causal_block_attention(jnp.concatenate([q_nope, q_rope], axis=-1), k, v)
    else:
        qa = jnp.einsum('bthd,chd->bthc', q_nope * k_norm[:QK_NOPE], w_uk)
        s_past = latent_scores(qa, q_rope, past)
        s_new = jnp.where(jnp.tril(jnp.ones((T, T), bool)), latent_scores(qa, q_rope, rows), -jnp.inf)
        p = jax.nn.softmax(jnp.concatenate([s_past, s_new], axis=-1), axis=-1)
        n_past = past.shape[1]
        ctx = (jnp.einsum('bhts,bsc->bthc', p[..., :n_past], past[..., :KV_LORA].astype(f32))
               + jnp.einsum('bhts,bsc->bthc', p[..., n_past:], c.astype(f32)))
        o = jnp.einsum('bthc,chv->bthv', ctx, w_uv)
    y = o.reshape(B, T, MLA_HEADS * V_HEAD).astype(x.dtype) @ w_out
    return x + y, rows

def swiglu_ffn(x, norm_g, w_gate_up, w_down):
    gate, up = jnp.split(rms_norm(x, norm_g) @ w_gate_up, 2, axis=-1)
    return x + (jax.nn.silu(gate) * up) @ w_down

def trunk(x, pos, gdn_S, gdn_conv, ssm_h, ssm_conv, cache_mla, page_table, wa, wc, wf):
    T = x.shape[1]
    chunk = CHUNK if T % CHUNK == 0 else T
    new_S, new_gc, new_h, new_sc, new_rows = [], [], [], [], []
    norm_ffn, w_gate_up, w_down = wf
    for layer in range(DEPTH):
        j = layer // 2
        if layer % 2 == 0:
            x, (S, gc, h, sc) = hybrid_layer(x, gdn_S[j], gdn_conv[j], ssm_h[j], ssm_conv[j], chunk,
                                             *[w[j] for w in wa])
            new_S.append(S)
            new_gc.append(gc)
            new_h.append(h)
            new_sc.append(sc)
        else:
            past = None if cache_mla is None else cache_mla[j, page_table].reshape(
                x.shape[0], -1, MLA_ROW)
            x, rows = mla_layer(x, pos, past, *[w[j] for w in wc])
            new_rows.append(rows)
        x = swiglu_ffn(x, norm_ffn[layer], w_gate_up[layer], w_down[layer])
    return (x, jnp.stack(new_S), jnp.stack(new_gc), jnp.stack(new_h), jnp.stack(new_sc),
            jnp.stack(new_rows))

def setup_inputs(seed: int = 0) -> dict:
    keys = iter(jax.random.split(jax.random.key(seed), 64))
    f32 = jnp.float32

    def normal(shape, scale=1.0):
        return jax.random.normal(next(keys), shape, f32) * scale

    def uniform(shape, lo, hi):
        return jax.random.uniform(next(keys), shape, f32, lo, hi)

    def gain(shape):
        return 1.0 + normal(shape, 0.02)

    def dt_bias(shape):
        dt = jnp.exp(uniform(shape, math.log(1e-3), math.log(1e-1)))
        return dt + jnp.log(-jnp.expm1(-dt))

    na, nc = N_A_LAYERS, N_C_LAYERS
    n_pages = PAST_LEN // PAGE_SIZE
    n_pool = (5 * DEC_BATCH * n_pages) // 4
    x_prompt = normal((BATCH, SEQ, D_MODEL))
    x_sample = normal((DEC_BATCH, DEC_SEQ, D_MODEL))
    state_gdn = normal((na, DEC_BATCH, GDN_HEADS, GDN_DK, GDN_DV), 0.1)
    state_gdn_conv = normal((na, DEC_BATCH, CONV_W - 1, GDN_CONV_CH))
    state_ssm = normal((na, DEC_BATCH, SSM_HEADS, SSM_P, SSM_N), 0.1)
    state_ssm_conv = normal((na, DEC_BATCH, CONV_W - 1, SSM_CONV_CH))
    cache_mla = jnp.concatenate([normal((nc, n_pool, PAGE_SIZE, KV_LORA)),
                                 normal((nc, n_pool, PAGE_SIZE, QK_ROPE)),
                                 uniform((nc, n_pool, PAGE_SIZE, MLA_HEADS), 0.7, 1.3)], axis=-1)
    page_table = jax.random.permutation(next(keys), n_pool)[:DEC_BATCH * n_pages].reshape(
        DEC_BATCH, n_pages).astype(jnp.int32)
    return {
        'x_prompt': x_prompt,
        'x_sample': x_sample,
        'state_gdn': state_gdn,
        'state_gdn_conv': state_gdn_conv,
        'state_ssm': state_ssm,
        'state_ssm_conv': state_ssm_conv,
        'cache_mla': cache_mla,
        'page_table': page_table,
        'norm_mix_a': gain((na, D_MODEL)),
        'w_in_a': normal((na, D_MODEL, IN_A), D_MODEL ** -0.5),
        'conv_gdn_w': normal((na, CONV_W, GDN_CONV_CH), CONV_W ** -0.5),
        'gdn_A_log': jnp.log(uniform((na, GDN_HEADS), 1.0, 16.0)),
        'gdn_dt_bias': dt_bias((na, GDN_HEADS)),
        'gdn_norm': gain((na, GDN_DV)),
        'conv_ssm_w': normal((na, CONV_W, SSM_CONV_CH), CONV_W ** -0.5),
        'conv_ssm_b': normal((na, SSM_CONV_CH), 0.1),
        'ssm_A_log': jnp.log(uniform((na, SSM_HEADS), 1.0, 16.0)),
        'ssm_dt_bias': dt_bias((na, SSM_HEADS)),
        'ssm_D': gain((na, SSM_HEADS)),
        'ssm_norm': gain((na, SSM_INNER)),
        'w_out_a': normal((na, MIX_A, D_MODEL), MIX_A ** -0.5),
        'norm_mix_c': gain((nc, D_MODEL)),
        'w_in_c': normal((nc, D_MODEL, MLA_IN), D_MODEL ** -0.5),
        'q_a_norm': gain((nc, Q_LORA)),
        'kv_a_norm': gain((nc, KV_LORA)),
        'w_uq': normal((nc, Q_LORA, MLA_HEADS * QK_HEAD), Q_LORA ** -0.5),
        'w_uk': normal((nc, KV_LORA, MLA_HEADS, QK_NOPE), KV_LORA ** -0.5),
        'w_uv': normal((nc, KV_LORA, MLA_HEADS, V_HEAD), KV_LORA ** -0.5),
        'q_norm': gain((nc, QK_HEAD)),
        'k_norm': gain((nc, QK_HEAD)),
        'w_out_c': normal((nc, MLA_HEADS * V_HEAD, D_MODEL), (MLA_HEADS * V_HEAD) ** -0.5),
        'norm_ffn': gain((DEPTH, D_MODEL)),
        'w_gate_up': normal((DEPTH, D_MODEL, 2 * D_FF), D_MODEL ** -0.5),
        'w_down': normal((DEPTH, D_FF, D_MODEL), D_FF ** -0.5),
    }

def reference(x_prompt, x_sample, state_gdn, state_gdn_conv, state_ssm, state_ssm_conv, cache_mla,
              page_table, norm_mix_a, w_in_a, conv_gdn_w, gdn_A_log, gdn_dt_bias, gdn_norm,
              conv_ssm_w, conv_ssm_b, ssm_A_log, ssm_dt_bias, ssm_D, ssm_norm, w_out_a,
              norm_mix_c, w_in_c, q_a_norm, kv_a_norm, w_uq, w_uk, w_uv, q_norm, k_norm, w_out_c,
              norm_ffn, w_gate_up, w_down):
    wa = (norm_mix_a, w_in_a, conv_gdn_w, gdn_A_log, gdn_dt_bias, gdn_norm, conv_ssm_w,
          conv_ssm_b, ssm_A_log, ssm_dt_bias, ssm_D, ssm_norm, w_out_a)
    wc = (norm_mix_c, w_in_c, q_a_norm, kv_a_norm, w_uq, w_uk, w_uv, q_norm, k_norm, w_out_c)
    wf = (norm_ffn, w_gate_up, w_down)
    b, t, _ = x_prompt.shape
    zero_S = jnp.zeros((N_A_LAYERS, b, GDN_HEADS, GDN_DK, GDN_DV), jnp.float32)
    zero_gc = jnp.zeros((N_A_LAYERS, b, CONV_W - 1, GDN_CONV_CH), x_prompt.dtype)
    zero_h = jnp.zeros((N_A_LAYERS, b, SSM_HEADS, SSM_P, SSM_N), jnp.float32)
    zero_sc = jnp.zeros((N_A_LAYERS, b, CONV_W - 1, SSM_CONV_CH), x_prompt.dtype)
    y_prompt, p_gdn, p_gdn_conv, p_ssm, p_ssm_conv, p_mla_rows = trunk(
        x_prompt, jnp.arange(t, dtype=jnp.float32), zero_S, zero_gc, zero_h, zero_sc, None, None,
        wa, wc, wf)
    past_len = page_table.shape[1] * PAGE_SIZE
    pos_s = past_len + jnp.arange(x_sample.shape[1], dtype=jnp.float32)
    y_sample, s_gdn, s_gdn_conv, s_ssm, s_ssm_conv, s_mla_rows = trunk(
        x_sample, pos_s, state_gdn, state_gdn_conv, state_ssm, state_ssm_conv, cache_mla,
        page_table, wa, wc, wf)
    return (y_prompt, y_sample, p_gdn, p_gdn_conv, p_ssm, p_ssm_conv, p_mla_rows,
            s_gdn, s_gdn_conv, s_ssm, s_ssm_conv, s_mla_rows)


_drawn_inputs = setup_inputs


def setup_inputs(seed=0):
    import zlib

    import numpy as np

    out = dict(_drawn_inputs(seed))
    spreads = {}
    factors = {'gdn_norm': 7.36,
     'ssm_D': 8.0,
     'ssm_norm': 4.444,
     'norm_mix_c': 2.974,
     'q_a_norm': 8.0,
     'kv_a_norm': 3.307,
     'q_norm': 8.0,
     'k_norm': 8.0,
     'norm_ffn': 3.356}
    for name, (base, spread) in spreads.items():
        noise = np.random.default_rng([zlib.crc32(name.encode()), seed]).standard_normal(out[name].shape)
        drawn = base * np.exp(spread * noise) if base else spread * noise
        out[name] = __import__('jax').numpy.asarray(drawn.astype(out[name].dtype))
    for name, factor in factors.items():
        out[name] = (out[name] * factor).astype(out[name].dtype)
    return out
```

```python
import numpy as np
import concourse.bass as bass
from concourse import mybir
from contextlib import ExitStack

F32 = mybir.dt.float32
ACT = mybir.ActivationFunctionType
ALU = mybir.AluOpType
AX = mybir.AxisListType

T, NS = 512, 8
TOK = T + NS
HALF = TOK // 2
D, DFF = 1024, 2816
KD, KF = D // 128, DFF // 128
EPS = 1e-6
GH, SH, SG = 4, 8, 2
NCH = T // 128
NDEC = GH + SH
NGATE = NDEC + GH
NCONV = 20
LV = 6
MH, NOPE, RD, QH, VH = 16, 64, 32, 96, 64
NPG, NPOOL, MROW = 8, 80, 304
PSCALE = QH ** -0.5
NEG = -1e30
SLOT = 11 * 128

TQ, TK, TV, TX, TB, TC, TZ, TSZ = 0, 4, 8, 12, 16, 18, 20, 24

R_L2, R_MIX, R_CQ, R_KV, R_KEY, R_HEAD = 1, 9, 17, 18, 19, 20
R_NORM = (0, 15, 16, R_HEAD + MH)
STAGES = [('proj', 7, 28), ('outa', 2, 8), ('gu0', 11, 44), ('dn0', 4, 8), ('inc', 2, 14), ('uq', 4, 0),
          ('outc', 2, 8), ('gu1', 11, 44), ('dn1', 4, 8)]
TURNS = {n: g for n, g, _ in STAGES}
GBASE = {n: sum(g for _, g, _ in STAGES[:k]) for k, (n, _, _) in enumerate(STAGES)}
TBASE = {n: sum(t for _, _, t in STAGES[:k]) // 2 for k, (n, _, _) in enumerate(STAGES)}

CONSTS = ['ident', 'triu', 'decaymask', 'causal', 'ones', 'ones_d', 'ones_128', 'ones_256', 'ones_512',
          'ones_96', 'rot96', 'rot32', 'headsel'] + [f'inv{l}' for l in range(LV + 1)]
C_GDN, C_D, C_SSM, C_QA, C_KVA, C_QN, C_KR, C_KN, C_EPS, NSMALL = 0, 1, 5, 9, 13, 15, 16, 17, 18, 19
SMALLS = ['w_gate', 'gains', 'convw', 'convb', 'small', 'gatec', 'prev', 'selb']


class Steps:

    def __init__(self, eng, own):
        self.eng, self.own, self.count, self.shift, self.last = eng, own, {}, {}, None

    def __call__(self, ins, sem=None):
        sem = sem or self.own
        ins.then_inc(sem, 1)
        self.count[sem.name] = self.count.get(sem.name, 0) + 1
        self.last = sem

    def sync(self):
        self.eng.wait_ge(self.last, self.shift.get(self.last.name, 0) + self.count[self.last.name])

    def loop(self, first, last, body, per):
        before = dict(self.count)
        with self.eng.Fori(first, last) as i:
            self.shift = {s.name: (i - first) * n for s, n in per}
            body(i)
        for s, n in per:
            made = self.count.get(s.name, 0) - before.get(s.name, 0)
            assert made == n, (s.name, made, n)
            self.count[s.name] = before.get(s.name, 0) + (last - first) * n
        looped = [s.name for s, _ in per]
        assert all(k in looped or v == before.get(k, 0) for k, v in self.count.items()), self.count
        self.shift = {}


def build(nc, A, O):
    ctx = ExitStack()
    with ctx:
        def sb(name, *shape):
            return ctx.enter_context(nc.sbuf_tensor(name, list(shape), F32))

        def sem(name):
            return ctx.enter_context(nc.semaphore(name))

        PS = ctx.enter_context(nc.psum_tensor("PS", [128, 8, 512], F32))
        xres, xn, mix = sb("xres", 128, KD, TOK), sb("xn", 128, KD, TOK), sb("mix", 128, KD, TOK)
        hid = sb("hid", 128, 28, TOK)
        wring = [sb(f"wring{u}", 128, SLOT) for u in range(4)]
        cst = sb("cst", 128, len(CONSTS), 128)
        rinv, sqsum, sq = sb("rinv", 128, 2, TOK), sb("sqsum", 128, TOK), sb("sq", 128, 2, TOK)
        selb = sb("selb", 8, 8, 128)
        gains, convw, convb = sb("gains", 128, 4, KD), sb("convw", 128, NCONV, 4), sb("convb", 128, NCONV)
        small, gatec = sb("small", 128, NSMALL), sb("gatec", 128, NGATE + NDEC)
        prev, convout_p, convout_s = sb("prev", 128, NCONV, 3, NS), sb("convout_p", 128, NCONV, 3), sb("convout_s", 128, NCONV, NS)
        wgate = sb("wgate", 128, KD, NGATE)
        graw, gabs, gexp, gone, grec, gln, gsp = (sb(n, 128, 5, NGATE) for n in
                                                  ("graw", "gabs", "gexp", "gone", "grec", "gln", "gsp"))
        la, nega = sb("la", 128, 5, NDEC), sb("nega", 128, NDEC)
        cumt, ecumt, bec = sb("cumt", 128, NCH, NDEC), sb("ecumt", 128, NCH, NDEC), sb("bec", 128, NCH, GH)
        beta, gdt = grec[:, :, NDEC:NGATE], gsp[:, :, GH:NDEC]
        ptab = ctx.enter_context(nc.sbuf_tensor("ptab", [1, NS * NPG], mybir.dt.int32))
        WORK = 12480
        work = sb("work", 128, WORK)
        at = [0]

        def take(*shape, rows=128):
            n = int(np.prod(shape))
            v = work[0:rows, at[0]:at[0] + n]
            at[0] += n
            assert at[0] <= WORK, at[0]
            if len(shape) == 2:
                return v.rearrange("p (a b) -> p a b", b=shape[1])
            if len(shape) == 3:
                return v.rearrange("p (a b c) -> p a b c", b=shape[1], c=shape[2])
            return v

        def const(name):
            return cst[:, CONSTS.index(name), :]

        def two(ap):
            return ap.rearrange("p (a t) -> p a t", a=2)

        def bank2(b, rows=128):
            return PS[0:rows, b:b + 2, 0:HALF]

        def by(ap, n):
            return ap.rearrange("p (h x) -> p h x", h=n)

        def over(ap, n):
            return ap.unsqueeze(2).broadcast_to([ap.shape[0], ap.shape[1], n])

        def across(ap, n):
            return ap.unsqueeze(1).broadcast_to([ap.shape[0], n, ap.shape[1]])

        ident = const('ident')

        raw = take(2, 3 + TOK)
        cacc = take(2, TOK)
        at[0] = 0
        arg, dect = xn[:, 0:3, 0:512], xn[:, 3:6, 0:512]
        bm, lt = xn[:, 6, 0:512], xn[:, 7, 0:512]
        xdt, xde = sq[:, 0, 0:512], sq[:, 1, 0:512]
        ecum = take(3, 512)
        attnt, kbe, kdec, vb, xinv, xinvt, yinv, wt, vnew, qe, sgdn, hssd = (take(512) for _ in range(12))
        mt = take(LV + 1, 512)
        scoret = take(2, 512)
        ce = (rinv[:, 0, 0:512], sqsum[:, 0:512])
        btm, kd, kdarg = rinv[:, 1, 0:256], take(NDEC), take(NDEC)
        at[0] = 0
        s0, h0 = take(GH, NS, 128), take(NS, 512)
        vals, valx, valb, ab = take(24), take(24, NS), take(24, NS), take(NDEC, NS)
        rhs2, vnt, qkp, vrow = take(GH * NS, 2), take(GH, NS), take(GH, NS), take(512)
        kb8, bcp, apx = take(GH, NS), take(SG, NS), take(4, 2, NS)
        xds, ysm, yt2, xrow, supd = take(4, NS), take(4, NS), take(4, NS), take(512), take(2, 512)
        sgate = work[:, WORK - 2 * TOK:WORK].rearrange("p (a t) -> p a t", a=2)
        at[0] = 0
        krrot, invr, cosg, qs = take(TOK, rows=32), take(TOK, rows=16), take(TOK), take(MH, NS)
        wkr, rotg, rotk = take(KD, RD), take(QH), take(RD, rows=32)
        vol = at[0]
        krraw, krg, krsq, krt = (work[0:32, vol + i * TOK:vol + (i + 1) * TOK] for i in range(4))
        qraw, qsq, qt1, qt2 = (take(TOK) for _ in range(4))
        qhd, khd, pm, ptsb, otm = take(2, TOK), take(2, T), take(4, 512), take(1280), take(4, 128)
        invm = take(2, T, rows=16)
        mx, nb, den, rden = (take(4) for _ in range(4))
        cqn, clat, knope, rope = hid[:, 0:4], hid[:, 4:6], hid[:, 6:14], hid[:, 14:18]
        hflat = hid[:, 18:28].rearrange("p a t -> p (a t)")
        wuv = hflat[:, 0:2048].rearrange("p (k n) -> p k n", k=2)
        wukt = hflat[:, 2048:4096].rearrange("p (h c) -> p h c", h=8)
        vtok = xn[:, :, :].rearrange("p a t -> p (a t)")[:, 0:4096].rearrange("p (a n) -> p a n", a=4)
        hs = [4096]

        def htake(a, b, rows=128):
            v = hflat[0:rows, hs[0]:hs[0] + a * b].rearrange("p (a b) -> p a b", b=b)
            hs[0] += a * b
            assert hs[0] <= 5200
            return v

        qkn, sp, mxp = htake(8, NS), htake(NPG, 16), htake(1, 16)
        qa = hflat[:, hs[0]:hs[0] + 256].rearrange("p (k h b) -> p k h b", k=2, b=NS); hs[0] += 256
        ctxt = hflat[:, hs[0]:hs[0] + 256].rearrange("p (k h b) -> p k h b", k=2, b=NS); hs[0] += 256
        qr, snew, diag2 = htake(MH, NS, rows=32), htake(1, NS, rows=16)[:, 0, :], htake(2, 16, rows=16)
        m16, sdif, pn, pnb, dsum, ctmp = (htake(1, 1, rows=16)[:, 0, :], htake(1, 1, rows=16)[:, 0, :],
                                          htake(1, 1, rows=16)[:, 0, :], htake(1, 16), htake(1, 16), htake(2, 16))
        pagebuf = []
        for flat in (hid[:, 6:18].rearrange("p a t -> p (a t)"), work[:, vol:vol + 5504]):
            pagebuf.append((flat[:, 0:NPG * MROW].rearrange("p (g r) -> p g r", g=NPG),
                            flat[:, 2432:2432 + 2048].rearrange("p (g k s) -> p g k s", g=NPG, k=2),
                            flat[0:32, 4480:4480 + 1024].rearrange("p (g s) -> p g s", g=NPG)))

        x_loaded, c_loaded, g_loaded = sem("x_loaded"), sem("c_loaded"), sem("g_loaded")
        w_loaded = [sem(f"w_loaded{u}") for u in range(4)]
        gemm_ready = [sem(f"gemm_ready{p}") for p in range(2)]
        tile_taken = [sem(f"tile_taken{p}") for p in range(2)]
        pages_loaded = [sem(f"pages_loaded{p}") for p in range(2)]

        names = """sq_ready sq_added sq_zeroed ssq_mm xn_ready gates_mm gprep_ready gact_ready la_ready cum_mm
            cumt_ready ecumt_ready raw_ready raw_zeroed conv_done silu_done l2sq_ready l2_mm l2_done
            cumB_mm arg_ready ecum_ready dect_ready kd_ready betaB_mm bm_ready kk_mm qk_mm ktm_mm vtm_mm
            lt_ready attn_ready kvs_ready mt_ready xinit_mm xinit_ready y_mm y_ready p_mm pt_mm x_ready vnew_mm
            w_mm w_ready qe_ready vnew_ready ot_mm ot_taken kv_mm s_ready bc_mm xtm_mm btm_mm score_ready
            xdt_ready btm_ready ce_ready yt_mm yt_taken hup_mm h_ready state_zero rec_stored st_loaded
            sprep_ready spread_mm valb_ready spread_ready rhs2_ready sv_mm vnt_ready qks_mm row_mm row_ready
            sel_mm sel_taken bcs_mm y0_mm xds_ready hsel_mm hsel_taken s_decayed osq_ready osq_mm
            mix_ready dve_own kr_mm kr_raw krsq_ready m_loaded cq_sq cq_mm cq_ready rot_ready krot_mm krot_ready
            kn_sq kn_mm kn_sum ln_ready rinv_ready v_mm v_ready q_mm qsq_ready qss_mm qrot_mm qh_ready
            invm_ready invb_mm k_ready s_mm nb_ready p_ready pt2_mm pt2_taken o_mm otm_ready ott_mm omix_ready
            pt_loaded gk_ready qa_mm qa_ready sn_mm snew_ready sc_mm smx_ready smt_mm sdif_ready pn_ready
            sdiag_ready sbc_mm ssub_ready sp_ready ctx_mm ctx_ready so_mm so_ready y_stored out_stored""".split()
        sems = {n: sem(n) for n in names}

        def s(name):
            return sems[name]

        def slot_freed(stage, i, u):
            tb = TBASE[stage]
            if stage in ('dn0', 'dn1'):
                return gemm_ready[u // 2], tb + i + 1
            if stage == 'uq':
                return s('q_mm'), i * 4 + (u + 1)
            if stage == 'inc':
                return gemm_ready[u % 2], tb + (u // 2 + 1 if i == 0 else 3 if u < 2 else 7)
            return gemm_ready[u % 2], tb + i * 2 + (u // 2 + 1)

        block = ctx.enter_context(nc.Block())

        @block.sync
        def _(sp_):
            for k in range(2):
                sp_.dma_start(xres[:, 4 * k:4 * k + 4], A['x'][:, 4 * k:4 * k + 4]).then_inc(x_loaded, 16)
            sp_.dma_start(ptab[:, :], A['page_table']).then_inc(s('pt_loaded'), 16)

            def load(stage, i, u):
                n = KD * 128 if stage not in ('dn0', 'dn1', 'uq') else 4 * QH if stage == 'uq' else SLOT
                sp_.dma_start(wring[u][:, 0:n], A['w_' + stage][i * 4 + u]).then_inc(w_loaded[u], 16)

            def pages():
                sp_.wait_ge(s('pt_loaded'), 16)
                sp_.wait_ge(s('omix_ready'), MH // 2)

                def two_sequences(i, again):
                    for p in range(2):
                        rows_, ct, krt_ = pagebuf[p]
                        if again:
                            sp_.wait_ge(s('ctx_mm'), i * 2 + (p - 1))
                        for g in range(NPG):
                            page = sp_.value_load(ptab[0:1, bass.ds((i * 2 + p) * NPG + g, 1)], min_val=0, max_val=NPOOL - 1)
                            sp_.dma_start(ct[:, g], A['cache_ct'][bass.ds(page, 1)].rearrange("a p k s -> p (a k) s"))\
                                .then_inc(pages_loaded[p], 16)
                            sp_.dma_start(krt_[:, g], A['cache_kt'][bass.ds(page, 1)].rearrange("a p s -> p (a s)"))\
                                .then_inc(pages_loaded[p], 16)
                            sp_.dma_start(rows_[:, g], A['cache'][bass.ds(page, 1)].rearrange("a p r -> p (a r)"))\
                                .then_inc(pages_loaded[p], 16)
                two_sequences(0, False)
                with sp_.Fori(1, NS // 2) as i:
                    two_sequences(i, True)

            before = None
            for stage, turns, _ in STAGES:
                for u in range(4):
                    if before:
                        sp_.wait_ge(*slot_freed(before, TURNS[before] - 1, u))
                    load(stage, 0, u)
                if stage == 'inc':
                    for u in range(4):
                        sp_.wait_ge(*slot_freed(stage, 0, u))
                        load(stage, 1, u)
                else:
                    with sp_.Fori(1, turns) as i:
                        for u in range(4):
                            sp_.wait_ge(*slot_freed(stage, i - 1, u))
                            load(stage, i, u)
                before = stage
                if stage == 'uq':
                    pages()
            for p in range(2):
                sp_.wait_ge(tile_taken[p], TBASE['dn1'] + 4)
            sp_.dma_start(O['y'], xres[:, :, :]).then_inc(s('y_stored'), 16)
            sp_.wait_ge(s('y_stored'), 16)

        @block.gpsimd
        def _(pool):
            pool.dma_start(cst[:, :, :], A['consts']).then_inc(c_loaded, 16)
            for dst, src in zip((wgate, gains, convw, convb, small, gatec, prev, selb), SMALLS):
                pool.dma_start(dst[:], A[src]).then_inc(g_loaded, 16)

            def sum_squares(n):
                if n:
                    pool.wait_ge(s('ssq_mm'), n)
                pool.memset(sqsum[:, :], 0.0).then_inc(s('sq_zeroed'), 1)
                pool.wait_ge(s('sq_zeroed'), n + 1)
                for k in range(KD):
                    pool.wait_ge(s('sq_ready'), 8 * n + k + 1)
                    if n or k:
                        pool.wait_ge(s('sq_added'), 8 * n + k)
                    pool.tensor_tensor(sqsum[:, :], sqsum[:, :], sq[:, k % 2, :], ALU.add).then_inc(s('sq_added'), 1)

            pool.memset(raw[:, 0, 0:3], 0.0)
            pool.memset(raw[:, 1, 0:3], 0.0).then_inc(s('raw_zeroed'), 1)
            sum_squares(0)
            pool.wait_ge(s('silu_done'), NCONV)
            pool.memset(sgdn, 0.0)
            pool.memset(hssd, 0.0).then_inc(s('state_zero'), 1)
            for c in range(NCH):
                pool.wait_ge(s('lt_ready'), c + 1)
                if c:
                    pool.wait_ge(s('x_ready'), LV * c)
                for l in range(LV + 1):
                    pool.tensor_tensor(by(mt[:, l], GH), by(lt, GH), across(const(f'inv{l}'), GH), ALU.mult)\
                        .then_inc(s('mt_ready'), 1)
            pool.wait_ge(s('s_ready'), NCH)
            pool.wait_ge(s('h_ready'), NCH)
            pool.dma_start(O['p_gdn'], sgdn).then_inc(s('rec_stored'), 16)
            pool.dma_start(O['p_ssm'], hssd).then_inc(s('rec_stored'), 16)
            pool.dma_start(O['conv_p'], convout_p[:, :, :]).then_inc(s('out_stored'), 16)
            pool.wait_ge(s('rec_stored'), 32)
            pool.wait_ge(s('ot_taken'), NCH)
            pool.wait_ge(s('yt_taken'), NCH)
            pool.dma_start(s0, A['s_gdn']).then_inc(s('st_loaded'), 16)
            pool.dma_start(h0, A['s_ssm']).then_inc(s('st_loaded'), 16)
            pool.wait_ge(s('spread_ready'), 1)
            pool.wait_ge(s('sv_mm'), 1)
            pool.wait_ge(s('y0_mm'), 1)
            for h in range(GH):
                pool.tensor_tensor(s0[:, h], s0[:, h], over(ab[:, h], 128), ALU.mult).then_inc(s('s_decayed'), 1)
            for b in range(NS):
                pool.tensor_tensor(by(h0[:, b], SH), by(h0[:, b], SH), over(ab[:, GH:, b], 64), ALU.mult)\
                    .then_inc(s('s_decayed'), 1)
            pool.dma_start(O['conv_s'][:, :, 2], convout_s[:, :, :]).then_inc(s('out_stored'), 16)
            pool.dma_start(O['conv_s'][:, :, 0:2], prev[:, :, 1:3]).then_inc(s('out_stored'), 16)
            pool.wait_ge(s('sel_taken'), NS)
            pool.dma_start(O['s_gdn'], s0).then_inc(s('out_stored'), 16)
            pool.wait_ge(s('hsel_taken'), NS)
            pool.dma_start(O['s_ssm'], h0).then_inc(s('out_stored'), 16)
            sum_squares(1)
            sum_squares(2)
            pool.wait_ge(s('out_stored'), 80)
            for dst, src in ((wkr, 'w_kr'), (rope, 'rope'), (wuv, 'w_uv'), (wukt, 'w_ukt')):
                pool.dma_start(dst, A[src]).then_inc(s('m_loaded'), 16)
            pool.wait_ge(s('cq_ready'), 2)
            pool.dma_start(O['rows_c'], clat).then_inc(s('out_stored'), 16)
            pool.wait_ge(s('krot_ready'), 1)
            pool.dma_start(O['rows_k'], krrot).then_inc(s('out_stored'), 16)
            pool.wait_ge(s('rinv_ready'), R_KEY + 1)
            pool.dma_start(O['rows_r'], invr).then_inc(s('out_stored'), 16)
            sum_squares(3)
            pool.wait_ge(s('out_stored'), 128)

        @block.tensor
        def _(pe):
            def mm(out, lhsT, rhs, start=True, stop=True):
                return pe.matmul(out, lhsT, rhs, start=start, stop=stop)

            def both(b, lhsT, rhs, start=True, stop=True):
                for h in range(2):
                    last = mm(PS[0:lhsT.shape[1], b + h, 0:HALF], lhsT, rhs[:, h * HALF:(h + 1) * HALF], start, stop)
                return last

            def gemm(stage, rhs, first=0, last=None):
                def turn(i):
                    for u in range(4):
                        pe.wait_ge(w_loaded[u], i * 16 + 16 * (GBASE[stage] + 1))
                        if stage in ('dn0', 'dn1'):
                            p, q, ks = u // 2, i, 11
                            if u % 2 == 0:
                                pe.wait_ge(tile_taken[p], TBASE[stage] + q)
                        else:
                            p, q, ks = u % 2, i * 2 + u // 2, KD
                            pe.wait_ge(tile_taken[p], TBASE[stage] + q)
                        for k in range(ks):
                            kk = (u % 2) * 11 + k if ks == 11 else k
                            ins = both(2 * p, wring[u][:, k * 128:(k + 1) * 128], rhs(kk), kk == 0,
                                       kk == (KF if ks == 11 else KD) - 1)
                        if ks == KD or u % 2:
                            ins.then_inc(gemm_ready[p], 1)
                last = TURNS[stage] if last is None else last
                if stage == 'proj' and first == 0:
                    turn(0)
                    first = 1
                if last - first > 1:
                    with pe.Fori(first, last) as i:
                        turn(i)
                else:
                    turn(first)

            def norm_sum(n):
                pe.wait_ge(s('sq_added'), 8 * (n + 1))
                both(4, const('ones_d'), sqsum).then_inc(s('ssq_mm'), 1)
                pe.wait_ge(s('xn_ready'), 8 * (n + 1))

            pe.wait_ge(c_loaded, 16)
            pe.wait_ge(g_loaded, 16 * len(SMALLS))
            norm_sum(0)
            for t in range(5):
                for k in range(KD):
                    toks = slice(t * 128, min((t + 1) * 128, TOK))
                    ins = mm(PS[0:toks.stop - toks.start, 6, t * NGATE:(t + 1) * NGATE], xn[:, k, toks], wgate[:, k, :],
                             k == 0, k == KD - 1)
            ins.then_inc(s('gates_mm'), 1)
            gemm('proj', lambda k: xn[:, k, :], 0, 5)
            pe.wait_ge(s('la_ready'), 1)
            for c in range(NCH):
                ins = mm(PS[:, 7, c * NDEC:(c + 1) * NDEC], const('triu'), la[:, c, :])
            ins.then_inc(s('cum_mm'), 1)
            for j in range(8):
                pe.wait_ge(s('l2sq_ready'), j + 1)
                if j >= 2:
                    pe.wait_ge(s('ln_ready'), R_L2 + j - 1)
                if j == 1:
                    pe.wait_ge(s('cumt_ready'), 1)
                both(4 + 2 * (j % 2), const('ones'), sq[:, j % 2, :]).then_inc(s('l2_mm'), 1)
            gemm('proj', lambda k: xn[:, k, :], 5, 7)

            pe.wait_ge(s('cumt_ready'), 1)
            pe.wait_ge(s('l2_done'), 8)
            pe.wait_ge(s('silu_done'), NCONV)
            for p in range(2):
                pe.wait_ge(tile_taken[p], 14)
            pe.wait_ge(s('ln_ready'), R_L2 + 8)
            for c in range(NCH):
                ts = slice(c * 128, (c + 1) * 128)
                if c:
                    pe.wait_ge(s('yt_taken'), c)
                    pe.wait_ge(s('h_ready'), c)
                    pe.wait_ge(s('ot_taken'), c)
                for h in range(NDEC):
                    ins = mm(PS[:, h // 4, (h % 4) * 128:(h % 4 + 1) * 128],
                             la[:, c, h:h + 1].broadcast_to([128, 128]), const('triu'))
                ins.then_inc(s('cumB_mm'), 1)
                if c:
                    pe.wait_ge(s('w_ready'), c)
                for h in range(GH):
                    ins = mm(PS[:, 3, h * 128:(h + 1) * 128], beta[:, c, h:h + 1].broadcast_to([128, 128]), ident)
                ins.then_inc(s('betaB_mm'), 1)
                if c:
                    pe.wait_ge(s('x_ready'), LV * c)
                for h in range(GH):
                    ins = mm(PS[:, 4, h * 128:(h + 1) * 128], hid[:, TK + h, ts], hid[:, TK + h, ts])
                ins.then_inc(s('kk_mm'), 1)
                for h in range(GH):
                    ins = mm(PS[:, 5, h * 128:(h + 1) * 128], hid[:, TK + h, ts], hid[:, TQ + h, ts])
                ins.then_inc(s('qk_mm'), 1)
                if c:
                    pe.wait_ge(s('vnew_ready'), c)
                for h in range(GH):
                    ins = pe.transpose(PS[:, 6, h * 128:(h + 1) * 128], hid[:, TK + h, ts], ident)
                ins.then_inc(s('ktm_mm'), 1)
                if c:
                    pe.wait_ge(s('s_ready'), c)
                for h in range(GH):
                    ins = pe.transpose(PS[:, 7, h * 128:(h + 1) * 128], hid[:, TV + h, ts], ident)
                ins.then_inc(s('vtm_mm'), 1)
                pe.wait_ge(s('ecum_ready'), c + 1)
                pe.wait_ge(s('arg_ready'), c + 1)
                for g in range(SG):
                    ins = mm(PS[:, 0, g * 128:(g + 1) * 128], hid[:, TB + g, ts], hid[:, TC + g, ts])
                ins.then_inc(s('bc_mm'), 1)
                for m in range(4):
                    ins = pe.transpose(PS[:, 1, m * 128:(m + 1) * 128], hid[:, TX + m, ts], ident)
                ins.then_inc(s('xtm_mm'), 1)
                for g in range(SG):
                    ins = pe.transpose(PS[:, 2, g * 128:(g + 1) * 128], hid[:, TB + g, ts], ident)
                ins.then_inc(s('btm_mm'), 1)
                pe.wait_ge(s('mt_ready'), (LV + 1) * c + 1)
                pe.wait_ge(s('bm_ready'), c + 1)
                for h in range(GH):
                    ins = mm(PS[:, 3, h * 128:(h + 1) * 128], mt[:, 0, h * 128:(h + 1) * 128], ident)
                ins.then_inc(s('xinit_mm'), 1)
                pe.wait_ge(s('xinit_ready'), c + 1)
                for l in range(LV):
                    n = LV * c + l
                    pe.wait_ge(s('mt_ready'), (LV + 1) * c + l + 2)
                    if l:
                        pe.wait_ge(s('x_ready'), n)
                    for h in range(GH):
                        hs_ = slice(h * 128, (h + 1) * 128)
                        ins = mm(PS[:, 3, hs_], mt[:, l + 1, hs_], xinv[:, hs_])
                    ins.then_inc(s('y_mm'), 1)
                    if l == 0:
                        pe.wait_ge(s('lt_ready'), c + 1)
                        pe.wait_ge(s('attn_ready'), c + 1)
                    pe.wait_ge(s('y_ready'), n + 1)
                    if l < LV - 1:
                        for h in range(GH):
                            hs_ = slice(h * 128, (h + 1) * 128)
                            ins = mm(PS[:, 4, hs_], xinvt[:, hs_], yinv[:, hs_])
                        ins.then_inc(s('p_mm'), 1)
                    for h in range(GH):
                        hs_ = slice(h * 128, (h + 1) * 128)
                        ins = mm(PS[:, 5, hs_], yinv[:, hs_], xinvt[:, hs_])
                    ins.then_inc(s('pt_mm'), 1)
                    if l == 1:
                        pe.wait_ge(s('score_ready'), c + 1)
                        pe.wait_ge(s('xdt_ready'), c + 1)
                        pe.wait_ge(s('ce_ready'), c + 1)
                        if c == 0:
                            pe.wait_ge(s('state_zero'), 1)
                        for h in range(SH):
                            o = PS[64 * (h % 2):64 * (h % 2) + 64, 0, (h // 2) * 128:(h // 2 + 1) * 128]
                            gs = slice((h % 4) * 128, (h % 4 + 1) * 128)
                            mm(o, xdt[:, h * 64:(h + 1) * 64], scoret[:, h // 4, gs], True, False)
                            ins = mm(o, hssd[:, h * 64:(h + 1) * 64], ce[h // 4][:, gs], False, True)
                        ins.then_inc(s('yt_mm'), 1)
                    if l == 2:
                        pe.wait_ge(s('btm_ready'), c + 1)
                        for g in range(SG):
                            ins = mm(PS[:, 1, g * 256:(g + 1) * 256], btm[:, g * 128:(g + 1) * 128],
                                     xde[:, g * 256:(g + 1) * 256])
                        ins.then_inc(s('hup_mm'), 1)
                pe.wait_ge(s('x_ready'), LV * (c + 1))
                pe.wait_ge(s('kvs_ready'), c + 1)
                for h in range(GH):
                    hs_ = slice(h * 128, (h + 1) * 128)
                    ins = mm(PS[:, 3, hs_], kbe[:, hs_], xinvt[:, hs_])
                ins.then_inc(s('w_mm'), 1)
                pe.wait_ge(s('w_ready'), c + 1)
                for h in range(GH):
                    hs_ = slice(h * 128, (h + 1) * 128)
                    mm(PS[:, 6, hs_], xinvt[:, hs_], vb[:, hs_], True, False)
                    ins = mm(PS[:, 6, hs_], wt[:, hs_], sgdn[:, hs_], False, True)
                ins.then_inc(s('vnew_mm'), 1)
                pe.wait_ge(s('vnew_ready'), c + 1)
                pe.wait_ge(s('qe_ready'), c + 1)
                pe.wait_ge(s('attn_ready'), c + 1)
                for h in range(GH):
                    hs_ = slice(h * 128, (h + 1) * 128)
                    mm(PS[:, 2, hs_], sgdn[:, hs_], qe[:, hs_], True, False)
                    ins = mm(PS[:, 2, hs_], vnew[:, hs_], attnt[:, hs_], False, True)
                ins.then_inc(s('ot_mm'), 1)
                for h in range(GH):
                    hs_ = slice(h * 128, (h + 1) * 128)
                    ins = mm(PS[:, 7, hs_], kdec[:, hs_], vnew[:, hs_])
                ins.then_inc(s('kv_mm'), 1)

            pe.wait_ge(s('sprep_ready'), 1)
            pe.wait_ge(s('yt_taken'), NCH)
            mm(PS[:, 0, 0:192], const('ones')[0:8, :], valx[0:8].rearrange("p a b -> p (a b)")).then_inc(s('spread_mm'), 1)
            pe.wait_ge(s('x_ready'), LV * NCH)
            for m in range(4):
                for e in range(2):
                    lhsT = supd[0:8, e, m * 128:(m + 1) * 128]
                    ins = mm(PS[:, 4, (m * 2 + e) * NS:(m * 2 + e + 1) * NS], lhsT, ident[0:8, 0:8])
            ins.then_inc(s('spread_mm'), 1)
            pe.wait_ge(s('sprep_ready'), 2)
            pe.wait_ge(s('ot_taken'), NCH)
            mm(PS[:, 2, 0:GH * NS], const('ones'), qkp.rearrange("p a b -> p (a b)")).then_inc(s('qks_mm'), 1)
            pe.wait_ge(s('sprep_ready'), 3)
            mm(PS[:, 5, 0:SG * NS], const('ones'), bcp.rearrange("p a b -> p (a b)")).then_inc(s('bcs_mm'), 1)
            pe.wait_ge(s('st_loaded'), 32)
            pe.wait_ge(s('rhs2_ready'), 1)
            pe.wait_ge(s('h_ready'), NCH)
            for h in range(GH):
                for b in range(NS):
                    e = h * NS + b
                    ins = mm(PS[:, 1, 2 * e:2 * e + 2], s0[:, h, b, :], rhs2[:, e, :])
            ins.then_inc(s('sv_mm'), 1)
            pe.wait_ge(s('vnew_ready'), NCH)
            for b in range(NS):
                for m in range(4):
                    ins = mm(PS[:, 6, m * NS + b:m * NS + b + 1], h0[:, b, m * 128:(m + 1) * 128],
                             hid[:, TC + m // 2, T + b:T + b + 1])
            ins.then_inc(s('y0_mm'), 1)
            pe.wait_ge(s('vnt_ready'), 1)
            for h in range(GH):
                ins = pe.transpose(PS[0:8, 3, h * 128:(h + 1) * 128], vnt[:, h, :], ident)
            ins.then_inc(s('row_mm'), 1)
            pe.wait_ge(s('xds_ready'), 1)
            pe.wait_ge(s('s_ready'), NCH)
            for m in range(4):
                ins = pe.transpose(PS[0:8, 7, m * 128:(m + 1) * 128], xds[:, m, :], ident)
            ins.then_inc(s('row_mm'), 1)
            pe.wait_ge(s('row_ready'), 1)
            pe.wait_ge(s('valb_ready'), 1)
            pe.wait_ge(s('spread_ready'), 1)
            for b in range(NS):
                if b >= 2:
                    pe.wait_ge(s('sel_taken'), b - 1)
                mm(PS[:, b % 2, :], selb[:, b, :], vrow[0:8, :]).then_inc(s('sel_mm'), 1)
            pe.wait_ge(s('row_ready'), 2)
            for b in range(NS):
                if b >= 2:
                    pe.wait_ge(s('hsel_taken'), b - 1)
                mm(PS[:, 2 + b % 2, :], selb[:, b, :], xrow[0:8, :]).then_inc(s('hsel_mm'), 1)
            for j in range(8):
                e = j if j < 4 else 4 + (j - 4) // 2
                pe.wait_ge(s('osq_ready'), j + 1)
                if e >= 2 and (j < 4 or j % 2 == 0):
                    pe.wait_ge(s('ln_ready'), R_MIX + e - 1)
                both(4 + 2 * (e % 2), const('ones_128' if j < 4 else 'ones_256'), sq[:, j % 2, :],
                     j < 4 or j % 2 == 0, j < 4 or j % 2 == 1).then_inc(s('osq_mm'), 1)
            pe.wait_ge(s('mix_ready'), 8)
            pe.wait_ge(s('sel_taken'), NS)
            pe.wait_ge(s('hsel_taken'), NS)
            gemm('outa', lambda k: mix[:, k, :])
            norm_sum(1)
            gemm('gu0', lambda k: xn[:, k, :])
            pe.wait_ge(tile_taken[1], TBASE['dn0'])
            gemm('dn0', lambda k: hid[:, k, :])
            norm_sum(2)

            tb = TBASE['inc']

            def mean_square(j):
                pe.wait_ge(s('cq_sq'), j + 1)
                if j == 4:
                    pe.wait_ge(tile_taken[0], tb + 3)
                both(6 if j < 4 else 0, const('ones_512' if j < 4 else 'ones_256'), sq[:, j % 2, :],
                     j in (0, 4), j in (3, 5)).then_inc(s('cq_mm'), 1)
            for j in range(6):
                pe.wait_ge(w_loaded[j % 4], 16 * (GBASE['inc'] + j // 4 + 1))
                pe.wait_ge(tile_taken[j % 2], tb + j // 2)
                for k in range(KD):
                    ins = both(2 * (j % 2), wring[j % 4][:, k * 128:(k + 1) * 128], xn[:, k, :], k == 0, k == KD - 1)
                ins.then_inc(gemm_ready[j % 2], 1)
                if 1 <= j <= 4:
                    mean_square(j - 1)
            pe.wait_ge(s('m_loaded'), 64)
            for k in range(KD):
                ins = both(4, wkr[:, k, :], xn[:, k, :], k == 0, k == KD - 1)
            ins.then_inc(s('kr_mm'), 1)
            mean_square(4)
            mean_square(5)
            pe.wait_ge(s('kr_raw'), 1)
            pe.wait_ge(s('rot_ready'), 1)
            both(4, rotk, krraw).then_inc(s('krot_mm'), 1)
            pe.wait_ge(s('cq_ready'), 2)
            for m in range(8):
                p = m % 2
                if m < 2:
                    pe.wait_ge(w_loaded[2 + m], 16 * (GBASE['inc'] + 2))
                    pe.wait_ge(w_loaded[3], 16 * (GBASE['inc'] + 2))
                pe.wait_ge(tile_taken[p], tb + 3 + m // 2)
                for k in range(2):
                    ins = both(2 * p, wring[2 + k][:, m * 128:(m + 1) * 128], clat[:, k, :], k == 0, k == 1)
                ins.then_inc(gemm_ready[p], 1)
                if m:
                    pe.wait_ge(s('kn_sq'), m)
                    both(6, const('headsel')[:, (m - 1) * 16:m * 16], sq[:, (m - 1) % 2, :], m == 1, False).then_inc(s('kn_mm'), 1)
            pe.wait_ge(s('kn_sq'), 8)
            both(6, const('headsel')[:, 112:128], sq[:, 1, :], False, False).then_inc(s('kn_mm'), 1)
            pe.wait_ge(s('krsq_ready'), 1)
            both(6, const('ones_96')[0:32, 0:16], krsq, False, True).then_inc(s('kn_sum'), 1)
            pe.wait_ge(s('krot_ready'), 1)
            for n in range(8):
                if n >= 2:
                    pe.wait_ge(s('v_ready'), n - 1)
                for k in range(2):
                    ins = mm(PS[:, 4 + n % 2, :], clat[:, k, (n // 2) * 128:(n // 2 + 1) * 128],
                             wuv[:, k, (n % 2) * 512:(n % 2 + 1) * 512], k == 0, k == 1)
                ins.then_inc(s('v_mm'), 1)

            def key_scale(n, b):
                pe.wait_ge(s('ln_ready'), n + (R_HEAD + 1))
                pe.wait_ge(s('invm_ready'), n + 1)
                mm(PS[0:QH, 2, :], const('ones')[0:16, 0:QH], invm[:, b, :]).then_inc(s('invb_mm'), 1)

            def step(i, u, last=False):
                h = i * 4 + u
                b = u % 2
                if not last:
                    pe.wait_ge(s('qh_ready'), h + 1)
                    g = i if u < 3 else i + 1
                    pe.wait_ge(w_loaded[(u + 1) % 4], g * 16 + 16 * (GBASE['uq'] + 1))
                    for k in range(4):
                        ins = both(0, wring[(u + 1) % 4][:, k * QH:(k + 1) * QH], cqn[:, k, :], k == 0, k == 3)
                    ins.then_inc(s('q_mm'), 1)
                pe.wait_ge(s('qh_ready'), h + 1)
                pe.wait_ge(s('k_ready'), h + 1)
                pe.wait_ge(s('pt2_taken'), h)
                pe.wait_ge(s('otm_ready'), h)
                for q in range(4):
                    ins = mm(PS[:, 4 + q, 0:(q + 1) * 128], qhd[0:QH, b, q * 128:(q + 1) * 128],
                             khd[0:QH, b, 0:(q + 1) * 128])
                ins.then_inc(s('s_mm'), 1)
                if not last:
                    pe.wait_ge(s('qsq_ready'), h + 2)
                    pe.wait_ge(s('k_ready'), h + 1)
                    pe.wait_ge(s('omix_ready'), i * 2 + u // 2)
                    both(2, const('ones_96')[0:QH, 0:QH], qsq[0:QH, :]).then_inc(s('qss_mm'), 1)
                    both(0, rotg[0:QH, :], qraw[0:QH, :]).then_inc(s('qrot_mm'), 1)
                    key_scale(h + 1, 1 - b)
                pe.wait_ge(s('p_ready'), h + 1)
                n = 0
                for kb in range(4):
                    for q in range(kb, 4):
                        ins = pe.transpose(PS[:, 4 + n // 4, (n % 4) * 128:(n % 4 + 1) * 128],
                                           pm[:, q, kb * 128:(kb + 1) * 128], ident)
                        n += 1
                ins.then_inc(s('pt2_mm'), 1)
                pe.wait_ge(s('pt2_taken'), h + 1)
                first = [0, 4, 7, 9]
                for q in range(4):
                    for kb in range(q + 1):
                        n = first[kb] + q - kb
                        ins = mm(PS[:, 7, q * VH:(q + 1) * VH], ptsb[:, n * 128:(n + 1) * 128],
                                 vtok[:, kb, bass.ds(h * VH, VH)] if not isinstance(h, int) else vtok[:, kb, h * VH:(h + 1) * VH],
                                 kb == 0, kb == q)
                ins.then_inc(s('o_mm'), 1)
                if u % 2:
                    pe.wait_ge(s('otm_ready'), h + 1)
                    if not last:
                        pe.wait_ge(s('ln_ready'), h + (R_HEAD + 2))
                    for q in range(4):
                        ins = pe.transpose(PS[:, 3, q * 128:(q + 1) * 128], otm[:, q, :], ident)
                    ins.then_inc(s('ott_mm'), 1)

            for p in range(2):
                pe.wait_ge(tile_taken[p], tb + 7)
            pe.wait_ge(w_loaded[0], 16 * (GBASE['uq'] + 1))
            for k in range(4):
                ins = both(0, wring[0][:, k * QH:(k + 1) * QH], cqn[:, k, :], k == 0, k == 3)
            ins.then_inc(s('q_mm'), 1)
            pe.wait_ge(s('qsq_ready'), 1)
            both(2, const('ones_96')[0:QH, 0:QH], qsq[0:QH, :]).then_inc(s('qss_mm'), 1)
            both(0, rotg[0:QH, :], qraw[0:QH, :]).then_inc(s('qrot_mm'), 1)
            key_scale(0, 0)
            pe.wait_ge(s('v_ready'), 8)
            pe.wait_ge(s('rinv_ready'), R_KEY + 1)
            for u in range(4):
                step(0, u)
            with pe.Fori(1, MH // 4 - 1) as i:
                for u in range(4):
                    step(i, u)
            for u in range(4):
                step(MH // 4 - 1, u, last=u == 3)

            pe.wait_ge(s('gk_ready'), 1)
            for h in range(MH):
                p = slice(64 * (h % 2), 64 * (h % 2) + 64)
                for k in range(2):
                    e = (k * 8 + h // 2) * NS
                    ins = mm(PS[:, h % 2, e:e + NS], wukt[p, h // 2, k * 128:(k + 1) * 128], qkn[p, h // 2, :])
            ins.then_inc(s('qa_mm'), 1)
            pe.wait_ge(s('qa_ready'), 1)
            for b in range(NS):
                for k in range(2):
                    mm(PS[0:16, 4, b:b + 1], qa[:, k, :, b], clat[:, k, T + b:T + b + 1], k == 0, False)
                ins = mm(PS[0:16, 4, b:b + 1], qr[:, :, b], krrot[:, T + b:T + b + 1], False, True)
            ins.then_inc(s('sn_mm'), 1)

            def sequence(i, p):
                b = i * 2 + p
                rows_, ct, krt_ = pagebuf[p]
                pe.wait_ge(pages_loaded[p], i * (16 * 3 * NPG) + 16 * 3 * NPG)
                pe.wait_ge(s('smx_ready'), b)
                for g in range(NPG):
                    o = PS[:, 2, g * 16:(g + 1) * 16]
                    for k in range(2):
                        mm(o, ct[:, g, k, :], qa[:, k, :, b], k == 0, False)
                    ins = mm(o, krt_[:, g, :], qr[:, :, b], False, True)
                ins.then_inc(s('sc_mm'), 1)
                pe.wait_ge(s('smx_ready'), b + 1)
                pe.transpose(PS[0:16, 3, 0:128], mxp[:, 0, :], ident).then_inc(s('smt_mm'), 1)
                pe.wait_ge(s('sdiag_ready'), b + 1)
                mm(PS[:, 4, 0:32], const('ones')[0:16, :], diag2.rearrange("p a b -> p (a b)")).then_inc(s('sbc_mm'), 1)
                pe.wait_ge(s('sp_ready'), b + 1)
                pe.wait_ge(s('ctx_ready'), b)
                for g in range(NPG):
                    mm(PS[:, 5, 0:16], const('ones'), sp[:, g, :], g == 0, g == NPG - 1)
                for k in range(2):
                    for g in range(NPG):
                        ins = mm(PS[:, 6, k * 16:(k + 1) * 16], rows_[:, g, k * 128:(k + 1) * 128], sp[:, g, :],
                                 g == 0, g == NPG - 1)
                ins.then_inc(s('ctx_mm'), 1)
            pe.wait_ge(s('omix_ready'), MH // 2)
            for p in range(2):
                sequence(0, p)
            with pe.Fori(1, NS // 2) as i:
                for p in range(2):
                    sequence(i, p)
            pe.wait_ge(s('ctx_ready'), NS)
            for h in range(MH):
                for k in range(2):
                    ins = mm(PS[64 * (h % 2):64 * (h % 2) + 64, 7, (h // 2) * NS:(h // 2 + 1) * NS],
                             wuv[:, k, h * VH:(h + 1) * VH], ctxt[:, k, h, :], k == 0, k == 1)
            ins.then_inc(s('so_mm'), 1)
            pe.wait_ge(s('so_ready'), 1)
            gemm('outc', lambda k: mix[:, k, :])
            norm_sum(3)
            gemm('gu1', lambda k: xn[:, k, :])
            pe.wait_ge(tile_taken[1], TBASE['dn1'])
            gemm('dn1', lambda k: hid[:, k, :])

        @block.scalar
        def _(act):
            act.wait_ge(c_loaded, 16)
            act.wait_ge(g_loaded, 16 * len(SMALLS))

            def square(n, k, ready):
                act.wait_ge(*ready)
                if 8 * n + k >= 2:
                    act.wait_ge(s('sq_added'), 8 * n + k - 1)
                act.activation(sq[:, k % 2, :], xres[:, k, :], ACT.Square).then_inc(s('sq_ready'), 1)

            def rsqrt(r, out, mean):
                act.activation(out, mean, ACT.Ln, bias=small[0:out.shape[0], C_EPS:C_EPS + 1]).then_inc(s('ln_ready'), 1)
                act.wait_ge(s('ln_ready'), r + 1)
                act.activation(out, out, ACT.Exp, scale=-0.5).then_inc(s('rinv_ready'), 1)

            def norm(n, stage=None):
                for k in range(KD):
                    square(n, k, (tile_taken[k % 2], TBASE[stage] + k // 2 + 1) if n else (x_loaded, 32))
                act.wait_ge(s('ssq_mm'), n + 1)
                rsqrt(R_NORM[n], two(rinv[:, R_NORM[n] % 2, :]), bank2(4))

            def silus(stage):
                def turn(i, first):
                    for q in range(2):
                        act.wait_ge(gemm_ready[0], TBASE[stage] + i * 2 + (q + 1))
                        if not first:
                            act.wait_ge(tile_taken[1], TBASE[stage] + i * 2 + (q - 1))
                        act.activation(two(sgate[:, q, :]), bank2(0), ACT.Silu).then_inc(tile_taken[0], 1)
                turn(0, True)
                with act.Fori(1, 11) as i:
                    turn(i, False)

            norm(0)
            act.activation(nega[:, :], gatec[:, NGATE:], ACT.Exp).then_inc(s('gact_ready'), 1)
            act.wait_ge(s('gprep_ready'), 1)
            act.activation(gexp[:, :, 0:NDEC], gabs[:, :, 0:NDEC], ACT.Exp, scale=-1.0)
            act.activation(gexp[:, :, NDEC:], graw[:, :, NDEC:], ACT.Exp, scale=-1.0).then_inc(s('gact_ready'), 1)
            act.wait_ge(s('gprep_ready'), 2)
            act.activation(gln[:, :, 0:NDEC], gone[:, :, 0:NDEC], ACT.Ln).then_inc(s('gact_ready'), 1)
            act.wait_ge(s('raw_zeroed'), 1)

            def conv_turn(i, first):
                def take_tile(u):
                    p = u % 2
                    act.wait_ge(gemm_ready[p], i * 2 + (u // 2 + 1))
                    if not (first and u < 2):
                        act.wait_ge(s('conv_done'), i * 4 + (u - 1))
                    act.activation(two(raw[:, p, 3:3 + TOK]), bank2(2 * p), ACT.Copy).then_inc(s('raw_ready'), 1)
                    act.activation(convout_p[:, i * 4 + u, :], PS[:, 2 * p + 1, T - 3 - HALF:T - HALF], ACT.Copy)
                    act.activation(convout_s[:, i * 4 + u, :], PS[:, 2 * p + 1, T - HALF:HALF], ACT.Copy)\
                        .then_inc(tile_taken[p], 1)

                def silu(u):
                    act.wait_ge(s('conv_done'), i * 4 + (u + 1))
                    bias = convb[:, bass.ds(i * 4 + u, 1)] if not isinstance(i, int) else convb[:, i * 4 + u:i * 4 + u + 1]
                    act.activation(hid[:, i * 4 + u, :], cacc[:, u % 2, :], ACT.Silu, bias=bias)\
                        .then_inc(s('silu_done'), 1)
                take_tile(0)
                for u in range(1, 4):
                    take_tile(u)
                    silu(u - 1)
                silu(3)
            conv_turn(0, True)
            with act.Fori(1, 5) as i:
                conv_turn(i, False)

            def l2_root(j):
                act.wait_ge(s('l2_mm'), j + 1)
                if j >= 2:
                    act.wait_ge(s('l2_done'), j - 1)
                rsqrt(R_L2 + j, two(rinv[:, (R_L2 + j) % 2, :]), bank2(4 + 2 * (j % 2)))
            for j in range(8):
                act.wait_ge(s('silu_done'), NCONV)
                if j >= 2:
                    act.wait_ge(s('l2_mm'), j - 1)
                act.activation(sq[:, j % 2, :], hid[:, j, :], ACT.Square).then_inc(s('l2sq_ready'), 1)
                if j:
                    l2_root(j - 1)
            l2_root(7)
            with act.Fori(0, 2) as i:
                for u in range(4):
                    act.wait_ge(gemm_ready[u % 2], i * 2 + (10 + u // 2 + 1))
                    act.activation(two(hid[:, i * 4 + (TZ + u), :]), bank2(2 * (u % 2)), ACT.Silu)\
                        .then_inc(tile_taken[u % 2], 1)
            act.wait_ge(s('cumt_ready'), 1)
            act.activation(ecumt[:, :, :], cumt[:, :, :], ACT.Exp).then_inc(s('ecumt_ready'), 1)

            for c in range(NCH):
                act.wait_ge(s('cumB_mm'), c + 1)
                if c:
                    act.wait_ge(s('s_ready'), c)
                    act.wait_ge(s('h_ready'), c)
                act.activation(ecum, PS[:, 0:3, :], ACT.Exp).then_inc(s('ecum_ready'), 1)
                act.wait_ge(s('arg_ready'), c + 1)
                act.activation(kd, kdarg, ACT.Exp).then_inc(s('kd_ready'), 1)
                act.activation(dect, arg, ACT.Exp).then_inc(s('dect_ready'), 1)
                act.wait_ge(s('btm_mm'), c + 1)
                act.activation(btm, PS[:, 2, 0:256], ACT.Copy).then_inc(s('btm_ready'), 1)
                for l in range(LV):
                    act.wait_ge(s('y_mm'), LV * c + l + 1)
                    act.activation(yinv, PS[:, 3, :], ACT.Copy).then_inc(s('y_ready'), 1)
                act.wait_ge(s('w_mm'), c + 1)
                act.activation(wt, PS[:, 3, :], ACT.Copy, scale=-1.0).then_inc(s('w_ready'), 1)
                act.wait_ge(s('vnew_mm'), c + 1)
                act.activation(vnew, PS[:, 6, :], ACT.Copy).then_inc(s('vnew_ready'), 1)
                act.wait_ge(s('ot_mm'), c + 1)
                act.activation(mix[:, 0:4, c * 128:(c + 1) * 128], by(PS[:, 2, :], GH), ACT.Copy).then_inc(s('ot_taken'), 1)

            act.wait_ge(s('spread_mm'), 1)
            act.activation(ab, PS[:, 0, 0:NDEC * NS].rearrange("p (a b) -> p a b", b=NS), ACT.Exp).then_inc(s('spread_ready'), 1)
            act.wait_ge(s('spread_mm'), 2)
            apx_ps = PS[:, 4, 0:64].rearrange("p (m e b) -> p m e b", e=2, b=NS)
            act.activation(apx[:, :, 0, :], apx_ps[:, :, 0, :], ACT.Exp)
            act.activation(apx[:, :, 1, :], apx_ps[:, :, 1, :], ACT.Copy).then_inc(s('spread_ready'), 1)
            act.wait_ge(s('row_mm'), 1)
            act.activation(vrow[0:8, :], PS[0:8, 3, :], ACT.Copy).then_inc(s('row_ready'), 1)
            act.wait_ge(s('row_mm'), 2)
            act.activation(xrow[0:8, :], PS[0:8, 7, :], ACT.Copy).then_inc(s('row_ready'), 1)
            act.wait_ge(s('xds_ready'), 2)

            def mix_root(e):
                act.wait_ge(s('osq_mm'), e + 1 if e < 4 else 4 + 2 * (e - 3))
                if e >= 2:
                    act.wait_ge(s('mix_ready'), e - 1)
                rsqrt(R_MIX + e, two(rinv[:, (R_MIX + e) % 2, :]), bank2(4 + 2 * (e % 2)))
            for j in range(8):
                if j >= 2:
                    act.wait_ge(s('osq_mm'), j - 1)
                act.activation(sq[:, j % 2, :], mix[:, j, :], ACT.Square).then_inc(s('osq_ready'), 1)
                if 1 <= j <= 4:
                    mix_root(j - 1)
                elif j == 6:
                    mix_root(4)
            mix_root(5)
            norm(1, 'outa')
            silus('gu0')
            norm(2, 'dn0')

            tb = TBASE['inc']
            for j in range(6):
                act.wait_ge(gemm_ready[j % 2], tb + j // 2 + 1)
                if j >= 2:
                    act.wait_ge(s('cq_mm'), j - 1)
                act.activation(two(sq[:, j % 2, :]), bank2(2 * (j % 2)), ACT.Square).then_inc(s('cq_sq'), 1)
                act.activation(two(hid[:, j, :]), bank2(2 * (j % 2)), ACT.Copy).then_inc(tile_taken[j % 2], 1)
            for r, b, n in ((R_CQ, 6, 4), (R_KV, 0, 6)):
                act.wait_ge(s('cq_mm'), n)
                rsqrt(r, two(rinv[:, r % 2, :]), bank2(b))
            act.wait_ge(s('kr_mm'), 1)
            act.activation(two(krsq), bank2(4, 32), ACT.Square).then_inc(s('krsq_ready'), 1)
            act.activation(two(krraw), bank2(4, 32), ACT.Copy).then_inc(s('kr_raw'), 1)
            for m in range(8):
                p = m % 2
                act.wait_ge(gemm_ready[p], tb + 3 + m // 2 + 1)
                if m >= 2:
                    act.wait_ge(s('kn_mm'), m - 1)
                act.activation(two(sq[:, p, :]), bank2(2 * p), ACT.Square).then_inc(s('kn_sq'), 1)
                act.activation(two(knope[:, m, :]), bank2(2 * p), ACT.Copy, scale=small[:, C_KN:C_KN + 1])\
                    .then_inc(tile_taken[p], 1)
            act.wait_ge(s('kn_sum'), 1)
            rsqrt(R_KEY, two(invr), bank2(6, 16))
            for n in range(8):
                act.wait_ge(s('v_mm'), n + 1)
                act.activation(vtok[:, n // 2, (n % 2) * 512:(n % 2 + 1) * 512], PS[:, 4 + n % 2, :], ACT.Copy)\
                    .then_inc(s('v_ready'), 1)

            def query(h, first=False):
                act.wait_ge(s('q_mm'), h + 1)
                if not first:
                    act.wait_ge(s('qrot_mm'), h)
                    act.wait_ge(s('qh_ready'), h)
                act.activation(two(qraw[0:QH, :]), bank2(0, QH), ACT.Copy)
                act.activation(two(qsq[0:QH, :]), bank2(0, QH), ACT.Square).then_inc(s('qsq_ready'), 1)

            def query_root(h, b):
                act.wait_ge(s('qss_mm'), h + 1)
                rsqrt(h + R_HEAD, two(rinv[0:QH, b, :]), bank2(2, QH))

            def step(i, u, last=False):
                h = i * 4 + u
                if not last:
                    query(h + 1)
                act.wait_ge(s('nb_ready'), h + 1)
                act.wait_ge(s('pt2_mm'), h)
                act.wait_ge(s('otm_ready'), h)
                for q in range(4):
                    ins = act.activation(pm[:, q, 0:(q + 1) * 128], PS[:, 4 + q, 0:(q + 1) * 128], ACT.Exp,
                                         bias=nb[:, q:q + 1], scale=PSCALE, accum_out=den[:, q:q + 1])
                ins.then_inc(s('p_ready'), 1)
                if not last:
                    query_root(h + 1, (u + 1) % 2)
                act.wait_ge(s('pt2_mm'), h + 1)
                act.wait_ge(s('o_mm'), h)
                act.activation(ptsb[:, 0:1024].rearrange("p (a n) -> p a n", a=2), PS[:, 4:6, :], ACT.Copy)
                act.activation(ptsb[:, 1024:1280], PS[:, 6, 0:256], ACT.Copy).then_inc(s('pt2_taken'), 1)
                if u % 2:
                    act.wait_ge(s('ott_mm'), i * 2 + (u // 2 + 1))
                    act.activation(mix[:, i * 2 + u // 2, 0:T], PS[:, 3, :], ACT.Copy).then_inc(s('omix_ready'), 1)
            query(0, True)
            query_root(0, 0)
            for u in range(4):
                step(0, u)
            with act.Fori(1, MH // 4 - 1) as i:
                for u in range(4):
                    step(i, u)
            for u in range(4):
                step(MH // 4 - 1, u, last=u == 3)

            act.wait_ge(s('qa_mm'), 1)
            for e in range(2):
                for k in range(2):
                    ins = act.activation(qa[:, k, e:MH:2, :], PS[:, e, k * 64:(k + 1) * 64].rearrange("p (m b) -> p m b", b=NS), ACT.Copy)
            ins.then_inc(s('qa_ready'), 1)
            with act.Fori(0, NS // 2) as i:
                for p in range(2):
                    b = i * 2 + p
                    act.wait_ge(s('sdif_ready'), b + 1)
                    act.activation(pn, sdif, ACT.Exp, scale=PSCALE).then_inc(s('pn_ready'), 1)
                    act.wait_ge(s('ssub_ready'), b + 1)
                    act.activation(sp, sp, ACT.Exp, scale=PSCALE).then_inc(s('sp_ready'), 1)
            act.wait_ge(s('so_mm'), 1)
            act.activation(mix[:, :, T:TOK], PS[:, 7, 0:64].rearrange("p (m b) -> p m b", b=NS), ACT.Copy).then_inc(s('so_ready'), 1)
            norm(3, 'outc')
            silus('gu1')

        @block.vector
        def _(dve):
            st = Steps(dve, s('dve_own'))
            own = s('dve_own')
            dve.wait_ge(c_loaded, 16)
            dve.wait_ge(g_loaded, 16 * len(SMALLS))
            tt, ts_, stt = dve.tensor_tensor, dve.tensor_scalar, dve.scalar_tensor_tensor

            def normalise(n):
                dve.wait_ge(s('rinv_ready'), R_NORM[n] + 1)
                for k in range(KD):
                    st(stt(out=xn[:, k, :], in0=xres[:, k, :], scalar=gains[:, n, k:k + 1], in1=rinv[:, R_NORM[n] % 2, :],
                           op0=ALU.mult, op1=ALU.mult), s('xn_ready'))

            def residual(stage):
                for k in range(KD):
                    p = k % 2
                    dve.wait_ge(gemm_ready[p], TBASE[stage] + k // 2 + 1)
                    st(tt(two(xres[:, k, :]), two(xres[:, k, :]), bank2(2 * p), ALU.add), tile_taken[p])

            def gate_up(stage):
                with dve.Fori(0, 11) as i:
                    for q in range(2):
                        dve.wait_ge(gemm_ready[1], TBASE[stage] + i * 2 + (q + 1))
                        dve.wait_ge(tile_taken[0], TBASE[stage] + i * 2 + (q + 1))
                        tt(two(hid[:, i * 2 + q, :]), two(sgate[:, q, :]), bank2(2), ALU.mult).then_inc(tile_taken[1], 1)

            normalise(0)
            dve.wait_ge(s('gates_mm'), 1)
            st(dve.memset(graw[:, :, :], 0.0))
            st.sync()
            st(tt(graw[:, 0:4, :], PS[:, 6, 0:4 * NGATE].rearrange("p (t n) -> p t n", n=NGATE), across(gatec[:, 0:NGATE], 4), ALU.add))
            st(tt(graw[0:NS, 4, :], PS[0:NS, 6, 4 * NGATE:5 * NGATE], gatec[0:NS, 0:NGATE], ALU.add))
            st.sync()
            st(stt(out=gabs[:, :, :], in0=graw[:, :, :], scalar=-1.0, in1=graw[:, :, :], op0=ALU.mult, op1=ALU.max), s('gprep_ready'))
            dve.wait_ge(s('gact_ready'), 2)
            st(ts_(gone[:, :, :], gexp[:, :, :], 1.0, None, ALU.add), s('gprep_ready'))
            st.sync()
            st(dve.reciprocal(grec[:, :, :], gone[:, :, :]))
            dc = slice(0, NDEC)
            st(ts_(gabs[:, :, dc], gone[:, :, dc], -1.0, None, ALU.add))
            st.sync()
            st(tt(gabs[:, :, dc], gexp[:, :, dc], gabs[:, :, dc], ALU.subtract))
            st.sync()
            st(tt(gabs[:, :, dc], gabs[:, :, dc], grec[:, :, dc], ALU.mult))
            dve.wait_ge(s('gact_ready'), 3)
            st.sync()
            st(tt(gabs[:, :, dc], gabs[:, :, dc], gln[:, :, dc], ALU.add))
            st.sync()
            st(stt(out=gsp[:, :, dc], in0=graw[:, :, dc], scalar=0.0, in1=gabs[:, :, dc], op0=ALU.max, op1=ALU.add))
            dve.wait_ge(s('gact_ready'), 1)
            st.sync()
            st(stt(out=la[:, :, :], in0=gsp[:, :, dc], scalar=-1.0, in1=across(nega[:, :], 5), op0=ALU.mult, op1=ALU.mult), s('la_ready'))

            def conv_turn(i, first):
                for u in range(4):
                    p, j = u % 2, i * 4 + u

                    def w(t):
                        return convw[:, j, t:t + 1]
                    dve.wait_ge(s('raw_ready'), j + 1)
                    if not (first and u < 2):
                        dve.wait_ge(s('silu_done'), i * 4 + (u - 1))
                    st(ts_(cacc[:, p, :], raw[:, p, 3:3 + TOK], w(3), None, ALU.mult))
                    for t in range(3):
                        st.sync()
                        st(stt(out=cacc[:, p, T:TOK], in0=prev[:, j, t, :], scalar=w(t), in1=cacc[:, p, T:TOK],
                               op0=ALU.mult, op1=ALU.add))
                        st(stt(out=cacc[:, p, 0:T], in0=raw[:, p, t:t + T], scalar=w(t), in1=cacc[:, p, 0:T],
                               op0=ALU.mult, op1=ALU.add), s('conv_done') if t == 2 else None)
            dve.wait_ge(s('raw_zeroed'), 1)
            conv_turn(0, True)
            st.loop(1, 5, lambda i: conv_turn(i, False), [(own, 24), (s('conv_done'), 4)])

            dve.wait_ge(s('cum_mm'), 1)
            st(dve.tensor_copy(cumt[:, :, :], PS[:, 7, 0:NCH * NDEC].rearrange("p (c n) -> p c n", n=NDEC)), s('cumt_ready'))
            for j in range(8):
                dve.wait_ge(s('rinv_ready'), R_L2 + j + 1)
                st(stt(out=hid[:, j, :], in0=hid[:, j, :], scalar=128 ** -0.5 if j < 4 else 1.0, in1=rinv[:, (R_L2 + j) % 2, :],
                       op0=ALU.mult, op1=ALU.mult), s('l2_done'))
            dve.wait_ge(s('ecumt_ready'), 1)
            st(tt(bec[:, :, :], beta[:, 0:NCH], ecumt[:, :, 0:GH], ALU.mult))
            st.sync()

            ident4 = across(ident, GH)
            for c in range(NCH):
                tc_ = slice(c * 128, (c + 1) * 128)
                dve.wait_ge(s('cumB_mm'), c + 1)
                dve.wait_ge(s('ecum_ready'), c + 1)
                if c == 0:
                    dve.wait_ge(gemm_ready[1], 14)
                    dve.wait_ge(s('silu_done'), NCONV)
                st(tt(kdarg.rearrange("p (a b) -> p a b", b=4), PS[:, 0:3, 127:512:128],
                      cumt[:, c, :].rearrange("p (a b) -> p a b", b=4), ALU.subtract))
                for h in range(NDEC):
                    hs_ = slice((h % 4) * 128, (h % 4 + 1) * 128)
                    st(stt(out=arg[:, h // 4, hs_], in0=PS[:, h // 4, hs_], scalar=cumt[:, c, h:h + 1],
                           in1=const('decaymask'), op0=ALU.subtract, op1=ALU.min), s('arg_ready') if h == NDEC - 1 else None)
                dve.wait_ge(s('dect_ready'), c + 1)
                dve.wait_ge(s('betaB_mm'), c + 1)
                st(tt(bm, dect[:, 0, :], PS[:, 3, :], ALU.mult), s('bm_ready'))
                dve.wait_ge(s('kk_mm'), c + 1)
                st.sync()
                st(tt(lt, PS[:, 4, :], bm, ALU.mult), s('lt_ready'))
                dve.wait_ge(s('qk_mm'), c + 1)
                st(tt(attnt, PS[:, 5, :], dect[:, 0, :], ALU.mult), s('attn_ready'))
                dve.wait_ge(s('mt_ready'), (LV + 1) * c + 1)
                st(tt(by(xinvt, GH), ident4, by(mt[:, 0], GH), ALU.subtract))
                dve.wait_ge(s('xinit_mm'), c + 1)
                st(tt(by(xinv, GH), ident4, by(PS[:, 3, :], GH), ALU.subtract), s('xinit_ready'))
                dve.wait_ge(s('kd_ready'), c + 1)
                dve.wait_ge(s('ktm_mm'), c + 1)
                st(tt(by(kbe, GH), by(PS[:, 6, :], GH), over(bec[:, c, :], 128), ALU.mult))
                st(tt(by(kdec, GH), by(PS[:, 6, :], GH), over(kd[:, 0:GH], 128), ALU.mult))
                dve.wait_ge(s('vtm_mm'), c + 1)
                st(tt(by(vb, GH), by(PS[:, 7, :], GH), over(beta[:, c, :], 128), ALU.mult), s('kvs_ready'))
                fill = []

                def ssd_scores():
                    dve.wait_ge(s('bc_mm'), c + 1)
                    for g in range(SG):
                        st(tt(by(scoret[:, g], 4), by(dect[:, 1 + g, :], 4), across(PS[:, 0, g * 128:(g + 1) * 128], 4), ALU.mult),
                           s('score_ready') if g else None)
                    dve.wait_ge(s('xtm_mm'), c + 1)
                    st(tt(by(xdt, SH), by(PS[:, 1, :], SH), over(gdt[:, c, :], 64), ALU.mult))
                    st.sync()
                    st(tt(by(xde, SH), by(xdt, SH), over(kd[:, GH:], 64), ALU.mult), s('xdt_ready'))
                    dve.wait_ge(s('ecum_ready'), c + 1)
                    for g in range(SG):
                        st(tt(by(ce[g], 4), across(hid[:, TC + g, tc_], 4), by(ecum[:, 1 + g], 4), ALU.mult),
                           s('ce_ready') if g else None)

                def ssd_out():
                    dve.wait_ge(s('yt_mm'), c + 1)
                    for m in range(4):
                        st(stt(out=mix[:, 4 + m, tc_], in0=hid[:, TX + m, tc_], scalar=small[:, C_D + m:C_D + m + 1],
                               in1=PS[:, 0, m * 128:(m + 1) * 128], op0=ALU.mult, op1=ALU.add))
                    st.sync()
                    st(tt(mix[:, 4:8, tc_], mix[:, 4:8, tc_], hid[:, TSZ:TSZ + 4, tc_], ALU.mult), s('yt_taken'))
                    last = ecum[:, 1:3, 127:512:128].rearrange("p a b -> p a b")
                    st(tt(hssd.rearrange("p (a b x) -> p a b x", a=2, b=4), hssd.rearrange("p (a b x) -> p a b x", a=2, b=4),
                          last.unsqueeze(3).broadcast_to([128, 2, 4, 64]), ALU.mult))

                def queries():
                    st(tt(by(qe, GH), hid[:, TQ:TQ + 4, tc_], by(ecum[:, 0], GH), ALU.mult), s('qe_ready'))
                fill = {0: ssd_scores, 2: ssd_out, 3: queries}
                for l in range(LV):
                    if l < LV - 1:
                        dve.wait_ge(s('p_mm'), (LV - 1) * c + l + 1)
                        st(tt(xinv, xinv, PS[:, 4, :], ALU.subtract))
                    dve.wait_ge(s('pt_mm'), LV * c + l + 1)
                    st(tt(xinvt, xinvt, PS[:, 5, :], ALU.subtract), s('x_ready'))
                    if l in fill:
                        fill[l]()
                dve.wait_ge(s('hup_mm'), c + 1)
                st.sync()
                st(tt(hssd, hssd, PS[:, 1, :], ALU.add), s('h_ready'))
                dve.wait_ge(s('kv_mm'), c + 1)
                for h in range(GH):
                    hs_ = slice(h * 128, (h + 1) * 128)
                    st(stt(out=sgdn[:, hs_], in0=sgdn[:, hs_], scalar=ecum[:, 0, h * 128 + 127:h * 128 + 128],
                           in1=PS[:, 7, hs_], op0=ALU.mult, op1=ALU.add), s('s_ready') if h == GH - 1 else None)

            dve.wait_ge(s('rec_stored'), 32)
            dve.wait_ge(s('ot_taken'), NCH)
            sc = slice(T, TOK)
            st(dve.tensor_copy(vals[0:8, 0:12], la[0:8, 4, :]))
            st(dve.tensor_copy(vals[0:8, 12:16], beta[0:8, 4, :]))
            st(dve.tensor_copy(vals[0:8, 16:24], gdt[0:8, 4, :]))
            st.sync()
            for e, col in ((0, GH), (1, 16)):
                st(dve.tensor_copy(by(supd[0:8, e], SH), over(vals[0:8, col:col + SH], 64)))
            st(tt(valx[0:8], over(vals[0:8, :], NS), across(ident[0:8, 0:8], 24), ALU.mult), s('sprep_ready'))
            st(tt(qkp, hid[:, TQ:TQ + 4, sc], hid[:, TK:TK + 4, sc], ALU.mult), s('sprep_ready'))
            st(tt(bcp, hid[:, TB:TB + 2, sc], hid[:, TC:TC + 2, sc], ALU.mult), s('sprep_ready'))
            dve.wait_ge(s('spread_mm'), 1)
            dve.wait_ge(s('spread_ready'), 1)
            st(dve.tensor_copy(valb, PS[:, 0, 0:192].rearrange("p (a b) -> p a b", b=NS)), s('valb_ready'))
            st.sync()
            st(tt(kb8, hid[:, TK:TK + 4, sc], valb[:, 12:16], ALU.mult))
            dve.wait_ge(s('spread_ready'), 1)
            st.sync()
            r2 = rhs2.rearrange("p (h b) e -> p h b e", b=NS)
            st(tt(r2[:, :, :, 0], kb8, ab[:, 0:GH], ALU.mult))
            st(tt(r2[:, :, :, 1], hid[:, TQ:TQ + 4, sc], ab[:, 0:GH], ALU.mult), s('rhs2_ready'))
            st(tt(vnt, hid[:, TV:TV + 4, sc], valb[:, 12:16], ALU.mult))
            dve.wait_ge(s('sv_mm'), 1)
            st.sync()
            sv = PS[:, 1, 0:2 * GH * NS].rearrange("p (h b e) -> p h b e", b=NS, e=2)
            st(tt(vnt, vnt, sv[:, :, :, 0], ALU.subtract), s('vnt_ready'))
            dve.wait_ge(s('qks_mm'), 1)
            st.sync()
            st(tt(kb8, vnt, PS[:, 2, 0:GH * NS].rearrange("p (h b) -> p h b", b=NS), ALU.mult))
            st.sync()
            st(tt(mix[:, 0:4, sc], kb8, sv[:, :, :, 1], ALU.add))
            dve.wait_ge(s('spread_ready'), 2)
            st(tt(xds, hid[:, TX:TX + 4, sc], apx[:, :, 1, :], ALU.mult), s('xds_ready'))
            dve.wait_ge(s('y0_mm'), 1)
            st(tt(ysm, PS[:, 6, 0:32].rearrange("p (m b) -> p m b", b=NS), apx[:, :, 0, :], ALU.mult))
            dve.wait_ge(s('bcs_mm'), 1)
            st.sync()
            st(tt(yt2.rearrange("p (g m) b -> p g m b", g=2), xds.rearrange("p (g m) b -> p g m b", g=2),
                  PS[:, 5, 0:16].rearrange("p (g b) -> p g b", b=NS).unsqueeze(2).broadcast_to([128, 2, 2, NS]), ALU.mult))
            st.sync()
            st(tt(ysm, ysm, yt2, ALU.add))
            st.sync()
            st(tt(yt2, hid[:, TX:TX + 4, sc], over(small[:, C_D:C_D + 4], NS), ALU.mult))
            st.sync()
            st(tt(ysm, ysm, yt2, ALU.add))
            st.sync()
            st(tt(mix[:, 4:8, sc], ysm, hid[:, TSZ:TSZ + 4, sc], ALU.mult), s('xds_ready'))
            for b in range(NS):
                dve.wait_ge(s('sel_mm'), b + 1)
                if b >= 2:
                    dve.wait_ge(s('sel_taken'), b - 1)
                st(tt(by(supd[:, b % 2], GH), by(PS[:, b % 2, :], GH), over(hid[:, TK:TK + 4, T + b], 128), ALU.mult))
                st.sync()
                if b == 0:
                    dve.wait_ge(s('s_decayed'), GH)
                st(tt(s0[:, :, b, :], s0[:, :, b, :], by(supd[:, b % 2], GH), ALU.add), s('sel_taken'))
            for b in range(NS):
                dve.wait_ge(s('hsel_mm'), b + 1)
                dve.wait_ge(s('sel_taken'), NS)
                if b >= 2:
                    dve.wait_ge(s('hsel_taken'), b - 1)
                st(tt(by(supd[:, b % 2], 2), by(PS[:, 2 + b % 2, :], 2), over(hid[:, TB:TB + 2, T + b], 256), ALU.mult))
                st.sync()
                dve.wait_ge(s('s_decayed'), GH + b + 1)
                st(tt(h0[:, b], h0[:, b], supd[:, b % 2], ALU.add), s('hsel_taken'))
            for e in range(6):
                dve.wait_ge(s('rinv_ready'), R_MIX + e + 1)
                root = rinv[:, (R_MIX + e) % 2, :]
                if e < 4:
                    st(stt(out=mix[:, e, :], in0=mix[:, e, :], scalar=small[:, C_GDN:C_GDN + 1], in1=root, op0=ALU.mult, op1=ALU.mult))
                    st.sync()
                    st(tt(mix[:, e, :], mix[:, e, :], hid[:, TZ + e, :], ALU.mult), s('mix_ready'))
                else:
                    for m in (2 * e - 4, 2 * e - 3):
                        st(stt(out=mix[:, m, :], in0=mix[:, m, :], scalar=small[:, C_SSM + m - 4:C_SSM + m - 3], in1=root,
                               op0=ALU.mult, op1=ALU.mult), s('mix_ready'))
            residual('outa')
            normalise(1)
            gate_up('gu0')
            residual('dn0')
            normalise(2)

            dve.wait_ge(s('m_loaded'), 64)
            st(ts_(cosg[0:QH, :], rope[0:QH, 0, :], small[0:QH, C_QN:C_QN + 1], None, ALU.mult))
            st(ts_(rotg[0:QH, :], const('rot96')[0:QH, 0:QH], small[0:QH, C_QN:C_QN + 1], None, ALU.mult))
            st(ts_(rotk, const('rot32')[0:32, 0:32], small[0:32, C_KR:C_KR + 1], None, ALU.mult), s('rot_ready'))
            dve.wait_ge(s('rinv_ready'), R_CQ + 1)
            dve.wait_ge(tile_taken[1], TBASE['inc'] + 2)
            for j in range(4):
                st(stt(out=cqn[:, j, :], in0=cqn[:, j, :], scalar=small[:, C_QA + j:C_QA + j + 1], in1=rinv[:, R_CQ % 2, :],
                       op0=ALU.mult, op1=ALU.mult), s('cq_ready') if j == 3 else None)
            dve.wait_ge(s('rinv_ready'), R_KV + 1)
            dve.wait_ge(tile_taken[1], TBASE['inc'] + 3)
            for j in range(2):
                st(stt(out=clat[:, j, :], in0=clat[:, j, :], scalar=small[:, C_KVA + j:C_KVA + j + 1], in1=rinv[:, R_KV % 2, :],
                       op0=ALU.mult, op1=ALU.mult), s('cq_ready') if j == 1 else None)
            dve.wait_ge(s('kr_raw'), 1)
            st(ts_(krg, krraw, small[0:32, C_KR:C_KR + 1], None, ALU.mult))
            st.sync()
            st(tt(krg, krg, rope[0:32, 2, :], ALU.mult))
            dve.wait_ge(s('krot_mm'), 1)
            st(tt(two(krt), bank2(4, 32), two(rope[0:32, 3, :]), ALU.mult))
            st.sync()
            st(tt(krrot, krg, krt, ALU.add), s('krot_ready'))
            dve.wait_ge(s('rinv_ready'), R_KEY + 1)
            dve.wait_ge(tile_taken[0], TBASE['outc'])
            dve.wait_ge(tile_taken[1], TBASE['outc'])

            def key_mask(h, b):
                col = ident[0:16, h:h + 1] if isinstance(h, int) else ident[0:16, bass.ds(h, 1)]
                st(ts_(invm[:, b, :], invr[:, 0:T], col, None, ALU.mult), s('invm_ready'))

            def query(h, pair, b):
                dve.wait_ge(s('qsq_ready'), h + 1)
                st(tt(qt1[0:QH, :], qraw[0:QH, :], cosg[0:QH, :], ALU.mult))
                dve.wait_ge(s('qrot_mm'), h + 1)
                st(tt(two(qt2[0:QH, :]), bank2(0, QH), two(rope[0:QH, 1, :]), ALU.mult))
                st.sync()
                st(tt(qt1[0:QH, :], qt1[0:QH, :], qt2[0:QH, :], ALU.add))
                st.sync()
                dve.wait_ge(s('rinv_ready'), h + (R_HEAD + 1))
                st(tt(qhd[0:QH, b, :], qt1[0:QH, :], rinv[0:QH, b, :], ALU.mult), s('qh_ready'))
                st.sync()
                st(dve.tensor_copy(qs[0:QH, h, :], qhd[0:QH, b, T:TOK]))
                dve.wait_ge(s('invb_mm'), h + 1)
                st(tt(khd[0:64, b, :], knope[64 * b:64 * b + 64, pair, 0:T], PS[0:64, 2, :], ALU.mult))
                st(tt(khd[64:96, b, :], krrot[:, 0:T], PS[0:32, 2, :], ALU.mult), s('k_ready'))

            def step(i, u, last=False):
                h, b = i * 4 + u, u % 2
                if not last:
                    key_mask(h + 1, 1 - b)
                dve.wait_ge(s('s_mm'), h + 1)
                for q in range(4):
                    blk = PS[:, 4 + q, q * 128:(q + 1) * 128]
                    st(tt(blk, blk, const('causal'), ALU.add))
                st.sync()
                for q in range(4):
                    st(dve.tensor_reduce(mx[:, q:q + 1], PS[:, 4 + q, 0:(q + 1) * 128], AX.X, ALU.max))
                st.sync()
                dve.wait_ge(s('p_ready'), h)
                st(ts_(nb, mx, -PSCALE, None, ALU.mult), s('nb_ready'))
                if not last:
                    query(h + 1, i * 2 + (u + 1) // 2, 1 - b)
                dve.wait_ge(s('o_mm'), h + 1)
                if b == 0:
                    dve.wait_ge(s('ott_mm'), i * 2 + u // 2)
                st(dve.reciprocal(rden, den))
                st.sync()
                st(tt(otm[:, :, b * VH:(b + 1) * VH], PS[:, 7, 0:4 * VH].rearrange("p (q v) -> p q v", v=VH), over(rden, VH), ALU.mult),
                   s('otm_ready'))
            key_mask(0, 0)
            query(0, 0, 0)
            per = [(own, 4 * (8 + 6)), (s('invm_ready'), 4), (s('nb_ready'), 4), (s('qh_ready'), 4),
                   (s('k_ready'), 4), (s('otm_ready'), 4)]
            for u in range(4):
                step(0, u)
            st.loop(1, MH // 4 - 1, lambda i: [step(i, u) for u in range(4)], per)
            for u in range(4):
                step(MH // 4 - 1, u, last=u == 3)

            st.sync()
            for p in range(2):
                src = qs[0:64, :, :].rearrange("p (m e) b -> p m e b", e=2)[:, :, p, :]
                st(ts_(qkn[64 * p:64 * p + 64], src, small[0:64, C_KN:C_KN + 1], None, ALU.mult))
            st(dve.tensor_copy(qr, qs[64:96]), s('gk_ready'))
            dve.wait_ge(s('sn_mm'), 1)
            st(tt(snew, PS[0:16, 4, 0:NS], invr[:, T:TOK], ALU.mult), s('snew_ready'))

            def sequence(i, p):
                b = i * 2 + p
                rows_ = pagebuf[p][0]
                sb_ = snew[:, bass.ds(b, 1)] if not isinstance(b, int) else snew[:, b:b + 1]
                dve.wait_ge(s('sc_mm'), b + 1)
                dve.wait_ge(s('ctx_mm'), b)
                st(tt(sp, PS[:, 2, 0:128].rearrange("p (g h) -> p g h", h=16), rows_[:, :, 288:304], ALU.mult))
                st.sync()
                st(dve.tensor_reduce(mxp[:, 0, :], sp.rearrange("p g h -> p h g"), AX.X, ALU.max), s('smx_ready'))
                dve.wait_ge(s('smt_mm'), b + 1)
                st(dve.tensor_reduce(m16, PS[0:16, 3, 0:128], AX.X, ALU.max))
                st.sync()
                st(tt(m16, m16, sb_, ALU.max))
                st.sync()
                st(tt(sdif, sb_, m16, ALU.subtract), s('sdif_ready'))
                st(ts_(diag2[:, 0, :], ident[0:16, 0:16], m16, None, ALU.mult))
                dve.wait_ge(s('pn_ready'), b + 1)
                st(ts_(diag2[:, 1, :], ident[0:16, 0:16], pn, None, ALU.mult), s('sdiag_ready'))
                dve.wait_ge(s('sbc_mm'), b + 1)
                st(tt(sp, sp, across(PS[:, 4, 0:16], NPG), ALU.subtract), s('ssub_ready'))
                st(dve.tensor_copy(pnb[:, 0, :], PS[:, 4, 16:32]))
                dve.wait_ge(s('ctx_mm'), b + 1)
                st.sync()
                st(tt(dsum[:, 0, :], pnb[:, 0, :], PS[:, 5, 0:16], ALU.add))
                st.sync()
                st(dve.reciprocal(dsum[:, 0, :], dsum[:, 0, :]))
                for k in range(2):
                    cn = clat[:, k, bass.ds(b + T, 1)] if not isinstance(b, int) else clat[:, k, T + b:T + b + 1]
                    st(stt(out=ctmp[:, k, :], in0=pnb[:, 0, :], scalar=cn, in1=PS[:, 6, k * 16:(k + 1) * 16], op0=ALU.mult, op1=ALU.add))
                st.sync()
                st(tt(ctxt[:, :, :, b], ctmp, across(dsum[:, 0, :], 2), ALU.mult), s('ctx_ready'))
            st.sync()
            per = [(own, 2 * 9), (s('smx_ready'), 2), (s('sdif_ready'), 2), (s('sdiag_ready'), 2), (s('ssub_ready'), 2), (s('ctx_ready'), 2)]
            for p in range(2):
                sequence(0, p)
            st.loop(1, NS // 2, lambda i: [sequence(i, p) for p in range(2)], per)
            residual('outc')
            normalise(3)
            dve.wait_ge(s('out_stored'), 128)
            gate_up('gu1')
            residual('dn1')


def _constants():
    r = np.arange(128)
    row, col = r[:, None], r[None, :]
    m = {'ident': row == col, 'triu': row <= col, 'ones': np.ones((128, 128)),
         'decaymask': np.where(col >= row, 0.0, NEG), 'causal': np.where(col <= row, 0.0, NEG)}
    for n, v in (('ones_d', D), ('ones_128', 128), ('ones_256', 256), ('ones_512', 512), ('ones_96', 96)):
        m[n] = np.full((128, 128), 1.0 / v)
    half = RD // 2
    for n, base in (('rot96', NOPE), ('rot32', 0)):
        z = np.zeros((128, 128))
        for e in range(half):
            z[base + half + e, base + e] = -1.0
            z[base + e, base + half + e] = 1.0
        m[n] = z
    z = np.zeros((128, 8, 16))
    for t in range(8):
        for p in range(128):
            z[p, t, 2 * t + p // 64] = 1.0 / QH
    m['headsel'] = z.reshape(128, 128)
    for l in range(LV + 1):
        b = 2 ** l
        m[f'inv{l}'] = (row // (2 * b) == col // (2 * b)) & ((col // b) % 2 == 1) & ((row // b) % 2 == 0)
    return np.stack([np.asarray(m[n], np.float32) for n in CONSTS], axis=1)


def _rope_tables():
    f32 = np.float32
    half = RD // 2
    freq = (f32(10000.0) ** (-np.arange(half, dtype=f32) / f32(half))).astype(f32)
    pos = np.concatenate([np.arange(T, dtype=f32), np.full(NS, NPG * 128, f32)])
    ang = (pos[:, None] * freq[None, :]).astype(f32)
    cos, sin = np.cos(ang).T.astype(f32), np.sin(ang).T.astype(f32)
    cos, sin = np.concatenate([cos, cos]), np.concatenate([sin, sin])
    t = np.zeros((128, 4, TOK), f32)
    t[0:NOPE, 0] = 1.0
    t[NOPE:QH, 0], t[NOPE:QH, 1] = cos, sin
    t[0:RD, 2], t[0:RD, 3] = cos, sin
    return t


def _cols(v, n):
    return np.ascontiguousarray(np.asarray(v).reshape(n, 128).T)


def _tiles(w, m=128):
    k, n = w.shape
    return np.ascontiguousarray(w.reshape(k // 128, 128, n // m, m).transpose(2, 1, 0, 3)).reshape(n // m, 128, -1)


def kernel(**inputs):
    import concourse.bacc as _bacc
    from concourse.bass_utils import run_bass_kernel_spmd as _run
    I = {k: np.asarray(v) for k, v in inputs.items()}
    f = {}
    x = np.concatenate([I['x_prompt'][0], I['x_sample'][:, 0]], axis=0)
    f['x'] = np.ascontiguousarray(x.T.reshape(KD, 128, TOK).transpose(1, 0, 2))
    w = I['w_in_a'][0]
    c = np.cumsum([0, 1536, 512, 4, 4, 512, 1024, 8])
    qkv, gz, ga, gb, sz, xbc, dt = (w[:, c[i]:c[i + 1]] for i in range(7))
    f['w_proj'] = _tiles(np.concatenate([qkv, xbc, gz, sz], axis=1))
    f['w_gate'] = np.ascontiguousarray(np.concatenate([ga, dt, gb], axis=1).reshape(KD, 128, NGATE).transpose(1, 0, 2))
    f['w_outa'], f['w_outc'] = _tiles(I['w_out_a'][0]), _tiles(I['w_out_c'][0])
    for l in range(2):
        gu = I['w_gate_up'][l].reshape(D, 2, KF, 128).transpose(0, 2, 1, 3).reshape(D, 2 * DFF)
        f[f'w_gu{l}'] = _tiles(gu)
        f[f'w_dn{l}'] = np.ascontiguousarray(I['w_down'][l].reshape(2, 11, 128, KD, 128).transpose(3, 0, 2, 1, 4)).reshape(16, 128, SLOT)
    wc = I['w_in_c'][0]
    uk = I['w_uk'][0]
    f['w_inc'] = np.concatenate([_tiles(wc[:, 0:768]), uk.reshape(2, 128, 1024)], axis=0)
    f['w_kr'] = np.ascontiguousarray(wc[:, 768:800].reshape(KD, 128, RD).transpose(1, 0, 2))
    f['w_uq'] = _tiles(I['w_uq'][0], QH)
    f['w_uv'] = np.ascontiguousarray(I['w_uv'][0].reshape(2, 128, 1024).transpose(1, 0, 2))
    f['w_ukt'] = np.ascontiguousarray(uk.transpose(1, 2, 0).reshape(8, 128, 256).transpose(1, 0, 2))
    f['consts'] = _constants()
    f['rope'] = _rope_tables()
    sel = np.zeros((8, 8, 128), np.float32)
    for b in range(8):
        sel[b, b] = 1.0
    f['selb'] = sel
    f['gains'] = np.stack([_cols(v, KD) for v in (I['norm_mix_a'][0], I['norm_ffn'][0], I['norm_mix_c'][0], I['norm_ffn'][1])], axis=1)
    cw = np.concatenate([I['conv_gdn_w'][0], I['conv_ssm_w'][0]], axis=1)
    f['convw'] = np.ascontiguousarray(cw.reshape(4, NCONV, 128).transpose(2, 1, 0))
    f['convb'] = _cols(np.concatenate([np.zeros(1536, np.float32), I['conv_ssm_b'][0]]), NCONV)
    sm = np.zeros((128, NSMALL), np.float32)
    sm[:, C_GDN] = I['gdn_norm'][0]
    sm[:, C_D:C_D + 4] = _cols(np.repeat(I['ssm_D'][0], 64), 4)
    sm[:, C_SSM:C_SSM + 4] = _cols(I['ssm_norm'][0], 4)
    sm[:, C_QA:C_QA + 4] = _cols(I['q_a_norm'][0], 4)
    sm[:, C_KVA:C_KVA + 2] = _cols(I['kv_a_norm'][0], 2)
    sm[0:QH, C_QN] = I['q_norm'][0]
    sm[0:RD, C_KR] = I['k_norm'][0][NOPE:]
    sm[:, C_EPS] = EPS
    sm[:, C_KN] = np.tile(I['k_norm'][0][:NOPE], 2)
    f['small'] = sm
    gc = np.concatenate([I['gdn_dt_bias'][0], I['ssm_dt_bias'][0], np.zeros(GH, np.float32), I['gdn_A_log'][0], I['ssm_A_log'][0]])
    f['gatec'] = np.ascontiguousarray(np.broadcast_to(gc, (128, NGATE + NDEC)))
    pv = np.concatenate([I['state_gdn_conv'][0], I['state_ssm_conv'][0]], axis=2)
    f['prev'] = np.ascontiguousarray(pv.reshape(NS, 3, NCONV, 128).transpose(3, 2, 1, 0))
    f['s_gdn'] = np.ascontiguousarray(I['state_gdn'][0].transpose(2, 1, 0, 3))
    f['s_ssm'] = np.ascontiguousarray(I['state_ssm'][0].transpose(3, 0, 1, 2)).reshape(128, NS, 512)
    f['page_table'] = np.ascontiguousarray(I['page_table'].reshape(1, NS * NPG))
    cm = I['cache_mla'][0]
    f['cache'] = np.ascontiguousarray(cm)
    f['cache_ct'] = np.ascontiguousarray(cm[:, :, 0:256].reshape(NPOOL, 128, 2, 128).transpose(0, 3, 2, 1))
    f['cache_kt'] = np.ascontiguousarray(cm[:, :, 256:288].transpose(0, 2, 1))

    nc = _bacc.Bacc("TRN2", target_bir_lowering=False, num_devices=1)
    arrays, A, O = {}, {}, {}
    for n, a in f.items():
        arrays[f"in_{n}"] = a
        A[n] = nc.dram_tensor(f"in_{n}", a.shape, mybir.dt.from_np(a.dtype), kind="ExternalInput").ap()
    outs = {'y': (128, KD, TOK), 'p_gdn': (128, 512), 'p_ssm': (128, 512), 'conv_p': (128, NCONV, 3), 'conv_s': (128, NCONV, 3, NS),
            's_gdn': (128, GH, NS, 128), 's_ssm': (128, NS, 512), 'rows_c': (128, 2, TOK), 'rows_k': (RD, TOK), 'rows_r': (16, TOK)}
    for n, shape in outs.items():
        O[n] = nc.dram_tensor(f"out_{n}", shape, F32, kind="ExternalOutput").ap()
    build(nc, A, O)
    r = _run(nc, [arrays], core_ids=[0]).results[0]
    g = {n: np.asarray(r[f"out_{n}"]) for n in outs}
    y = g['y'].transpose(1, 0, 2).reshape(D, TOK).T
    y_prompt, y_sample = y[None, :T], y[T:, None]
    p_gdn = g['p_gdn'].reshape(128, GH, 128).transpose(1, 0, 2)[None, None]
    s_gdn = g['s_gdn'].transpose(2, 1, 0, 3)[None]
    p_ssm = g['p_ssm'].reshape(128, SH, 64).transpose(1, 2, 0)[None, None]
    s_ssm = g['s_ssm'].reshape(128, NS, SH, 64).transpose(1, 2, 3, 0)[None]
    cp = g['conv_p'].transpose(2, 1, 0).reshape(3, NCONV * 128)
    cs = g['conv_s'].transpose(3, 2, 1, 0).reshape(NS, 3, NCONV * 128)
    rows = np.concatenate([g['rows_c'].transpose(1, 0, 2).reshape(256, TOK), g['rows_k'], g['rows_r']], axis=0).T
    out = (y_prompt, y_sample, p_gdn, cp[None, None, :, :1536], p_ssm, cp[None, None, :, 1536:], rows[None, None, :T],
           s_gdn, cs[None, :, :, :1536], s_ssm, cs[None, :, :, 1536:], rows[None, T:, None])
    return tuple(np.ascontiguousarray(o) for o in out)
```

```python
import numpy as np
import concourse.bass as bass
from concourse import mybir
from contextlib import ExitStack

F32, F32R = mybir.dt.float32, mybir.dt.float32r
ACT = mybir.ActivationFunctionType
ALU = mybir.AluOpType
AX = mybir.AxisListType

T, NS = 512, 8
TOK = T + NS
HALF = TOK // 2
D, DFF = 1024, 2816
KD, KF = D // 128, DFF // 128
EPS = 1e-6
GH, SH, SG = 4, 8, 2
NCH = T // 128
NDEC = GH + SH
NGATE = NDEC + GH
NCONV = 20
LV = 6
MH, NOPE, RD, QH, VH = 16, 64, 32, 96, 64
NPG, NPOOL = 8, 80
PROW = 256 + 3 * 128
PSCALE = QH ** -0.5
NEG = -1e30
SLOT = KD * 128

TQ, TK, TV, TX, TB, TC, TZ, TSZ = 0, 4, 8, 12, 16, 18, 20, 24

R_L2, R_MIX, R_CQ, R_KV, R_KEY, R_HEAD = 1, 9, 17, 18, 19, 20
R_NORM = (0, 15, 16, R_HEAD + MH)
STAGES = [('proj', 7, 28), ('outa', 2, 8), ('gu0', 11, 44), ('dn0', 6, 8), ('inc', 2, 14), ('uq', 4, 0),
          ('outc', 2, 8), ('gu1', 11, 44), ('dn1', 6, 8)]
TURNS = {n: g for n, g, _ in STAGES}
GBASE = {n: sum(g for _, g, _ in STAGES[:k]) for k, (n, _, _) in enumerate(STAGES)}
TBASE = {n: sum(t for _, _, t in STAGES[:k]) // 2 for k, (n, _, _) in enumerate(STAGES)}

FBASE = {'gu0': 0, 'dn0': 44, 'gu1': 68, 'dn1': 112}
DOWN = [8, 8, 6]
LN_EXP = 'natural_log_exp_and_others'

CONSTS = ['ident', 'triu', 'decaymask', 'causal', 'ones', 'ones_d', 'ones_128', 'ones_256', 'ones_512',
          'ones_96', 'rot96', 'rot32', 'headsel'] + [f'inv{l}' for l in range(LV + 1)]
C_GDN, C_D, C_SSM, C_QA, C_KVA, C_QN, C_KR, C_KN, C_EPS, NSMALL = 0, 1, 5, 9, 13, 15, 16, 17, 18, 19
SMALLS = ['w_gate', 'gains', 'convw', 'convb', 'small', 'gatec', 'prev', 'selb']


class Steps:

    def __init__(self, eng, own):
        self.eng, self.own, self.count, self.shift, self.last = eng, own, {}, {}, None

    def __call__(self, ins, sem=None):
        sem = sem or self.own
        ins.then_inc(sem, 1)
        self.count[sem.name] = self.count.get(sem.name, 0) + 1
        self.last = sem

    def sync(self):
        self.eng.wait_ge(self.last, self.shift.get(self.last.name, 0) + self.count[self.last.name])

    def loop(self, first, last, body, per):
        before = dict(self.count)
        with self.eng.Fori(first, last) as i:
            self.shift = {s.name: (i - first) * n for s, n in per}
            body(i)
        for s, n in per:
            made = self.count.get(s.name, 0) - before.get(s.name, 0)
            assert made == n, (s.name, made, n)
            self.count[s.name] = before.get(s.name, 0) + (last - first) * n
        looped = [s.name for s, _ in per]
        assert all(k in looped or v == before.get(k, 0) for k, v in self.count.items()), self.count
        self.shift = {}


def build(nc, A, O):
    ctx = ExitStack()
    with ctx:
        def sb(name, *shape):
            return ctx.enter_context(nc.sbuf_tensor(name, list(shape), F32))

        def sem(name):
            return ctx.enter_context(nc.semaphore(name))

        def by3(ap):
            return ap.rearrange("p (a t) -> p a t", t=TOK)

        PS = ctx.enter_context(nc.psum_tensor("PS", [128, 8, 512], F32))
        xres = sb("xres", 128, KD, TOK)
        WORK = 12480
        base = nc.sbuf_base
        arena = sb("arena", 128, (2 * KD + 28) * TOK + WORK)
        xn = by3(arena[:, 0:KD * TOK])
        mix = by3(arena[:, KD * TOK:2 * KD * TOK])
        hid = by3(arena[:, 2 * KD * TOK:(2 * KD + 28) * TOK])
        work = arena[:, (2 * KD + 28) * TOK:]

        def split(name, first, tiles):
            return nc.alloc_sbuf_tensor_at(name, [128, tiles, TOK], F32R, offset=base + 4 * first * TOK)

        xnh, xnl = split("xnh", 0, KD), split("xnl", KD, KD)
        hidh, hidl = split("hidh", 2 * KD, KF), split("hidl", 2 * KD + KF, KF)
        tail = (2 * KD + 2 * KF) * TOK
        spots = [nc.alloc_sbuf_tensor_at(f"wsplit{e}", [128, SLOT], F32R, offset=base + 4 * (tail + e * SLOT)) for e in range(3)]
        stream = nc.sbuf_base
        ring_words = sb("ring_words", 128, 5 * SLOT)
        wring = [nc.alloc_sbuf_tensor_at(f"wring{u}", [128, SLOT], F32, offset=stream + 4 * u * SLOT) for u in range(4)]
        spots.append(nc.alloc_sbuf_tensor_at("wsplit3", [128, SLOT], F32R, offset=stream + 16 * SLOT))
        whi, wlo = spots[0:2], spots[2:4]
        cst = sb("cst", 128, len(CONSTS), 128)
        rinv, sqsum, sq = sb("rinv", 128, 2, TOK), sb("sqsum", 128, TOK), sb("sq", 128, 2, TOK)
        selb = sb("selb", 8, 8, 128)
        gains, convw, convb = sb("gains", 128, 4, KD), sb("convw", 128, NCONV, 4), sb("convb", 128, NCONV)
        small, gatec = sb("small", 128, NSMALL), sb("gatec", 128, NGATE + NDEC)
        prev, convout_p, convout_s = sb("prev", 128, NCONV, 3, NS), sb("convout_p", 128, NCONV, 3), sb("convout_s", 128, NCONV, NS)
        wgate = sb("wgate", 128, KD, NGATE)
        graw, gabs, gexp, gone, grec, gln, gsp = (sb(n, 128, 5, NGATE) for n in
                                                  ("graw", "gabs", "gexp", "gone", "grec", "gln", "gsp"))
        la, nega = sb("la", 128, 5, NDEC), sb("nega", 128, NDEC)
        cumt, ecumt, bec = sb("cumt", 128, NCH, NDEC), sb("ecumt", 128, NCH, NDEC), sb("bec", 128, NCH, GH)
        beta, gdt = grec[:, :, NDEC:NGATE], gsp[:, :, GH:NDEC]
        ptab = ctx.enter_context(nc.sbuf_tensor("ptab", [1, NS * NPG], mybir.dt.int32))
        at = [0]

        def take(*shape, rows=128):
            n = int(np.prod(shape))
            v = work[0:rows, at[0]:at[0] + n]
            at[0] += n
            assert at[0] <= WORK, at[0]
            if len(shape) == 2:
                return v.rearrange("p (a b) -> p a b", b=shape[1])
            if len(shape) == 3:
                return v.rearrange("p (a b c) -> p a b c", b=shape[1], c=shape[2])
            return v

        def const(name):
            return cst[:, CONSTS.index(name), :]

        def two(ap):
            return ap.rearrange("p (a t) -> p a t", a=2)

        def bank2(b, rows=128):
            return PS[0:rows, b:b + 2, 0:HALF]

        def by(ap, n):
            return ap.rearrange("p (h x) -> p h x", h=n)

        def over(ap, n):
            return ap.unsqueeze(2).broadcast_to([ap.shape[0], ap.shape[1], n])

        def across(ap, n):
            return ap.unsqueeze(1).broadcast_to([ap.shape[0], n, ap.shape[1]])

        ident = const('ident')

        raw = take(2, 3 + TOK)
        cacc = take(2, TOK)
        at[0] = 0
        arg, dect = xn[:, 0:3, 0:512], xn[:, 3:6, 0:512]
        bm, lt = xn[:, 6, 0:512], xn[:, 7, 0:512]
        xdt, xde = sq[:, 0, 0:512], sq[:, 1, 0:512]
        ecum = take(3, 512)
        attnt, kbe, kdec, vb, xinv, xinvt, yinv, wt, vnew, qe, sgdn, hssd = (take(512) for _ in range(12))
        mt = take(LV + 1, 512)
        scoret = take(2, 512)
        ce = (rinv[:, 0, 0:512], sqsum[:, 0:512])
        btm, kd, kdarg = rinv[:, 1, 0:256], take(NDEC), take(NDEC)
        at[0] = 0
        s0, h0 = take(GH, NS, 128), take(NS, 512)
        vals, valx, valb, ab = take(24), take(24, NS), take(24, NS), take(NDEC, NS)
        rhs2, vnt, qkp, vrow = take(GH * NS, 2), take(GH, NS), take(GH, NS), take(512)
        kb8, bcp, apx = take(GH, NS), take(SG, NS), take(4, 2, NS)
        xds, ysm, yt2, xrow, supd = take(4, NS), take(4, NS), take(4, NS), take(512), take(2, 512)
        sgate = nc.alloc_sbuf_tensor_at("sgate", [128, 2, TOK], F32, offset=base + 4 * ((2 * KD + 28) * TOK + WORK - 2 * TOK))
        at[0] = 0
        krrot, invr, cosg, qs = take(TOK, rows=32), take(TOK, rows=16), take(TOK), take(MH, NS)
        wkr, rotg, rotk = take(KD, RD), take(QH), take(RD, rows=32)
        vol = at[0]
        krraw, krg, krsq, krt = (work[0:32, vol + i * TOK:vol + (i + 1) * TOK] for i in range(4))
        qraw, qsq, qt1, qt2 = (take(TOK) for _ in range(4))
        qhd, khd, pm, ptsb, otm = take(2, TOK), take(2, T), take(4, 512), take(1280), take(4, 128)
        invm = take(2, T, rows=16)
        mx, nb, den, rden = (take(4) for _ in range(4))
        cqn, clat, knope, rope = hid[:, 0:4], hid[:, 4:6], hid[:, 6:14], hid[:, 14:18]
        hflat = hid[:, 18:28].rearrange("p a t -> p (a t)")
        wuv = hflat[:, 0:2048].rearrange("p (k n) -> p k n", k=2)
        wukt = hflat[:, 2048:4096].rearrange("p (h c) -> p h c", h=8)
        vtok = xn[:, :, :].rearrange("p a t -> p (a t)")[:, 0:4096].rearrange("p (a n) -> p a n", a=4)
        hs = [4096]

        def htake(a, b, rows=128):
            v = hflat[0:rows, hs[0]:hs[0] + a * b].rearrange("p (a b) -> p a b", b=b)
            hs[0] += a * b
            assert hs[0] <= 5200
            return v

        qkn = htake(8, 2 * NS).rearrange("p m (e b) -> p m e b", e=2)
        qa = hflat[:, hs[0]:hs[0] + 256].rearrange("p (k h b) -> p k h b", k=2, b=NS); hs[0] += 256
        ctxt = hflat[:, hs[0]:hs[0] + 256].rearrange("p (k h b) -> p k h b", k=2, b=NS); hs[0] += 256
        qr, snew, pnd, pnn = htake(MH, NS, rows=32), htake(1, NS, rows=16)[:, 0, :], htake(MH, NS, rows=16), htake(1, NS, rows=16)[:, 0, :]
        m16, nb16, den16, pn16, rden16 = (htake(1, 2, rows=16)[:, 0, :] for _ in range(5))
        pagebuf = [flat[:, 0:NPG * PROW].rearrange("p (g r) -> p g r", g=NPG)
                   for flat in (hid[:, 6:18].rearrange("p a t -> p (a t)"), ring_words, work[:, vol:], work[:, vol + NPG * PROW:])]
        values = xn.rearrange("p a t -> p (a t)")
        prob = values[0:16, 0:2048].rearrange("p (a n) -> p a n", a=2)
        spt = values[:, 2048:2304].rearrange("p (a n) -> p a n", a=2)
        ctxn = values[0:16, 2304:2816].rearrange("p (a n) -> p a n", a=2)
        qseq = values[:, 2816:2912].rearrange("p (a k h) -> p a k h", a=2, k=3)

        x_loaded, c_loaded, g_loaded = sem("x_loaded"), sem("c_loaded"), sem("g_loaded")
        w_loaded = [sem(f"w_loaded{u}") for u in range(4)]
        gemm_ready = [sem(f"gemm_ready{p}") for p in range(2)]
        tile_taken = [sem(f"tile_taken{p}") for p in range(2)]
        pages_loaded = [sem(f"pages_loaded{p}") for p in range(4)]

        names = """sq_ready sq_added sq_zeroed ssq_mm xn_ready gates_mm gprep_ready gact_ready la_ready 
            cumt_ready ecumt_ready raw_ready zeroed conv_done silu_done l2sq_ready l2_mm l2_done
            cumB_mm arg_ready ecum_ready dect_ready kd_ready betaB_mm bm_ready kk_mm qk_mm ktm_mm vtm_mm
            lt_ready attn_ready kvs_ready mt_ready xinit_mm xinit_ready y_mm y_ready p_mm pt_mm x_ready vnew_mm
            w_mm w_ready qe_ready vnew_ready ot_mm ot_taken kv_mm s_ready bc_mm xtm_mm btm_mm score_ready
            xdt_ready btm_ready ce_ready yt_mm yt_taken hup_mm h_ready rec_stored st_loaded
            sprep_ready spread_mm valb_ready spread_ready rhs2_ready sv_mm vnt_ready qks_mm row_mm row_ready
            sel_mm sel_taken y0_mm xds_ready hsel_mm hsel_taken s_decayed osq_ready osq_mm
            mix_ready dve_own kr_mm kr_raw krsq_ready cq_sq cq_mm cq_ready rot_ready krot_ready
            kn_sq kn_mm kn_sum ln_ready rinv_ready v_mm v_ready q_mm qsq_ready qss_mm qrot_mm qh_ready
            invm_ready invb_mm k_ready s_mm nb_ready p_ready pt2_mm pt2_taken o_mm otm_ready ott_mm omix_ready
            gk_ready sample_mm qa_ready snew_ready sc_mm smx_ready 
            sp_ready ctx_mm ctx_ready so_ready y_stored out_stored
            w_hi w_split part_done xn_raw xn_hi hid_hi hid_ready sc_taken spt_mm
            spt_taken ctt_mm rden_ready ctxn_ready qseq_ready""".split()
        sems = {n: sem(n) for n in names}

        def s(name):
            return sems[name]

        def slot_freed(stage, i, u):
            tb = TBASE[stage]
            if stage in FBASE:
                return s('w_split'), i * 4 + (FBASE[stage] + u + 1)
            if stage == 'uq':
                return s('q_mm'), i * 4 + (u + 1)
            if stage == 'inc':
                return gemm_ready[u % 2], tb + (u // 2 + 1 if i == 0 else 3 if u < 2 else 7)
            return gemm_ready[u % 2], tb + i * 2 + (u // 2 + 1)

        block = ctx.enter_context(nc.Block())

        @block.sync
        def _(sp_):
            for k in range(2):
                sp_.dma_start(xres[:, 4 * k:4 * k + 4], A['x'][:, 4 * k:4 * k + 4]).then_inc(x_loaded, 16)
            sp_.dma_start(ptab[:, :], A['page_table']).then_inc(x_loaded, 16)

            def load(stage, i, u):
                if stage in ('dn0', 'dn1'):
                    tile, part = divmod(i * 4 + u, 3)
                    first, n = sum(DOWN[:part]) * 128, DOWN[part] * 128
                    src = A['w_' + stage][tile, :, first:first + n]
                else:
                    n, src = 4 * QH if stage == 'uq' else SLOT, A['w_' + stage][i * 4 + u]
                sp_.dma_start(wring[u][:, 0:n], src).then_inc(w_loaded[u], 16)

            def pages():
                sp_.wait_ge(x_loaded, 48)

                for b in range(NS):
                    if b >= 4:
                        sp_.wait_ge(s('ctx_mm'), b - 3)
                    elif b == 0:
                        sp_.wait_ge(s('qh_ready'), MH)
                        sp_.wait_ge(s('k_ready'), MH)
                    elif b == 1:
                        sp_.wait_ge(s('q_mm'), MH)
                    else:
                        sp_.wait_ge(s('omix_ready'), MH // 2)
                    for g in range(NPG):
                        page = sp_.value_load(ptab[0:1, b * NPG + g:b * NPG + g + 1], min_val=0, max_val=NPOOL - 1)
                        sp_.dma_start(pagebuf[b % 4][:, g], A['pages'][bass.ds(page, 1)].rearrange("a p r -> p (a r)"))\
                            .then_inc(pages_loaded[b % 4], 16)

            before = None
            for stage, turns, _ in STAGES:
                for u in range(4):
                    if before == 'uq':
                        sp_.wait_ge(s('ctx_mm'), 6)
                    elif before:
                        sp_.wait_ge(*slot_freed(before, TURNS[before] - 1, u))
                    load(stage, 0, u)
                if stage in ('inc', 'dn0', 'dn1'):
                    for i in range(1, turns):
                        for u in range(4):
                            sp_.wait_ge(*slot_freed(stage, i - 1, u))
                            load(stage, i, u)
                else:
                    with sp_.Fori(1, turns) as i:
                        for u in range(4):
                            sp_.wait_ge(*slot_freed(stage, i - 1, u))
                            load(stage, i, u)
                before = stage
                if stage == 'uq':
                    pages()
            for p in range(2):
                sp_.wait_ge(tile_taken[p], TBASE['dn1'] + 4)
            sp_.dma_start(O['y'], xres[:, :, :]).then_inc(s('y_stored'), 16)
            sp_.wait_ge(s('y_stored'), 16)

        @block.gpsimd
        def _(pool):
            pool.dma_start(cst[:, :, :], A['consts']).then_inc(c_loaded, 16)
            for dst, src in zip((wgate, gains, convw, convb, small, gatec, prev, selb), SMALLS):
                pool.dma_start(dst[:], A[src]).then_inc(g_loaded, 16)

            def sum_squares(n):
                if n:
                    pool.wait_ge(s('ssq_mm'), n)
                pool.memset(sqsum[:, :], 0.0).then_inc(s('sq_zeroed'), 1)
                pool.wait_ge(s('sq_zeroed'), n + 1)
                for k in range(KD):
                    pool.wait_ge(s('sq_ready'), 8 * n + k + 1)
                    if n or k:
                        pool.wait_ge(s('sq_added'), 8 * n + k)
                    pool.tensor_tensor(sqsum[:, :], sqsum[:, :], sq[:, k % 2, :], ALU.add).then_inc(s('sq_added'), 1)

            pool.memset(raw[:, 0, 0:3], 0.0)
            pool.memset(raw[:, 1, 0:3], 0.0).then_inc(s('zeroed'), 1)
            sum_squares(0)
            pool.wait_ge(s('silu_done'), NCONV)
            pool.memset(sgdn, 0.0)
            pool.memset(hssd, 0.0).then_inc(s('zeroed'), 1)
            for c in range(NCH):
                pool.wait_ge(s('lt_ready'), c + 1)
                if c:
                    pool.wait_ge(s('x_ready'), LV * c)
                for l in range(LV + 1):
                    pool.tensor_tensor(by(mt[:, l], GH), by(lt, GH), across(const(f'inv{l}'), GH), ALU.mult)\
                        .then_inc(s('mt_ready'), 1)
            pool.wait_ge(s('s_ready'), NCH)
            pool.wait_ge(s('h_ready'), NCH)
            pool.dma_start(O['p_gdn'], sgdn).then_inc(s('rec_stored'), 16)
            pool.dma_start(O['p_ssm'], hssd).then_inc(s('rec_stored'), 16)
            pool.dma_start(O['conv_p'], convout_p[:, :, :]).then_inc(s('out_stored'), 16)
            pool.wait_ge(s('rec_stored'), 32)
            pool.wait_ge(s('ot_taken'), NCH)
            pool.wait_ge(s('yt_taken'), NCH)
            pool.dma_start(s0, A['s_gdn']).then_inc(s('st_loaded'), 16)
            pool.dma_start(h0, A['s_ssm']).then_inc(s('st_loaded'), 16)
            pool.wait_ge(s('spread_ready'), 1)
            pool.wait_ge(s('sv_mm'), 1)
            pool.wait_ge(s('y0_mm'), 1)
            for h in range(GH):
                pool.tensor_tensor(s0[:, h], s0[:, h], over(ab[:, h], 128), ALU.mult).then_inc(s('s_decayed'), 1)
            for b in range(NS):
                pool.tensor_tensor(by(h0[:, b], SH), by(h0[:, b], SH), over(ab[:, GH:, b], 64), ALU.mult)\
                    .then_inc(s('s_decayed'), 1)
            pool.dma_start(O['conv_s'][:, :, 2], convout_s[:, :, :]).then_inc(s('out_stored'), 16)
            pool.dma_start(O['conv_s'][:, :, 0:2], prev[:, :, 1:3]).then_inc(s('out_stored'), 16)
            pool.wait_ge(s('sel_taken'), NS)
            pool.dma_start(O['s_gdn'], s0).then_inc(s('out_stored'), 16)
            pool.wait_ge(s('hsel_taken'), NS)
            pool.dma_start(O['s_ssm'], h0).then_inc(s('out_stored'), 16)
            sum_squares(1)
            sum_squares(2)
            pool.wait_ge(s('out_stored'), 80)
            for dst, src in ((wkr, 'w_kr'), (rope, 'rope'), (wuv, 'w_uv'), (wukt, 'w_ukt')):
                pool.dma_start(dst, A[src]).then_inc(g_loaded, 16)
            pool.wait_ge(s('cq_ready'), 2)
            pool.dma_start(O['rows_c'], clat).then_inc(s('out_stored'), 16)
            pool.wait_ge(s('krot_ready'), 1)
            pool.dma_start(O['rows_k'], krrot).then_inc(s('out_stored'), 16)
            pool.wait_ge(s('rinv_ready'), R_KEY + 1)
            pool.dma_start(O['rows_r'], invr).then_inc(s('out_stored'), 16)
            pool.wait_ge(s('qa_ready'), 1)
            pool.wait_ge(s('gk_ready'), 1)
            pool.wait_ge(s('omix_ready'), MH // 2)

            def queries(i, p, first=False):
                b = i * 2 + p
                at_ = slice(b, b + 1) if isinstance(b, int) else bass.ds(b, 1)
                if not first:
                    pool.wait_ge(s('sc_mm'), b - 1)
                pool.tensor_copy(qseq[:, p, 0:2, :].unsqueeze(3), qa[:, :, :, at_])
                pool.tensor_copy(qseq[0:32, p, 2, :].unsqueeze(2), qr[:, :, at_]).then_inc(s('qseq_ready'), 1)
            for p in range(2):
                queries(0, p, first=True)
            with pool.Fori(1, NS // 2) as i:
                for p in range(2):
                    queries(i, p)
            sum_squares(3)
            pool.wait_ge(s('out_stored'), 128)

        @block.tensor
        def _(pe):
            def mm(out, lhsT, rhs, start=True, stop=True):
                return pe.matmul(out, lhsT, rhs, start=start, stop=stop)

            def both(b, lhsT, rhs, start=True, stop=True):
                for h in range(2):
                    last = mm(PS[0:lhsT.shape[1], b + h, 0:HALF], lhsT, rhs[:, h * HALF:(h + 1) * HALF], start, stop)
                return last

            def ffn(stage, high, low):
                def piece(p, u, chunks, k0, last, done):
                    for k in range(chunks):
                        wh, wl = (w[u % 2][:, k * 128:(k + 1) * 128] for w in (whi, wlo))
                        both(2 * p, wh, high[:, k0 + k, :], k0 + k == 0, False)
                        both(2 * p, wh, low[:, k0 + k, :], False, False)
                        ins = both(2 * p, wl, high[:, k0 + k, :], False, last and k == chunks - 1)
                    ins.then_inc(done, 1)

                def up(i):
                    for u in range(4):
                        p = u % 2
                        pe.wait_ge(tile_taken[p], i * 2 + (TBASE[stage] + u // 2))
                        pe.wait_ge(s('w_split'), i * 4 + (FBASE[stage] + u + 1))
                        piece(p, u, KD, 0, True, gemm_ready[p])

                def down(i):
                    for e in range(12):
                        tile, part = divmod(e, 3)
                        p = tile % 2
                        if part == 0:
                            pe.wait_ge(tile_taken[p], i * 2 + (TBASE[stage] + tile // 2))
                        pe.wait_ge(s('w_split'), i * 12 + (FBASE[stage] + e + 1))
                        piece(p, e, DOWN[part], sum(DOWN[:part]), part == 2, gemm_ready[p] if part == 2 else s('part_done'))
                with pe.Fori(0, 2 if stage in ('dn0', 'dn1') else TURNS[stage]) as i:
                    down(i) if stage in ('dn0', 'dn1') else up(i)

            def gemm(stage, rhs, first=0, last=None):
                def turn(i):
                    for u in range(4):
                        pe.wait_ge(w_loaded[u], i * 16 + 16 * (GBASE[stage] + 1))
                        p = u % 2
                        pe.wait_ge(tile_taken[p], i * 2 + (TBASE[stage] + u // 2))
                        for k in range(KD):
                            ins = both(2 * p, wring[u][:, k * 128:(k + 1) * 128], rhs(k), k == 0, k == KD - 1)
                        ins.then_inc(gemm_ready[p], 1)
                last = TURNS[stage] if last is None else last
                if stage == 'proj' and first == 0:
                    turn(0)
                    first = 1
                if last - first > 1:
                    with pe.Fori(first, last) as i:
                        turn(i)
                else:
                    turn(first)

            def norm_sum(n):
                pe.wait_ge(s('sq_added'), 8 * (n + 1))
                both(4, const('ones_d'), sqsum).then_inc(s('ssq_mm'), 1)
                pe.wait_ge(s('xn_ready'), 8 * (n + 1))

            pe.wait_ge(c_loaded, 16)
            pe.wait_ge(g_loaded, 16 * len(SMALLS))
            norm_sum(0)
            for t in range(5):
                for k in range(KD):
                    toks = slice(t * 128, min((t + 1) * 128, TOK))
                    ins = mm(PS[0:toks.stop - toks.start, 6, t * NGATE:(t + 1) * NGATE], xn[:, k, toks], wgate[:, k, :],
                             k == 0, k == KD - 1)
            ins.then_inc(s('gates_mm'), 1)
            gemm('proj', lambda k: xn[:, k, :], 0, 5)
            pe.wait_ge(s('la_ready'), 1)
            for c in range(NCH):
                ins = mm(PS[:, 7, c * NDEC:(c + 1) * NDEC], const('triu'), la[:, c, :])
            ins.then_inc(s('gates_mm'), 1)
            for j in range(8):
                pe.wait_ge(s('l2sq_ready'), j + 1)
                if j >= 2:
                    pe.wait_ge(s('ln_ready'), R_L2 + j - 1)
                if j == 1:
                    pe.wait_ge(s('cumt_ready'), 1)
                both(4 + 2 * (j % 2), const('ones'), sq[:, j % 2, :]).then_inc(s('l2_mm'), 1)
            gemm('proj', lambda k: xn[:, k, :], 5, 7)

            pe.wait_ge(s('cumt_ready'), 1)
            pe.wait_ge(s('l2_done'), 8)
            pe.wait_ge(s('silu_done'), NCONV)
            for p in range(2):
                pe.wait_ge(tile_taken[p], 14)
            pe.wait_ge(s('ln_ready'), R_L2 + 8)
            for c in range(NCH):
                ts = slice(c * 128, (c + 1) * 128)
                if c:
                    pe.wait_ge(s('yt_taken'), c)
                    pe.wait_ge(s('h_ready'), c)
                    pe.wait_ge(s('ot_taken'), c)
                for h in range(NDEC):
                    ins = mm(PS[:, h // 4, (h % 4) * 128:(h % 4 + 1) * 128],
                             la[:, c, h:h + 1].broadcast_to([128, 128]), const('triu'))
                ins.then_inc(s('cumB_mm'), 1)
                if c:
                    pe.wait_ge(s('w_ready'), c)
                for h in range(GH):
                    ins = mm(PS[:, 3, h * 128:(h + 1) * 128], beta[:, c, h:h + 1].broadcast_to([128, 128]), ident)
                ins.then_inc(s('betaB_mm'), 1)
                if c:
                    pe.wait_ge(s('x_ready'), LV * c)
                for h in range(GH):
                    ins = mm(PS[:, 4, h * 128:(h + 1) * 128], hid[:, TK + h, ts], hid[:, TK + h, ts])
                ins.then_inc(s('kk_mm'), 1)
                for h in range(GH):
                    ins = mm(PS[:, 5, h * 128:(h + 1) * 128], hid[:, TK + h, ts], hid[:, TQ + h, ts])
                ins.then_inc(s('qk_mm'), 1)
                if c:
                    pe.wait_ge(s('vnew_ready'), c)
                for h in range(GH):
                    ins = pe.transpose(PS[:, 6, h * 128:(h + 1) * 128], hid[:, TK + h, ts], ident)
                ins.then_inc(s('ktm_mm'), 1)
                if c:
                    pe.wait_ge(s('s_ready'), c)
                for h in range(GH):
                    ins = pe.transpose(PS[:, 7, h * 128:(h + 1) * 128], hid[:, TV + h, ts], ident)
                ins.then_inc(s('vtm_mm'), 1)
                pe.wait_ge(s('ecum_ready'), c + 1)
                pe.wait_ge(s('arg_ready'), c + 1)
                for g in range(SG):
                    ins = mm(PS[:, 0, g * 128:(g + 1) * 128], hid[:, TB + g, ts], hid[:, TC + g, ts])
                ins.then_inc(s('bc_mm'), 1)
                for m in range(4):
                    ins = pe.transpose(PS[:, 1, m * 128:(m + 1) * 128], hid[:, TX + m, ts], ident)
                ins.then_inc(s('xtm_mm'), 1)
                for g in range(SG):
                    ins = pe.transpose(PS[:, 2, g * 128:(g + 1) * 128], hid[:, TB + g, ts], ident)
                ins.then_inc(s('btm_mm'), 1)
                pe.wait_ge(s('mt_ready'), (LV + 1) * c + 1)
                pe.wait_ge(s('bm_ready'), c + 1)
                for h in range(GH):
                    ins = mm(PS[:, 3, h * 128:(h + 1) * 128], mt[:, 0, h * 128:(h + 1) * 128], ident)
                ins.then_inc(s('xinit_mm'), 1)
                pe.wait_ge(s('xinit_ready'), c + 1)
                for l in range(LV):
                    n = LV * c + l
                    pe.wait_ge(s('mt_ready'), (LV + 1) * c + l + 2)
                    if l:
                        pe.wait_ge(s('x_ready'), n)
                    for h in range(GH):
                        hs_ = slice(h * 128, (h + 1) * 128)
                        ins = mm(PS[:, 3, hs_], mt[:, l + 1, hs_], xinv[:, hs_])
                    ins.then_inc(s('y_mm'), 1)
                    if l == 0:
                        pe.wait_ge(s('lt_ready'), c + 1)
                        pe.wait_ge(s('attn_ready'), c + 1)
                    pe.wait_ge(s('y_ready'), n + 1)
                    if l < LV - 1:
                        for h in range(GH):
                            hs_ = slice(h * 128, (h + 1) * 128)
                            ins = mm(PS[:, 4, hs_], xinvt[:, hs_], yinv[:, hs_])
                        ins.then_inc(s('p_mm'), 1)
                    for h in range(GH):
                        hs_ = slice(h * 128, (h + 1) * 128)
                        ins = mm(PS[:, 5, hs_], yinv[:, hs_], xinvt[:, hs_])
                    ins.then_inc(s('pt_mm'), 1)
                    if l == 1:
                        pe.wait_ge(s('score_ready'), c + 1)
                        pe.wait_ge(s('xdt_ready'), c + 1)
                        pe.wait_ge(s('ce_ready'), c + 1)
                        if c == 0:
                            pe.wait_ge(s('zeroed'), 2)
                        for h in range(SH):
                            o = PS[64 * (h % 2):64 * (h % 2) + 64, 0, (h // 2) * 128:(h // 2 + 1) * 128]
                            gs = slice((h % 4) * 128, (h % 4 + 1) * 128)
                            mm(o, xdt[:, h * 64:(h + 1) * 64], scoret[:, h // 4, gs], True, False)
                            ins = mm(o, hssd[:, h * 64:(h + 1) * 64], ce[h // 4][:, gs], False, True)
                        ins.then_inc(s('yt_mm'), 1)
                    if l == 2:
                        pe.wait_ge(s('btm_ready'), c + 1)
                        for g in range(SG):
                            ins = mm(PS[:, 1, g * 256:(g + 1) * 256], btm[:, g * 128:(g + 1) * 128],
                                     xde[:, g * 256:(g + 1) * 256])
                        ins.then_inc(s('hup_mm'), 1)
                pe.wait_ge(s('x_ready'), LV * (c + 1))
                pe.wait_ge(s('kvs_ready'), c + 1)
                for h in range(GH):
                    hs_ = slice(h * 128, (h + 1) * 128)
                    ins = mm(PS[:, 3, hs_], kbe[:, hs_], xinvt[:, hs_])
                ins.then_inc(s('w_mm'), 1)
                pe.wait_ge(s('w_ready'), c + 1)
                for h in range(GH):
                    hs_ = slice(h * 128, (h + 1) * 128)
                    mm(PS[:, 6, hs_], xinvt[:, hs_], vb[:, hs_], True, False)
                    ins = mm(PS[:, 6, hs_], wt[:, hs_], sgdn[:, hs_], False, True)
                ins.then_inc(s('vnew_mm'), 1)
                pe.wait_ge(s('vnew_ready'), c + 1)
                pe.wait_ge(s('qe_ready'), c + 1)
                pe.wait_ge(s('attn_ready'), c + 1)
                for h in range(GH):
                    hs_ = slice(h * 128, (h + 1) * 128)
                    mm(PS[:, 2, hs_], sgdn[:, hs_], qe[:, hs_], True, False)
                    ins = mm(PS[:, 2, hs_], vnew[:, hs_], attnt[:, hs_], False, True)
                ins.then_inc(s('ot_mm'), 1)
                for h in range(GH):
                    hs_ = slice(h * 128, (h + 1) * 128)
                    ins = mm(PS[:, 7, hs_], kdec[:, hs_], vnew[:, hs_])
                ins.then_inc(s('kv_mm'), 1)

            pe.wait_ge(s('sprep_ready'), 1)
            pe.wait_ge(s('yt_taken'), NCH)
            mm(PS[:, 0, 0:192], const('ones')[0:8, :], valx[0:8].rearrange("p a b -> p (a b)")).then_inc(s('spread_mm'), 1)
            pe.wait_ge(s('x_ready'), LV * NCH)
            for m in range(4):
                for e in range(2):
                    lhsT = supd[0:8, e, m * 128:(m + 1) * 128]
                    ins = mm(PS[:, 4, (m * 2 + e) * NS:(m * 2 + e + 1) * NS], lhsT, ident[0:8, 0:8])
            ins.then_inc(s('spread_mm'), 1)
            pe.wait_ge(s('sprep_ready'), 2)
            pe.wait_ge(s('ot_taken'), NCH)
            mm(PS[:, 2, 0:GH * NS], const('ones'), qkp.rearrange("p a b -> p (a b)")).then_inc(s('qks_mm'), 1)
            pe.wait_ge(s('sprep_ready'), 3)
            mm(PS[:, 5, 0:SG * NS], const('ones'), bcp.rearrange("p a b -> p (a b)")).then_inc(s('qks_mm'), 1)
            pe.wait_ge(s('st_loaded'), 32)
            pe.wait_ge(s('rhs2_ready'), 1)
            pe.wait_ge(s('h_ready'), NCH)
            for h in range(GH):
                for b in range(NS):
                    e = h * NS + b
                    ins = mm(PS[:, 1, 2 * e:2 * e + 2], s0[:, h, b, :], rhs2[:, e, :])
            ins.then_inc(s('sv_mm'), 1)
            pe.wait_ge(s('vnew_ready'), NCH)
            for b in range(NS):
                for m in range(4):
                    ins = mm(PS[:, 6, m * NS + b:m * NS + b + 1], h0[:, b, m * 128:(m + 1) * 128],
                             hid[:, TC + m // 2, T + b:T + b + 1])
            ins.then_inc(s('y0_mm'), 1)
            pe.wait_ge(s('vnt_ready'), 1)
            for h in range(GH):
                ins = pe.transpose(PS[0:8, 3, h * 128:(h + 1) * 128], vnt[:, h, :], ident)
            ins.then_inc(s('row_mm'), 1)
            pe.wait_ge(s('xds_ready'), 1)
            pe.wait_ge(s('s_ready'), NCH)
            for m in range(4):
                ins = pe.transpose(PS[0:8, 7, m * 128:(m + 1) * 128], xds[:, m, :], ident)
            ins.then_inc(s('row_mm'), 1)
            pe.wait_ge(s('row_ready'), 1)
            pe.wait_ge(s('valb_ready'), 1)
            pe.wait_ge(s('spread_ready'), 1)
            for b in range(NS):
                if b >= 2:
                    pe.wait_ge(s('sel_taken'), b - 1)
                mm(PS[:, b % 2, :], selb[:, b, :], vrow[0:8, :]).then_inc(s('sel_mm'), 1)
            pe.wait_ge(s('row_ready'), 2)
            for b in range(NS):
                if b >= 2:
                    pe.wait_ge(s('hsel_taken'), b - 1)
                mm(PS[:, 2 + b % 2, :], selb[:, b, :], xrow[0:8, :]).then_inc(s('hsel_mm'), 1)
            for j in range(8):
                e = j if j < 4 else 4 + (j - 4) // 2
                pe.wait_ge(s('osq_ready'), j + 1)
                if e >= 2 and (j < 4 or j % 2 == 0):
                    pe.wait_ge(s('ln_ready'), R_MIX + e - 1)
                both(4 + 2 * (e % 2), const('ones_128' if j < 4 else 'ones_256'), sq[:, j % 2, :],
                     j < 4 or j % 2 == 0, j < 4 or j % 2 == 1).then_inc(s('osq_mm'), 1)
            pe.wait_ge(s('mix_ready'), 8)
            pe.wait_ge(s('sel_taken'), NS)
            pe.wait_ge(s('hsel_taken'), NS)
            gemm('outa', lambda k: mix[:, k, :])
            norm_sum(1)
            ffn('gu0', xnh, xnl)
            pe.wait_ge(s('hid_ready'), KF)
            ffn('dn0', hidh, hidl)
            norm_sum(2)

            tb = TBASE['inc']

            def mean_square(j):
                pe.wait_ge(s('cq_sq'), j + 1)
                if j == 4:
                    pe.wait_ge(tile_taken[0], tb + 3)
                both(6 if j < 4 else 0, const('ones_512' if j < 4 else 'ones_256'), sq[:, j % 2, :],
                     j in (0, 4), j in (3, 5)).then_inc(s('cq_mm'), 1)
            for j in range(6):
                pe.wait_ge(w_loaded[j % 4], 16 * (GBASE['inc'] + j // 4 + 1))
                pe.wait_ge(tile_taken[j % 2], tb + j // 2)
                for k in range(KD):
                    ins = both(2 * (j % 2), wring[j % 4][:, k * 128:(k + 1) * 128], xn[:, k, :], k == 0, k == KD - 1)
                ins.then_inc(gemm_ready[j % 2], 1)
                if 1 <= j <= 4:
                    mean_square(j - 1)
            pe.wait_ge(g_loaded, 16 * (len(SMALLS) + 4))
            for k in range(KD):
                ins = both(4, wkr[:, k, :], xn[:, k, :], k == 0, k == KD - 1)
            ins.then_inc(s('kr_mm'), 1)
            mean_square(4)
            mean_square(5)
            pe.wait_ge(s('kr_raw'), 1)
            pe.wait_ge(s('rot_ready'), 1)
            both(4, rotk, krraw).then_inc(s('kr_mm'), 1)
            pe.wait_ge(s('cq_ready'), 2)
            for m in range(8):
                p = m % 2
                if m < 2:
                    pe.wait_ge(w_loaded[2 + m], 16 * (GBASE['inc'] + 2))
                    pe.wait_ge(w_loaded[3], 16 * (GBASE['inc'] + 2))
                pe.wait_ge(tile_taken[p], tb + 3 + m // 2)
                for k in range(2):
                    ins = both(2 * p, wring[2 + k][:, m * 128:(m + 1) * 128], clat[:, k, :], k == 0, k == 1)
                ins.then_inc(gemm_ready[p], 1)
                if m:
                    pe.wait_ge(s('kn_sq'), m)
                    both(6, const('headsel')[:, (m - 1) * 16:m * 16], sq[:, (m - 1) % 2, :], m == 1, False).then_inc(s('kn_mm'), 1)
            pe.wait_ge(s('kn_sq'), 8)
            both(6, const('headsel')[:, 112:128], sq[:, 1, :], False, False).then_inc(s('kn_mm'), 1)
            pe.wait_ge(s('krsq_ready'), 1)
            both(6, const('ones_96')[0:32, 0:16], krsq, False, True).then_inc(s('kn_sum'), 1)
            pe.wait_ge(s('krot_ready'), 1)
            for n in range(8):
                if n >= 2:
                    pe.wait_ge(s('v_ready'), n - 1)
                for k in range(2):
                    ins = mm(PS[:, 4 + n % 2, :], clat[:, k, (n // 2) * 128:(n // 2 + 1) * 128],
                             wuv[:, k, (n % 2) * 512:(n % 2 + 1) * 512], k == 0, k == 1)
                ins.then_inc(s('v_mm'), 1)

            def key_scale(n, b):
                pe.wait_ge(s('ln_ready'), n + (R_HEAD + 1))
                pe.wait_ge(s('invm_ready'), n + 1)
                mm(PS[0:QH, 2, :], const('ones')[0:16, 0:QH], invm[:, b, :]).then_inc(s('invb_mm'), 1)

            def step(i, u, last=False):
                h = i * 4 + u
                b = u % 2
                if not last:
                    pe.wait_ge(s('qh_ready'), h + 1)
                    g = i if u < 3 else i + 1
                    pe.wait_ge(w_loaded[(u + 1) % 4], g * 16 + 16 * (GBASE['uq'] + 1))
                    for k in range(4):
                        ins = both(0, wring[(u + 1) % 4][:, k * QH:(k + 1) * QH], cqn[:, k, :], k == 0, k == 3)
                    ins.then_inc(s('q_mm'), 1)
                pe.wait_ge(s('qh_ready'), h + 1)
                pe.wait_ge(s('k_ready'), h + 1)
                pe.wait_ge(s('pt2_taken'), h)
                pe.wait_ge(s('otm_ready'), h)
                for q in range(4):
                    ins = mm(PS[:, 4 + q, 0:(q + 1) * 128], qhd[0:QH, b, q * 128:(q + 1) * 128],
                             khd[0:QH, b, 0:(q + 1) * 128])
                ins.then_inc(s('s_mm'), 1)
                if not last:
                    pe.wait_ge(s('qsq_ready'), h + 2)
                    pe.wait_ge(s('k_ready'), h + 1)
                    pe.wait_ge(s('omix_ready'), i * 2 + u // 2)
                    both(2, const('ones_96')[0:QH, 0:QH], qsq[0:QH, :]).then_inc(s('qss_mm'), 1)
                    both(0, rotg[0:QH, :], qraw[0:QH, :]).then_inc(s('qrot_mm'), 1)
                    key_scale(h + 1, 1 - b)
                pe.wait_ge(s('p_ready'), h + 1)
                n = 0
                for kb in range(4):
                    for q in range(kb, 4):
                        ins = pe.transpose(PS[:, 4 + n // 4, (n % 4) * 128:(n % 4 + 1) * 128],
                                           pm[:, q, kb * 128:(kb + 1) * 128], ident)
                        n += 1
                ins.then_inc(s('pt2_mm'), 1)
                pe.wait_ge(s('pt2_taken'), h + 1)
                first = [0, 4, 7, 9]
                for q in range(4):
                    for kb in range(q + 1):
                        n = first[kb] + q - kb
                        ins = mm(PS[:, 7, q * VH:(q + 1) * VH], ptsb[:, n * 128:(n + 1) * 128],
                                 vtok[:, kb, bass.ds(h * VH, VH)] if not isinstance(h, int) else vtok[:, kb, h * VH:(h + 1) * VH],
                                 kb == 0, kb == q)
                ins.then_inc(s('o_mm'), 1)
                if u % 2:
                    pe.wait_ge(s('otm_ready'), h + 1)
                    if not last:
                        pe.wait_ge(s('ln_ready'), h + (R_HEAD + 2))
                    for q in range(4):
                        ins = pe.transpose(PS[:, 3, q * 128:(q + 1) * 128], otm[:, q, :], ident)
                    ins.then_inc(s('ott_mm'), 1)

            for p in range(2):
                pe.wait_ge(tile_taken[p], tb + 7)
            pe.wait_ge(w_loaded[0], 16 * (GBASE['uq'] + 1))
            for k in range(4):
                ins = both(0, wring[0][:, k * QH:(k + 1) * QH], cqn[:, k, :], k == 0, k == 3)
            ins.then_inc(s('q_mm'), 1)
            pe.wait_ge(s('qsq_ready'), 1)
            both(2, const('ones_96')[0:QH, 0:QH], qsq[0:QH, :]).then_inc(s('qss_mm'), 1)
            both(0, rotg[0:QH, :], qraw[0:QH, :]).then_inc(s('qrot_mm'), 1)
            key_scale(0, 0)
            pe.wait_ge(s('v_ready'), 8)
            pe.wait_ge(s('rinv_ready'), R_KEY + 1)
            for u in range(4):
                step(0, u)
            with pe.Fori(1, MH // 4 - 1) as i:
                for u in range(4):
                    step(i, u)
            for u in range(4):
                step(MH // 4 - 1, u, last=u == 3)

            pe.wait_ge(s('gk_ready'), 1)
            for m in range(MH // 2):
                for k in range(2):
                    e = (k * 8 + m) * 2 * NS
                    ins = mm(PS[:, 0, e:e + 2 * NS], wukt[:, m, k * 128:(k + 1) * 128], qkn[:, m].rearrange("p e b -> p (e b)"))
            ins.then_inc(s('sample_mm'), 1)
            pe.wait_ge(s('qa_ready'), 1)
            for b in range(NS):
                for k in range(2):
                    mm(PS[0:16, 4, b:b + 1], qa[:, k, :, b], clat[:, k, T + b:T + b + 1], k == 0, False)
                ins = mm(PS[0:16, 4, b:b + 1], qr[:, :, b], krrot[:, T + b:T + b + 1], False, True)
            ins.then_inc(s('sample_mm'), 1)

            def scores(b):
                p, buf = b % 2, pagebuf[b % 4]
                pe.wait_ge(pages_loaded[b % 4], 16 * NPG * (b // 4 + 1))
                pe.wait_ge(s('qseq_ready'), b + 1)
                if b >= 2:
                    pe.wait_ge(s('sc_taken'), b - 1)
                for half in range(2):
                    o, gs = PS[0:16, 2 * p + half, :], slice(4 * half, 4 * half + 4)
                    for k in range(2):
                        mm(o, qseq[:, p, k, :], buf[:, gs, 256 + k * 128:384 + k * 128], k == 0, False)
                    ins = mm(o, qseq[0:32, p, 2, :], buf[0:32, gs, 512:640], False, True)
                ins.then_inc(s('sc_mm'), 1)

            def context_turned(p):
                for k in range(2):
                    ins = mm(PS[:, 7, k * 16:(k + 1) * 16], ctxn[:, p, k * 128:(k + 1) * 128], ident[0:16, 0:16])
                ins.then_inc(s('ctt_mm'), 1)

            pe.wait_ge(s('omix_ready'), MH // 2)
            scores(0)
            for b in range(NS):
                p = b % 2
                if b + 1 < NS:
                    scores(b + 1)
                pe.wait_ge(s('sp_ready'), b + 1)
                if b >= 2:
                    pe.wait_ge(s('spt_taken'), b - 1)
                for g in range(NPG):
                    ins = pe.transpose(PS[:, 4 + p, g * 16:(g + 1) * 16], prob[:, p, g * 128:(g + 1) * 128], ident[0:16, 0:16])
                ins.then_inc(s('spt_mm'), 1)
                if b:
                    if b >= 2:
                        pe.wait_ge(s('ctx_ready'), b - 1)
                    pe.wait_ge(s('ctxn_ready'), b)
                    context_turned(1 - p)
                pe.wait_ge(s('spt_taken'), b + 1)
                for g in range(NPG):
                    ins = mm(PS[0:16, 6, 0:256], spt[:, p, g * 16:(g + 1) * 16], pagebuf[b % 4][:, g, 0:256], g == 0, g == NPG - 1)
                ins.then_inc(s('ctx_mm'), 1)
            pe.wait_ge(s('ctx_ready'), NS - 1)
            pe.wait_ge(s('ctxn_ready'), NS)
            context_turned(1)
            pe.wait_ge(s('snew_ready'), 2)
            pe.wait_ge(s('spt_taken'), NS)
            mm(PS[:, 5, 0:MH * NS], const('ones')[0:16, :], pnd.rearrange("p h b -> p (h b)")).then_inc(s('sample_mm'), 1)
            pe.wait_ge(s('snew_ready'), 3)
            for m in range(MH // 2):
                for k in range(2):
                    ins = mm(PS[:, 7, m * 16:(m + 1) * 16], wuv[:, k, m * 128:(m + 1) * 128],
                             ctxt[:, k, 2 * m:2 * m + 2, :].rearrange("p h b -> p (h b)"), k == 0, k == 1)
            ins.then_inc(s('sample_mm'), 1)
            pe.wait_ge(s('so_ready'), 1)
            gemm('outc', lambda k: mix[:, k, :])
            norm_sum(3)
            ffn('gu1', xnh, xnl)
            pe.wait_ge(s('hid_ready'), 2 * KF)
            ffn('dn1', hidh, hidl)

        @block.scalar
        def _(act):
            act.preload_act_table_set(LN_EXP)
            act.wait_ge(c_loaded, 16)
            act.wait_ge(g_loaded, 16 * len(SMALLS))

            def square(n, k, ready):
                act.wait_ge(*ready)
                if 8 * n + k >= 2:
                    act.wait_ge(s('sq_added'), 8 * n + k - 1)
                act.activation(sq[:, k % 2, :], xres[:, k, :], ACT.Square).then_inc(s('sq_ready'), 1)

            def rsqrt(r, out, mean):
                act.activation(out, mean, ACT.Ln, bias=small[0:out.shape[0], C_EPS:C_EPS + 1]).then_inc(s('ln_ready'), 1)
                act.wait_ge(s('ln_ready'), r + 1)
                act.activation(out, out, ACT.Exp, scale=-0.5).then_inc(s('rinv_ready'), 1)

            def norm_root(n):
                act.wait_ge(s('ssq_mm'), n + 1)
                rsqrt(R_NORM[n], two(rinv[:, R_NORM[n] % 2, :]), bank2(4))

            def high(stage, i, u):
                w = SLOT if stage[0] == 'g' else DOWN[(i * 4 + u) % 3] * 128
                act.wait_ge(w_loaded[u], i * 16 + 16 * (GBASE[stage] + 1))
                act.activation(whi[u % 2][:, 0:w], wring[u][:, 0:w], ACT.Copy).then_inc(s('w_hi'), 1)

            def ffn(l, n, before):
                gu, dn = f'gu{l}', f'dn{l}'
                for k in range(KD):
                    square(n, k, (tile_taken[k % 2], TBASE[before] + k // 2 + 1))
                for u in range(2):
                    high(gu, 0, u)
                norm_root(n)
                for k in range(KD):
                    act.wait_ge(s('xn_raw'), KD * l + k + 1)
                    act.activation(xnh[:, k, :], sgate[:, k % 2, :], ACT.Copy).then_inc(s('xn_hi'), 1)
                act.wait_ge(s('out_stored'), 80 if l == 0 else 128)

                def turn(i, first=False, last=False):
                    for u in range(4):
                        q, j = u // 2, i * 2 + u // 2
                        act.wait_ge(gemm_ready[u % 2], j + (TBASE[gu] + 1))
                        if u < 2:
                            high(gu, i, u + 2)
                        elif last:
                            high(dn, 0, u - 2)
                        else:
                            high(gu, i + 1, u - 2)
                        if u % 2 == 0:
                            if not (l == 0 and first):
                                act.wait_ge(s('hid_ready'), j + (KF * l - 1))
                            act.activation(two(sgate[:, q, :]), bank2(0), ACT.Silu).then_inc(tile_taken[0], 1)
                        else:
                            act.wait_ge(tile_taken[1], j + (TBASE[gu] + 1))
                            hq = hidh[:, j, :]
                            act.activation(hq, sgate[:, q, :], ACT.Copy).then_inc(s('hid_hi'), 1)
                turn(0, first=True)
                with act.Fori(1, TURNS[gu] - 1) as i:
                    turn(i)
                turn(TURNS[gu] - 1, last=True)
                if l == 0:
                    act.preload_act_table_set(LN_EXP)
                for e in range(3 * KD):
                    tile, part = divmod(e, 3)
                    if part < 2:
                        act.wait_ge(s('part_done'), 2 * KD * l + 2 * tile + part + 1)
                    else:
                        act.wait_ge(gemm_ready[tile % 2], TBASE[dn] + tile // 2 + 1)
                    if e + 2 < 3 * KD:
                        high(dn, (e + 2) // 4, (e + 2) % 4)
                    if part == 2 and l == 0:
                        square(2, tile, (tile_taken[tile % 2], TBASE[dn] + tile // 2 + 1))
                if l == 0:
                    norm_root(2)

            for k in range(KD):
                square(0, k, (x_loaded, 48))
            norm_root(0)
            act.activation(nega[:, :], gatec[:, NGATE:], ACT.Exp).then_inc(s('gact_ready'), 1)
            act.wait_ge(s('gprep_ready'), 1)
            act.activation(gexp[:, :, 0:NDEC], gabs[:, :, 0:NDEC], ACT.Exp, scale=-1.0)
            act.activation(gexp[:, :, NDEC:], graw[:, :, NDEC:], ACT.Exp, scale=-1.0).then_inc(s('gact_ready'), 1)
            act.wait_ge(s('gprep_ready'), 2)
            act.activation(gln[:, :, 0:NDEC], gone[:, :, 0:NDEC], ACT.Ln).then_inc(s('gact_ready'), 1)
            act.wait_ge(s('zeroed'), 1)

            def conv_turn(i, first):
                def take_tile(u):
                    p = u % 2
                    act.wait_ge(gemm_ready[p], i * 2 + (u // 2 + 1))
                    if not (first and u < 2):
                        act.wait_ge(s('conv_done'), i * 4 + (u - 1))
                    act.activation(two(raw[:, p, 3:3 + TOK]), bank2(2 * p), ACT.Copy).then_inc(s('raw_ready'), 1)
                    act.activation(convout_p[:, i * 4 + u, :], PS[:, 2 * p + 1, T - 3 - HALF:T - HALF], ACT.Copy)
                    act.activation(convout_s[:, i * 4 + u, :], PS[:, 2 * p + 1, T - HALF:HALF], ACT.Copy)\
                        .then_inc(tile_taken[p], 1)

                def silu(u):
                    act.wait_ge(s('conv_done'), i * 4 + (u + 1))
                    bias = convb[:, bass.ds(i * 4 + u, 1)] if not isinstance(i, int) else convb[:, i * 4 + u:i * 4 + u + 1]
                    act.activation(hid[:, i * 4 + u, :], cacc[:, u % 2, :], ACT.Silu, bias=bias)\
                        .then_inc(s('silu_done'), 1)
                take_tile(0)
                for u in range(1, 4):
                    take_tile(u)
                    silu(u - 1)
                silu(3)
            conv_turn(0, True)
            with act.Fori(1, 5) as i:
                conv_turn(i, False)

            act.preload_act_table_set(LN_EXP)

            def l2_root(j):
                act.wait_ge(s('l2_mm'), j + 1)
                if j >= 2:
                    act.wait_ge(s('l2_done'), j - 1)
                rsqrt(R_L2 + j, two(rinv[:, (R_L2 + j) % 2, :]), bank2(4 + 2 * (j % 2)))
            for j in range(8):
                act.wait_ge(s('silu_done'), NCONV)
                if j >= 2:
                    act.wait_ge(s('l2_mm'), j - 1)
                act.activation(sq[:, j % 2, :], hid[:, j, :], ACT.Square).then_inc(s('l2sq_ready'), 1)
                if j:
                    l2_root(j - 1)
            l2_root(7)
            with act.Fori(0, 2) as i:
                for u in range(4):
                    act.wait_ge(gemm_ready[u % 2], i * 2 + (10 + u // 2 + 1))
                    act.activation(two(hid[:, i * 4 + (TZ + u), :]), bank2(2 * (u % 2)), ACT.Silu)\
                        .then_inc(tile_taken[u % 2], 1)
            act.preload_act_table_set(LN_EXP)
            act.wait_ge(s('cumt_ready'), 1)
            act.activation(ecumt[:, :, :], cumt[:, :, :], ACT.Exp).then_inc(s('ecumt_ready'), 1)

            for c in range(NCH):
                act.wait_ge(s('cumB_mm'), c + 1)
                if c:
                    act.wait_ge(s('s_ready'), c)
                    act.wait_ge(s('h_ready'), c)
                act.activation(ecum, PS[:, 0:3, :], ACT.Exp).then_inc(s('ecum_ready'), 1)
                act.wait_ge(s('arg_ready'), c + 1)
                act.activation(kd, kdarg, ACT.Exp).then_inc(s('kd_ready'), 1)
                act.activation(dect, arg, ACT.Exp).then_inc(s('dect_ready'), 1)
                act.wait_ge(s('btm_mm'), c + 1)
                act.activation(btm, PS[:, 2, 0:256], ACT.Copy).then_inc(s('btm_ready'), 1)
                for l in range(LV):
                    act.wait_ge(s('y_mm'), LV * c + l + 1)
                    act.activation(yinv, PS[:, 3, :], ACT.Copy).then_inc(s('y_ready'), 1)
                act.wait_ge(s('w_mm'), c + 1)
                act.activation(wt, PS[:, 3, :], ACT.Copy, scale=-1.0).then_inc(s('w_ready'), 1)
                act.wait_ge(s('vnew_mm'), c + 1)
                act.activation(vnew, PS[:, 6, :], ACT.Copy).then_inc(s('vnew_ready'), 1)
                act.wait_ge(s('ot_mm'), c + 1)
                act.activation(mix[:, 0:4, c * 128:(c + 1) * 128], by(PS[:, 2, :], GH), ACT.Copy).then_inc(s('ot_taken'), 1)

            act.wait_ge(s('spread_mm'), 1)
            act.activation(ab, PS[:, 0, 0:NDEC * NS].rearrange("p (a b) -> p a b", b=NS), ACT.Exp).then_inc(s('spread_ready'), 1)
            act.wait_ge(s('spread_mm'), 2)
            apx_ps = PS[:, 4, 0:64].rearrange("p (m e b) -> p m e b", e=2, b=NS)
            act.activation(apx[:, :, 0, :], apx_ps[:, :, 0, :], ACT.Exp)
            act.activation(apx[:, :, 1, :], apx_ps[:, :, 1, :], ACT.Copy).then_inc(s('spread_ready'), 1)
            act.wait_ge(s('row_mm'), 1)
            act.activation(vrow[0:8, :], PS[0:8, 3, :], ACT.Copy).then_inc(s('row_ready'), 1)
            act.wait_ge(s('row_mm'), 2)
            act.activation(xrow[0:8, :], PS[0:8, 7, :], ACT.Copy).then_inc(s('row_ready'), 1)
            act.wait_ge(s('xds_ready'), 2)

            def mix_root(e):
                act.wait_ge(s('osq_mm'), e + 1 if e < 4 else 4 + 2 * (e - 3))
                if e >= 2:
                    act.wait_ge(s('mix_ready'), e - 1)
                rsqrt(R_MIX + e, two(rinv[:, (R_MIX + e) % 2, :]), bank2(4 + 2 * (e % 2)))
            for j in range(8):
                if j >= 2:
                    act.wait_ge(s('osq_mm'), j - 1)
                act.activation(sq[:, j % 2, :], mix[:, j, :], ACT.Square).then_inc(s('osq_ready'), 1)
                if 1 <= j <= 4:
                    mix_root(j - 1)
                elif j == 6:
                    mix_root(4)
            mix_root(5)
            ffn(0, 1, 'outa')

            tb = TBASE['inc']
            for j in range(6):
                act.wait_ge(gemm_ready[j % 2], tb + j // 2 + 1)
                if j >= 2:
                    act.wait_ge(s('cq_mm'), j - 1)
                act.activation(two(sq[:, j % 2, :]), bank2(2 * (j % 2)), ACT.Square).then_inc(s('cq_sq'), 1)
                act.activation(two(hid[:, j, :]), bank2(2 * (j % 2)), ACT.Copy).then_inc(tile_taken[j % 2], 1)
            for r, b, n in ((R_CQ, 6, 4), (R_KV, 0, 6)):
                act.wait_ge(s('cq_mm'), n)
                rsqrt(r, two(rinv[:, r % 2, :]), bank2(b))
            act.wait_ge(s('kr_mm'), 1)
            act.activation(two(krsq), bank2(4, 32), ACT.Square).then_inc(s('krsq_ready'), 1)
            act.activation(two(krraw), bank2(4, 32), ACT.Copy).then_inc(s('kr_raw'), 1)
            for m in range(8):
                p = m % 2
                act.wait_ge(gemm_ready[p], tb + 3 + m // 2 + 1)
                if m >= 2:
                    act.wait_ge(s('kn_mm'), m - 1)
                act.activation(two(sq[:, p, :]), bank2(2 * p), ACT.Square).then_inc(s('kn_sq'), 1)
                act.activation(two(knope[:, m, :]), bank2(2 * p), ACT.Copy, scale=small[:, C_KN:C_KN + 1])\
                    .then_inc(tile_taken[p], 1)
            act.wait_ge(s('kn_sum'), 1)
            rsqrt(R_KEY, two(invr), bank2(6, 16))
            for n in range(8):
                act.wait_ge(s('v_mm'), n + 1)
                act.activation(vtok[:, n // 2, (n % 2) * 512:(n % 2 + 1) * 512], PS[:, 4 + n % 2, :], ACT.Copy)\
                    .then_inc(s('v_ready'), 1)

            def query(h, first=False):
                act.wait_ge(s('q_mm'), h + 1)
                if not first:
                    act.wait_ge(s('qrot_mm'), h)
                    act.wait_ge(s('qh_ready'), h)
                act.activation(two(qraw[0:QH, :]), bank2(0, QH), ACT.Copy)
                act.activation(two(qsq[0:QH, :]), bank2(0, QH), ACT.Square).then_inc(s('qsq_ready'), 1)

            def query_root(h, b):
                act.wait_ge(s('qss_mm'), h + 1)
                rsqrt(h + R_HEAD, two(rinv[0:QH, b, :]), bank2(2, QH))

            def step(i, u, last=False):
                h = i * 4 + u
                if not last:
                    query(h + 1)
                act.wait_ge(s('nb_ready'), h + 1)
                act.wait_ge(s('pt2_mm'), h)
                act.wait_ge(s('otm_ready'), h)
                for q in range(4):
                    ins = act.activation(pm[:, q, 0:(q + 1) * 128], PS[:, 4 + q, 0:(q + 1) * 128], ACT.Exp,
                                         bias=nb[:, q:q + 1], scale=PSCALE, accum_out=den[:, q:q + 1])
                ins.then_inc(s('p_ready'), 1)
                if not last:
                    query_root(h + 1, (u + 1) % 2)
                act.wait_ge(s('pt2_mm'), h + 1)
                act.wait_ge(s('o_mm'), h)
                act.activation(ptsb[:, 0:1024].rearrange("p (a n) -> p a n", a=2), PS[:, 4:6, :], ACT.Copy)
                act.activation(ptsb[:, 1024:1280], PS[:, 6, 0:256], ACT.Copy).then_inc(s('pt2_taken'), 1)
                if u % 2:
                    act.wait_ge(s('ott_mm'), i * 2 + (u // 2 + 1))
                    act.activation(mix[:, i * 2 + u // 2, 0:T], PS[:, 3, :], ACT.Copy).then_inc(s('omix_ready'), 1)
            query(0, True)
            query_root(0, 0)
            for u in range(4):
                step(0, u)
            with act.Fori(1, MH // 4 - 1) as i:
                for u in range(4):
                    step(i, u)
            for u in range(4):
                step(MH // 4 - 1, u, last=u == 3)

            act.wait_ge(s('sample_mm'), 1)
            act.activation(qa[:, :, :, :], PS[:, 0, 0:256].rearrange("p (k h b) -> p k h b", k=2, b=NS), ACT.Copy).then_inc(s('qa_ready'), 1)

            def context_out(b, last):
                act.wait_ge(s('ctt_mm'), last)
                out = ctxt[:, :, :, b] if isinstance(b, int) else ctxt[:, :, :, bass.ds(b, 1)].rearrange("p k h b -> p k (h b)")
                act.activation(out, PS[:, 7, 0:32].rearrange("p (k h) -> p k h", k=2), ACT.Copy).then_inc(s('ctx_ready'), 1)

            def sequence(i, p, first=False):
                b = i * 2 + p
                sn = snew[:, b:b + 1] if isinstance(b, int) else snew[:, bass.ds(b, 1)]
                act.wait_ge(s('smx_ready'), b + 1)
                if not first:
                    act.wait_ge(s('rden_ready'), b - 1)
                act.activation(pn16[:, p:p + 1], sn, ACT.Exp, bias=nb16[:, p:p + 1], scale=PSCALE)
                act.activation(prob[:, p], prob[:, p], ACT.Exp, bias=nb16[:, p:p + 1], scale=PSCALE, accum_out=den16[:, p:p + 1])\
                    .then_inc(s('sp_ready'), 1)
                act.wait_ge(s('spt_mm'), b + 1)
                if not first:
                    act.wait_ge(s('ctx_mm'), b - 1)
                act.activation(spt[:, p], PS[:, 4 + p, 0:128], ACT.Copy).then_inc(s('spt_taken'), 1)
                if not (first and p == 0):
                    context_out(b - 1, b)
                act.wait_ge(s('ctx_mm'), b + 1)
                act.wait_ge(s('rden_ready'), b + 1)
                act.activation(ctxn[:, p], PS[0:16, 6, 0:256], ACT.Copy, scale=rden16[:, p:p + 1]).then_inc(s('ctxn_ready'), 1)
            for p in range(2):
                sequence(0, p, first=True)
            with act.Fori(1, NS // 2) as i:
                for p in range(2):
                    sequence(i, p)
            context_out(NS - 1, NS)
            act.wait_ge(s('sample_mm'), 4)
            for e in range(2):
                so = PS[64 * e:64 * e + 64, 7, 0:MH * NS].rearrange("p (m e b) -> p m e b", e=2, b=NS)
                ins = act.activation(mix[64 * e:64 * e + 64, :, T:TOK], so[:, :, e, :], ACT.Copy)
            ins.then_inc(s('so_ready'), 1)
            ffn(1, 3, 'outc')

        @block.vector
        def _(dve):
            st = Steps(dve, s('dve_own'))
            own = s('dve_own')
            dve.wait_ge(c_loaded, 16)
            dve.wait_ge(g_loaded, 16 * len(SMALLS))
            tt, ts_, stt = dve.tensor_tensor, dve.tensor_scalar, dve.scalar_tensor_tensor

            def normalise(n):
                dve.wait_ge(s('rinv_ready'), R_NORM[n] + 1)
                for k in range(KD):
                    st(stt(out=xn[:, k, :], in0=xres[:, k, :], scalar=gains[:, n, k:k + 1], in1=rinv[:, R_NORM[n] % 2, :],
                           op0=ALU.mult, op1=ALU.mult), s('xn_ready'))

            def residual(stage):
                for k in range(KD):
                    p = k % 2
                    dve.wait_ge(gemm_ready[p], TBASE[stage] + k // 2 + 1)
                    st(tt(two(xres[:, k, :]), two(xres[:, k, :]), bank2(2 * p), ALU.add), tile_taken[p])

            def low(stage, i, u):
                w = SLOT if stage[0] == 'g' else DOWN[(i * 4 + u) % 3] * 128
                dve.wait_ge(s('w_hi'), i * 4 + (FBASE[stage] + u + 1))
                tt(wlo[u % 2][:, 0:w], wring[u][:, 0:w], whi[u % 2][:, 0:w].bitcast(F32), ALU.subtract).then_inc(s('w_split'), 1)

            def ffn(l, n):
                gu, dn = f'gu{l}', f'dn{l}'
                for u in range(2):
                    low(gu, 0, u)
                dve.wait_ge(s('rinv_ready'), R_NORM[n] + 1)

                def raw_tile(k):
                    st(stt(out=sgate[:, k % 2, :], in0=xres[:, k, :], scalar=gains[:, n, k:k + 1], in1=rinv[:, R_NORM[n] % 2, :],
                           op0=ALU.mult, op1=ALU.mult), s('xn_raw'))
                raw_tile(0)
                for k in range(KD):
                    if k + 1 < KD:
                        if k:
                            dve.wait_ge(s('xn_ready'), KD * n + k)
                        raw_tile(k + 1)
                    dve.wait_ge(s('xn_hi'), KD * l + k + 1)
                    st(tt(xnl[:, k, :], sgate[:, k % 2, :], xnh[:, k, :].bitcast(F32), ALU.subtract), s('xn_ready'))
                dve.wait_ge(s('out_stored'), 80 if l == 0 else 128)

                def turn(i, last=False):
                    for u in range(4):
                        q, j = u // 2, i * 2 + u // 2
                        dve.wait_ge(gemm_ready[u % 2], j + (TBASE[gu] + 1))
                        if u % 2:
                            dve.wait_ge(tile_taken[0], j + (TBASE[gu] + 1))
                            tt(two(sgate[:, q, :]), two(sgate[:, q, :]), bank2(2), ALU.mult).then_inc(tile_taken[1], 1)
                        if u < 2:
                            low(gu, i, u + 2)
                        elif last:
                            low(dn, 0, u - 2)
                        else:
                            low(gu, i + 1, u - 2)
                        if u % 2:
                            dve.wait_ge(s('hid_hi'), j + (KF * l + 1))
                            hh, hl = hidh[:, j, :], hidl[:, j, :]
                            tt(hl, sgate[:, q, :], hh.bitcast(F32), ALU.subtract).then_inc(s('hid_ready'), 1)
                with dve.Fori(0, TURNS[gu] - 1) as i:
                    turn(i)
                turn(TURNS[gu] - 1, last=True)
                for e in range(3 * KD):
                    tile, part = divmod(e, 3)
                    p = tile % 2
                    if part == 2:
                        dve.wait_ge(gemm_ready[p], TBASE[dn] + tile // 2 + 1)
                        st(tt(two(xres[:, tile, :]), two(xres[:, tile, :]), bank2(2 * p), ALU.add), tile_taken[p])
                    if e + 2 < 3 * KD:
                        low(dn, (e + 2) // 4, (e + 2) % 4)

            normalise(0)
            dve.wait_ge(s('gates_mm'), 1)
            st(dve.memset(graw[:, :, :], 0.0))
            st.sync()
            st(tt(graw[:, 0:4, :], PS[:, 6, 0:4 * NGATE].rearrange("p (t n) -> p t n", n=NGATE), across(gatec[:, 0:NGATE], 4), ALU.add))
            st(tt(graw[0:NS, 4, :], PS[0:NS, 6, 4 * NGATE:5 * NGATE], gatec[0:NS, 0:NGATE], ALU.add))
            st.sync()
            st(stt(out=gabs[:, :, :], in0=graw[:, :, :], scalar=-1.0, in1=graw[:, :, :], op0=ALU.mult, op1=ALU.max), s('gprep_ready'))
            dve.wait_ge(s('gact_ready'), 2)
            st(ts_(gone[:, :, :], gexp[:, :, :], 1.0, None, ALU.add), s('gprep_ready'))
            st.sync()
            st(dve.reciprocal(grec[:, :, :], gone[:, :, :]))
            dc = slice(0, NDEC)
            st(ts_(gabs[:, :, dc], gone[:, :, dc], -1.0, None, ALU.add))
            st.sync()
            st(tt(gabs[:, :, dc], gexp[:, :, dc], gabs[:, :, dc], ALU.subtract))
            st.sync()
            st(tt(gabs[:, :, dc], gabs[:, :, dc], grec[:, :, dc], ALU.mult))
            dve.wait_ge(s('gact_ready'), 3)
            st.sync()
            st(tt(gabs[:, :, dc], gabs[:, :, dc], gln[:, :, dc], ALU.add))
            st.sync()
            st(stt(out=gsp[:, :, dc], in0=graw[:, :, dc], scalar=0.0, in1=gabs[:, :, dc], op0=ALU.max, op1=ALU.add))
            dve.wait_ge(s('gact_ready'), 1)
            st.sync()
            st(stt(out=la[:, :, :], in0=gsp[:, :, dc], scalar=-1.0, in1=across(nega[:, :], 5), op0=ALU.mult, op1=ALU.mult), s('la_ready'))

            def conv_turn(i, first):
                for u in range(4):
                    p, j = u % 2, i * 4 + u

                    def w(t):
                        return convw[:, j, t:t + 1]
                    dve.wait_ge(s('raw_ready'), j + 1)
                    if not (first and u < 2):
                        dve.wait_ge(s('silu_done'), i * 4 + (u - 1))
                    st(ts_(cacc[:, p, :], raw[:, p, 3:3 + TOK], w(3), None, ALU.mult))
                    for t in range(3):
                        st.sync()
                        st(stt(out=cacc[:, p, T:TOK], in0=prev[:, j, t, :], scalar=w(t), in1=cacc[:, p, T:TOK],
                               op0=ALU.mult, op1=ALU.add))
                        st(stt(out=cacc[:, p, 0:T], in0=raw[:, p, t:t + T], scalar=w(t), in1=cacc[:, p, 0:T],
                               op0=ALU.mult, op1=ALU.add), s('conv_done') if t == 2 else None)
            dve.wait_ge(s('zeroed'), 1)
            conv_turn(0, True)
            st.loop(1, 5, lambda i: conv_turn(i, False), [(own, 24), (s('conv_done'), 4)])

            dve.wait_ge(s('gates_mm'), 2)
            st(dve.tensor_copy(cumt[:, :, :], PS[:, 7, 0:NCH * NDEC].rearrange("p (c n) -> p c n", n=NDEC)), s('cumt_ready'))
            for j in range(8):
                dve.wait_ge(s('rinv_ready'), R_L2 + j + 1)
                st(stt(out=hid[:, j, :], in0=hid[:, j, :], scalar=128 ** -0.5 if j < 4 else 1.0, in1=rinv[:, (R_L2 + j) % 2, :],
                       op0=ALU.mult, op1=ALU.mult), s('l2_done'))
            dve.wait_ge(s('ecumt_ready'), 1)
            st(tt(bec[:, :, :], beta[:, 0:NCH], ecumt[:, :, 0:GH], ALU.mult))
            st.sync()

            ident4 = across(ident, GH)
            for c in range(NCH):
                tc_ = slice(c * 128, (c + 1) * 128)
                dve.wait_ge(s('cumB_mm'), c + 1)
                dve.wait_ge(s('ecum_ready'), c + 1)
                if c == 0:
                    dve.wait_ge(gemm_ready[1], 14)
                    dve.wait_ge(s('silu_done'), NCONV)
                st(tt(kdarg.rearrange("p (a b) -> p a b", b=4), PS[:, 0:3, 127:512:128],
                      cumt[:, c, :].rearrange("p (a b) -> p a b", b=4), ALU.subtract))
                for h in range(NDEC):
                    hs_ = slice((h % 4) * 128, (h % 4 + 1) * 128)
                    st(stt(out=arg[:, h // 4, hs_], in0=PS[:, h // 4, hs_], scalar=cumt[:, c, h:h + 1],
                           in1=const('decaymask'), op0=ALU.subtract, op1=ALU.min), s('arg_ready') if h == NDEC - 1 else None)
                dve.wait_ge(s('dect_ready'), c + 1)
                dve.wait_ge(s('betaB_mm'), c + 1)
                st(tt(bm, dect[:, 0, :], PS[:, 3, :], ALU.mult), s('bm_ready'))
                dve.wait_ge(s('kk_mm'), c + 1)
                st.sync()
                st(tt(lt, PS[:, 4, :], bm, ALU.mult), s('lt_ready'))
                dve.wait_ge(s('qk_mm'), c + 1)
                st(tt(attnt, PS[:, 5, :], dect[:, 0, :], ALU.mult), s('attn_ready'))
                dve.wait_ge(s('mt_ready'), (LV + 1) * c + 1)
                st(tt(by(xinvt, GH), ident4, by(mt[:, 0], GH), ALU.subtract))
                dve.wait_ge(s('xinit_mm'), c + 1)
                st(tt(by(xinv, GH), ident4, by(PS[:, 3, :], GH), ALU.subtract), s('xinit_ready'))
                dve.wait_ge(s('kd_ready'), c + 1)
                dve.wait_ge(s('ktm_mm'), c + 1)
                st(tt(by(kbe, GH), by(PS[:, 6, :], GH), over(bec[:, c, :], 128), ALU.mult))
                st(tt(by(kdec, GH), by(PS[:, 6, :], GH), over(kd[:, 0:GH], 128), ALU.mult))
                dve.wait_ge(s('vtm_mm'), c + 1)
                st(tt(by(vb, GH), by(PS[:, 7, :], GH), over(beta[:, c, :], 128), ALU.mult), s('kvs_ready'))
                fill = []

                def ssd_scores():
                    dve.wait_ge(s('bc_mm'), c + 1)
                    for g in range(SG):
                        st(tt(by(scoret[:, g], 4), by(dect[:, 1 + g, :], 4), across(PS[:, 0, g * 128:(g + 1) * 128], 4), ALU.mult),
                           s('score_ready') if g else None)
                    dve.wait_ge(s('xtm_mm'), c + 1)
                    st(tt(by(xdt, SH), by(PS[:, 1, :], SH), over(gdt[:, c, :], 64), ALU.mult))
                    st.sync()
                    st(tt(by(xde, SH), by(xdt, SH), over(kd[:, GH:], 64), ALU.mult), s('xdt_ready'))
                    dve.wait_ge(s('ecum_ready'), c + 1)
                    for g in range(SG):
                        st(tt(by(ce[g], 4), across(hid[:, TC + g, tc_], 4), by(ecum[:, 1 + g], 4), ALU.mult),
                           s('ce_ready') if g else None)

                def ssd_out():
                    dve.wait_ge(s('yt_mm'), c + 1)
                    for m in range(4):
                        st(stt(out=mix[:, 4 + m, tc_], in0=hid[:, TX + m, tc_], scalar=small[:, C_D + m:C_D + m + 1],
                               in1=PS[:, 0, m * 128:(m + 1) * 128], op0=ALU.mult, op1=ALU.add))
                    st.sync()
                    st(tt(mix[:, 4:8, tc_], mix[:, 4:8, tc_], hid[:, TSZ:TSZ + 4, tc_], ALU.mult), s('yt_taken'))
                    last = ecum[:, 1:3, 127:512:128].rearrange("p a b -> p a b")
                    st(tt(hssd.rearrange("p (a b x) -> p a b x", a=2, b=4), hssd.rearrange("p (a b x) -> p a b x", a=2, b=4),
                          last.unsqueeze(3).broadcast_to([128, 2, 4, 64]), ALU.mult))

                def queries():
                    st(tt(by(qe, GH), hid[:, TQ:TQ + 4, tc_], by(ecum[:, 0], GH), ALU.mult), s('qe_ready'))
                fill = {0: ssd_scores, 2: ssd_out, 3: queries}
                for l in range(LV):
                    if l < LV - 1:
                        dve.wait_ge(s('p_mm'), (LV - 1) * c + l + 1)
                        st(tt(xinv, xinv, PS[:, 4, :], ALU.subtract))
                    dve.wait_ge(s('pt_mm'), LV * c + l + 1)
                    st(tt(xinvt, xinvt, PS[:, 5, :], ALU.subtract), s('x_ready'))
                    if l in fill:
                        fill[l]()
                dve.wait_ge(s('hup_mm'), c + 1)
                st.sync()
                st(tt(hssd, hssd, PS[:, 1, :], ALU.add), s('h_ready'))
                dve.wait_ge(s('kv_mm'), c + 1)
                for h in range(GH):
                    hs_ = slice(h * 128, (h + 1) * 128)
                    st(stt(out=sgdn[:, hs_], in0=sgdn[:, hs_], scalar=ecum[:, 0, h * 128 + 127:h * 128 + 128],
                           in1=PS[:, 7, hs_], op0=ALU.mult, op1=ALU.add), s('s_ready') if h == GH - 1 else None)

            dve.wait_ge(s('rec_stored'), 32)
            dve.wait_ge(s('ot_taken'), NCH)
            sc = slice(T, TOK)
            st(dve.tensor_copy(vals[0:8, 0:12], la[0:8, 4, :]))
            st(dve.tensor_copy(vals[0:8, 12:16], beta[0:8, 4, :]))
            st(dve.tensor_copy(vals[0:8, 16:24], gdt[0:8, 4, :]))
            st.sync()
            for e, col in ((0, GH), (1, 16)):
                st(dve.tensor_copy(by(supd[0:8, e], SH), over(vals[0:8, col:col + SH], 64)))
            st(tt(valx[0:8], over(vals[0:8, :], NS), across(ident[0:8, 0:8], 24), ALU.mult), s('sprep_ready'))
            st(tt(qkp, hid[:, TQ:TQ + 4, sc], hid[:, TK:TK + 4, sc], ALU.mult), s('sprep_ready'))
            st(tt(bcp, hid[:, TB:TB + 2, sc], hid[:, TC:TC + 2, sc], ALU.mult), s('sprep_ready'))
            dve.wait_ge(s('spread_mm'), 1)
            dve.wait_ge(s('spread_ready'), 1)
            st(dve.tensor_copy(valb, PS[:, 0, 0:192].rearrange("p (a b) -> p a b", b=NS)), s('valb_ready'))
            st.sync()
            st(tt(kb8, hid[:, TK:TK + 4, sc], valb[:, 12:16], ALU.mult))
            dve.wait_ge(s('spread_ready'), 1)
            st.sync()
            r2 = rhs2.rearrange("p (h b) e -> p h b e", b=NS)
            st(tt(r2[:, :, :, 0], kb8, ab[:, 0:GH], ALU.mult))
            st(tt(r2[:, :, :, 1], hid[:, TQ:TQ + 4, sc], ab[:, 0:GH], ALU.mult), s('rhs2_ready'))
            st(tt(vnt, hid[:, TV:TV + 4, sc], valb[:, 12:16], ALU.mult))
            dve.wait_ge(s('sv_mm'), 1)
            st.sync()
            sv = PS[:, 1, 0:2 * GH * NS].rearrange("p (h b e) -> p h b e", b=NS, e=2)
            st(tt(vnt, vnt, sv[:, :, :, 0], ALU.subtract), s('vnt_ready'))
            dve.wait_ge(s('qks_mm'), 1)
            st.sync()
            st(tt(kb8, vnt, PS[:, 2, 0:GH * NS].rearrange("p (h b) -> p h b", b=NS), ALU.mult))
            st.sync()
            st(tt(mix[:, 0:4, sc], kb8, sv[:, :, :, 1], ALU.add))
            dve.wait_ge(s('spread_ready'), 2)
            st(tt(xds, hid[:, TX:TX + 4, sc], apx[:, :, 1, :], ALU.mult), s('xds_ready'))
            dve.wait_ge(s('y0_mm'), 1)
            st(tt(ysm, PS[:, 6, 0:32].rearrange("p (m b) -> p m b", b=NS), apx[:, :, 0, :], ALU.mult))
            dve.wait_ge(s('qks_mm'), 2)
            st.sync()
            st(tt(yt2.rearrange("p (g m) b -> p g m b", g=2), xds.rearrange("p (g m) b -> p g m b", g=2),
                  PS[:, 5, 0:16].rearrange("p (g b) -> p g b", b=NS).unsqueeze(2).broadcast_to([128, 2, 2, NS]), ALU.mult))
            st.sync()
            st(tt(ysm, ysm, yt2, ALU.add))
            st.sync()
            st(tt(yt2, hid[:, TX:TX + 4, sc], over(small[:, C_D:C_D + 4], NS), ALU.mult))
            st.sync()
            st(tt(ysm, ysm, yt2, ALU.add))
            st.sync()
            st(tt(mix[:, 4:8, sc], ysm, hid[:, TSZ:TSZ + 4, sc], ALU.mult), s('xds_ready'))
            for b in range(NS):
                dve.wait_ge(s('sel_mm'), b + 1)
                if b >= 2:
                    dve.wait_ge(s('sel_taken'), b - 1)
                st(tt(by(supd[:, b % 2], GH), by(PS[:, b % 2, :], GH), over(hid[:, TK:TK + 4, T + b], 128), ALU.mult))
                st.sync()
                if b == 0:
                    dve.wait_ge(s('s_decayed'), GH)
                st(tt(s0[:, :, b, :], s0[:, :, b, :], by(supd[:, b % 2], GH), ALU.add), s('sel_taken'))
            for b in range(NS):
                dve.wait_ge(s('hsel_mm'), b + 1)
                dve.wait_ge(s('sel_taken'), NS)
                if b >= 2:
                    dve.wait_ge(s('hsel_taken'), b - 1)
                st(tt(by(supd[:, b % 2], 2), by(PS[:, 2 + b % 2, :], 2), over(hid[:, TB:TB + 2, T + b], 256), ALU.mult))
                st.sync()
                dve.wait_ge(s('s_decayed'), GH + b + 1)
                st(tt(h0[:, b], h0[:, b], supd[:, b % 2], ALU.add), s('hsel_taken'))
            for e in range(6):
                dve.wait_ge(s('rinv_ready'), R_MIX + e + 1)
                root = rinv[:, (R_MIX + e) % 2, :]
                if e < 4:
                    st(stt(out=mix[:, e, :], in0=mix[:, e, :], scalar=small[:, C_GDN:C_GDN + 1], in1=root, op0=ALU.mult, op1=ALU.mult))
                    st.sync()
                    st(tt(mix[:, e, :], mix[:, e, :], hid[:, TZ + e, :], ALU.mult), s('mix_ready'))
                else:
                    for m in (2 * e - 4, 2 * e - 3):
                        st(stt(out=mix[:, m, :], in0=mix[:, m, :], scalar=small[:, C_SSM + m - 4:C_SSM + m - 3], in1=root,
                               op0=ALU.mult, op1=ALU.mult), s('mix_ready'))
            residual('outa')
            ffn(0, 1)
            normalise(2)

            dve.wait_ge(g_loaded, 16 * (len(SMALLS) + 4))
            st(ts_(cosg[0:QH, :], rope[0:QH, 0, :], small[0:QH, C_QN:C_QN + 1], None, ALU.mult))
            st(ts_(rotg[0:QH, :], const('rot96')[0:QH, 0:QH], small[0:QH, C_QN:C_QN + 1], None, ALU.mult))
            st(ts_(rotk, const('rot32')[0:32, 0:32], small[0:32, C_KR:C_KR + 1], None, ALU.mult), s('rot_ready'))
            dve.wait_ge(s('rinv_ready'), R_CQ + 1)
            dve.wait_ge(tile_taken[1], TBASE['inc'] + 2)
            for j in range(4):
                st(stt(out=cqn[:, j, :], in0=cqn[:, j, :], scalar=small[:, C_QA + j:C_QA + j + 1], in1=rinv[:, R_CQ % 2, :],
                       op0=ALU.mult, op1=ALU.mult), s('cq_ready') if j == 3 else None)
            dve.wait_ge(s('rinv_ready'), R_KV + 1)
            dve.wait_ge(tile_taken[1], TBASE['inc'] + 3)
            for j in range(2):
                st(stt(out=clat[:, j, :], in0=clat[:, j, :], scalar=small[:, C_KVA + j:C_KVA + j + 1], in1=rinv[:, R_KV % 2, :],
                       op0=ALU.mult, op1=ALU.mult), s('cq_ready') if j == 1 else None)
            dve.wait_ge(s('kr_raw'), 1)
            st(ts_(krg, krraw, small[0:32, C_KR:C_KR + 1], None, ALU.mult))
            st.sync()
            st(tt(krg, krg, rope[0:32, 2, :], ALU.mult))
            dve.wait_ge(s('kr_mm'), 2)
            st(tt(two(krt), bank2(4, 32), two(rope[0:32, 3, :]), ALU.mult))
            st.sync()
            st(tt(krrot, krg, krt, ALU.add), s('krot_ready'))
            dve.wait_ge(s('rinv_ready'), R_KEY + 1)
            dve.wait_ge(tile_taken[0], TBASE['outc'])
            dve.wait_ge(tile_taken[1], TBASE['outc'])

            def key_mask(h, b):
                col = ident[0:16, h:h + 1] if isinstance(h, int) else ident[0:16, bass.ds(h, 1)]
                st(ts_(invm[:, b, :], invr[:, 0:T], col, None, ALU.mult), s('invm_ready'))

            def query(h, pair, b):
                dve.wait_ge(s('qsq_ready'), h + 1)
                st(tt(qt1[0:QH, :], qraw[0:QH, :], cosg[0:QH, :], ALU.mult))
                dve.wait_ge(s('qrot_mm'), h + 1)
                st(tt(two(qt2[0:QH, :]), bank2(0, QH), two(rope[0:QH, 1, :]), ALU.mult))
                st.sync()
                st(tt(qt1[0:QH, :], qt1[0:QH, :], qt2[0:QH, :], ALU.add))
                st.sync()
                dve.wait_ge(s('rinv_ready'), h + (R_HEAD + 1))
                st(tt(qhd[0:QH, b, :], qt1[0:QH, :], rinv[0:QH, b, :], ALU.mult), s('qh_ready'))
                st.sync()
                st(dve.tensor_copy(qs[0:QH, h, :], qhd[0:QH, b, T:TOK]))
                dve.wait_ge(s('invb_mm'), h + 1)
                st(tt(khd[0:64, b, :], knope[64 * b:64 * b + 64, pair, 0:T], PS[0:64, 2, :], ALU.mult))
                st(tt(khd[64:96, b, :], krrot[:, 0:T], PS[0:32, 2, :], ALU.mult), s('k_ready'))

            def step(i, u, last=False):
                h, b = i * 4 + u, u % 2
                if not last:
                    key_mask(h + 1, 1 - b)
                dve.wait_ge(s('s_mm'), h + 1)
                for q in range(4):
                    blk = PS[:, 4 + q, q * 128:(q + 1) * 128]
                    st(tt(blk, blk, const('causal'), ALU.add))
                st.sync()
                for q in range(4):
                    st(dve.tensor_reduce(mx[:, q:q + 1], PS[:, 4 + q, 0:(q + 1) * 128], AX.X, ALU.max))
                st.sync()
                dve.wait_ge(s('p_ready'), h)
                st(ts_(nb, mx, -PSCALE, None, ALU.mult), s('nb_ready'))
                if not last:
                    query(h + 1, i * 2 + (u + 1) // 2, 1 - b)
                dve.wait_ge(s('o_mm'), h + 1)
                if b == 0:
                    dve.wait_ge(s('ott_mm'), i * 2 + u // 2)
                st(dve.reciprocal(rden, den))
                st.sync()
                st(tt(otm[:, :, b * VH:(b + 1) * VH], PS[:, 7, 0:4 * VH].rearrange("p (q v) -> p q v", v=VH), over(rden, VH), ALU.mult),
                   s('otm_ready'))
            key_mask(0, 0)
            query(0, 0, 0)
            per = [(own, 4 * (8 + 6)), (s('invm_ready'), 4), (s('nb_ready'), 4), (s('qh_ready'), 4),
                   (s('k_ready'), 4), (s('otm_ready'), 4)]
            for u in range(4):
                step(0, u)
            st.loop(1, MH // 4 - 1, lambda i: [step(i, u) for u in range(4)], per)
            for u in range(4):
                step(MH // 4 - 1, u, last=u == 3)

            st.sync()
            st(dve.memset(qkn[:, :, :, :], 0.0))
            st.sync()
            for p in range(2):
                src = qs[0:64, :, :].rearrange("p (m e) b -> p m e b", e=2)[:, :, p, :]
                st(ts_(qkn[64 * p:64 * p + 64, :, p, :], src, small[0:64, C_KN:C_KN + 1], None, ALU.mult))
            st(dve.tensor_copy(qr, qs[64:96]), s('gk_ready'))
            dve.wait_ge(s('sample_mm'), 2)
            st(tt(snew, PS[0:16, 4, 0:NS], invr[:, T:TOK], ALU.mult), s('snew_ready'))

            for b in range(NS):
                p, here = b % 2, slice(b, b + 1)
                m_, nb_, dn_, pn_, rd_ = (v[:, p:p + 1] for v in (m16, nb16, den16, pn16, rden16))
                dve.wait_ge(s('sc_mm'), b + 1)
                if b >= 2:
                    dve.wait_ge(s('spt_mm'), b - 1)
                st(tt(prob[:, p].rearrange("p (g s) -> p g s", g=NPG), PS[0:16, 2 * p:2 * p + 2, :].rearrange("p a (g s) -> p (a g) s", s=128),
                      pagebuf[b % 4][32:48, :, 512:640], ALU.mult), s('sc_taken'))
                st.sync()
                st(dve.tensor_reduce(m_, prob[:, p], AX.X, ALU.max))
                st.sync()
                st(tt(m_, m_, snew[:, here], ALU.max))
                st.sync()
                st(ts_(nb_, m_, -PSCALE, None, ALU.mult), s('smx_ready'))
                dve.wait_ge(s('sp_ready'), b + 1)
                if b >= 2:
                    dve.wait_ge(s('ctxn_ready'), b - 1)
                st(tt(dn_, dn_, pn_, ALU.add))
                st.sync()
                st(dve.reciprocal(rd_, dn_))
                st.sync()
                st(tt(pnn[:, here], pn_, rd_, ALU.mult), s('rden_ready'))
            st.sync()
            st(tt(pnd, over(ident[0:16, 0:16], NS), across(pnn, MH), ALU.mult), s('snew_ready'))
            dve.wait_ge(s('sample_mm'), 3)
            dve.wait_ge(s('ctx_ready'), NS)
            new = spt[:, :, :].rearrange("p a (h b) -> p a h b", b=NS)
            for k in range(2):
                st(tt(new[:, k], PS[:, 5, 0:MH * NS].rearrange("p (h b) -> p h b", b=NS), across(clat[:, k, T:TOK], MH), ALU.mult))
            st.sync()
            st(tt(ctxt[:, :, :, :], ctxt[:, :, :, :], new, ALU.add), s('snew_ready'))
            residual('outc')
            ffn(1, 3)


def _constants():
    r = np.arange(128)
    row, col = r[:, None], r[None, :]
    m = {'ident': row == col, 'triu': row <= col, 'ones': np.ones((128, 128)),
         'decaymask': np.where(col >= row, 0.0, NEG), 'causal': np.where(col <= row, 0.0, NEG)}
    for n, v in (('ones_d', D), ('ones_128', 128), ('ones_256', 256), ('ones_512', 512), ('ones_96', 96)):
        m[n] = np.full((128, 128), 1.0 / v)
    half = RD // 2
    for n, base in (('rot96', NOPE), ('rot32', 0)):
        z = np.zeros((128, 128))
        for e in range(half):
            z[base + half + e, base + e] = -1.0
            z[base + e, base + half + e] = 1.0
        m[n] = z
    z = np.zeros((128, 8, 16))
    for t in range(8):
        for p in range(128):
            z[p, t, 2 * t + p // 64] = 1.0 / QH
    m['headsel'] = z.reshape(128, 128)
    for l in range(LV + 1):
        b = 2 ** l
        m[f'inv{l}'] = (row // (2 * b) == col // (2 * b)) & ((col // b) % 2 == 1) & ((row // b) % 2 == 0)
    return np.stack([np.asarray(m[n], np.float32) for n in CONSTS], axis=1)


def _rope_tables():
    f32 = np.float32
    half = RD // 2
    freq = (f32(10000.0) ** (-np.arange(half, dtype=f32) / f32(half))).astype(f32)
    pos = np.concatenate([np.arange(T, dtype=f32), np.full(NS, NPG * 128, f32)])
    ang = (pos[:, None] * freq[None, :]).astype(f32)
    cos, sin = np.cos(ang).T.astype(f32), np.sin(ang).T.astype(f32)
    cos, sin = np.concatenate([cos, cos]), np.concatenate([sin, sin])
    t = np.zeros((128, 4, TOK), f32)
    t[0:NOPE, 0] = 1.0
    t[NOPE:QH, 0], t[NOPE:QH, 1] = cos, sin
    t[0:RD, 2], t[0:RD, 3] = cos, sin
    return t


def _cols(v, n):
    return np.ascontiguousarray(np.asarray(v).reshape(n, 128).T)


def _tiles(w, m=128):
    k, n = w.shape
    return np.ascontiguousarray(w.reshape(k // 128, 128, n // m, m).transpose(2, 1, 0, 3)).reshape(n // m, 128, -1)


def kernel(**inputs):
    import concourse.bacc as _bacc
    from concourse.bass_utils import run_bass_kernel_spmd as _run
    I = {k: np.asarray(v) for k, v in inputs.items()}
    f = {}
    x = np.concatenate([I['x_prompt'][0], I['x_sample'][:, 0]], axis=0)
    f['x'] = np.ascontiguousarray(x.T.reshape(KD, 128, TOK).transpose(1, 0, 2))
    w = I['w_in_a'][0]
    c = np.cumsum([0, 1536, 512, 4, 4, 512, 1024, 8])
    qkv, gz, ga, gb, sz, xbc, dt = (w[:, c[i]:c[i + 1]] for i in range(7))
    f['w_proj'] = _tiles(np.concatenate([qkv, xbc, gz, sz], axis=1))
    f['w_gate'] = np.ascontiguousarray(np.concatenate([ga, dt, gb], axis=1).reshape(KD, 128, NGATE).transpose(1, 0, 2))
    f['w_outa'], f['w_outc'] = _tiles(I['w_out_a'][0]), _tiles(I['w_out_c'][0])
    for l in range(2):
        gu = I['w_gate_up'][l].reshape(D, 2, KF, 128).transpose(0, 2, 1, 3).reshape(D, 2 * DFF)
        f[f'w_gu{l}'] = _tiles(gu)
        f[f'w_dn{l}'] = np.ascontiguousarray(I['w_down'][l].reshape(KF, 128, KD, 128).transpose(2, 1, 0, 3)).reshape(KD, 128, KF * 128)
    wc = I['w_in_c'][0]
    uk = I['w_uk'][0]
    f['w_inc'] = np.concatenate([_tiles(wc[:, 0:768]), uk.reshape(2, 128, 1024)], axis=0)
    f['w_kr'] = np.ascontiguousarray(wc[:, 768:800].reshape(KD, 128, RD).transpose(1, 0, 2))
    f['w_uq'] = _tiles(I['w_uq'][0], QH)
    f['w_uv'] = np.ascontiguousarray(I['w_uv'][0].reshape(2, 128, 1024).transpose(1, 0, 2))
    f['w_ukt'] = np.ascontiguousarray(uk.transpose(1, 2, 0).reshape(8, 128, 256).transpose(1, 0, 2))
    f['consts'] = _constants()
    f['rope'] = _rope_tables()
    sel = np.zeros((8, 8, 128), np.float32)
    for b in range(8):
        sel[b, b] = 1.0
    f['selb'] = sel
    f['gains'] = np.stack([_cols(v, KD) for v in (I['norm_mix_a'][0], I['norm_ffn'][0], I['norm_mix_c'][0], I['norm_ffn'][1])], axis=1)
    cw = np.concatenate([I['conv_gdn_w'][0], I['conv_ssm_w'][0]], axis=1)
    f['convw'] = np.ascontiguousarray(cw.reshape(4, NCONV, 128).transpose(2, 1, 0))
    f['convb'] = _cols(np.concatenate([np.zeros(1536, np.float32), I['conv_ssm_b'][0]]), NCONV)
    sm = np.zeros((128, NSMALL), np.float32)
    sm[:, C_GDN] = I['gdn_norm'][0]
    sm[:, C_D:C_D + 4] = _cols(np.repeat(I['ssm_D'][0], 64), 4)
    sm[:, C_SSM:C_SSM + 4] = _cols(I['ssm_norm'][0], 4)
    sm[:, C_QA:C_QA + 4] = _cols(I['q_a_norm'][0], 4)
    sm[:, C_KVA:C_KVA + 2] = _cols(I['kv_a_norm'][0], 2)
    sm[0:QH, C_QN] = I['q_norm'][0]
    sm[0:RD, C_KR] = I['k_norm'][0][NOPE:]
    sm[:, C_EPS] = EPS
    sm[:, C_KN] = np.tile(I['k_norm'][0][:NOPE], 2)
    f['small'] = sm
    gc = np.concatenate([I['gdn_dt_bias'][0], I['ssm_dt_bias'][0], np.zeros(GH, np.float32), I['gdn_A_log'][0], I['ssm_A_log'][0]])
    f['gatec'] = np.ascontiguousarray(np.broadcast_to(gc, (128, NGATE + NDEC)))
    pv = np.concatenate([I['state_gdn_conv'][0], I['state_ssm_conv'][0]], axis=2)
    f['prev'] = np.ascontiguousarray(pv.reshape(NS, 3, NCONV, 128).transpose(3, 2, 1, 0))
    f['s_gdn'] = np.ascontiguousarray(I['state_gdn'][0].transpose(2, 1, 0, 3))
    f['s_ssm'] = np.ascontiguousarray(I['state_ssm'][0].transpose(3, 0, 1, 2)).reshape(128, NS, 512)
    f['page_table'] = np.ascontiguousarray(I['page_table'].reshape(1, NS * NPG))
    cm = I['cache_mla'][0]
    pages = np.zeros((NPOOL, 128, PROW), np.float32)
    pages[:, :, 0:256] = cm[:, :, 0:256]
    pages[:, :, 256:512] = cm[:, :, 0:256].reshape(NPOOL, 128, 2, 128).transpose(0, 3, 2, 1).reshape(NPOOL, 128, 256)
    pages[:, 0:48, 512:640] = cm[:, :, 256:304].transpose(0, 2, 1)
    f['pages'] = pages

    nc = _bacc.Bacc("TRN2", target_bir_lowering=False, num_devices=1)
    arrays, A, O = {}, {}, {}
    for n, a in f.items():
        arrays[f"in_{n}"] = a
        A[n] = nc.dram_tensor(f"in_{n}", a.shape, mybir.dt.from_np(a.dtype), kind="ExternalInput").ap()
    outs = {'y': (128, KD, TOK), 'p_gdn': (128, 512), 'p_ssm': (128, 512), 'conv_p': (128, NCONV, 3), 'conv_s': (128, NCONV, 3, NS),
            's_gdn': (128, GH, NS, 128), 's_ssm': (128, NS, 512), 'rows_c': (128, 2, TOK), 'rows_k': (RD, TOK), 'rows_r': (16, TOK)}
    for n, shape in outs.items():
        O[n] = nc.dram_tensor(f"out_{n}", shape, F32, kind="ExternalOutput").ap()
    build(nc, A, O)
    r = _run(nc, [arrays], core_ids=[0]).results[0]
    g = {n: np.asarray(r[f"out_{n}"]) for n in outs}
    y = g['y'].transpose(1, 0, 2).reshape(D, TOK).T
    y_prompt, y_sample = y[None, :T], y[T:, None]
    p_gdn = g['p_gdn'].reshape(128, GH, 128).transpose(1, 0, 2)[None, None]
    s_gdn = g['s_gdn'].transpose(2, 1, 0, 3)[None]
    p_ssm = g['p_ssm'].reshape(128, SH, 64).transpose(1, 2, 0)[None, None]
    s_ssm = g['s_ssm'].reshape(128, NS, SH, 64).transpose(1, 2, 3, 0)[None]
    cp = g['conv_p'].transpose(2, 1, 0).reshape(3, NCONV * 128)
    cs = g['conv_s'].transpose(3, 2, 1, 0).reshape(NS, 3, NCONV * 128)
    rows = np.concatenate([g['rows_c'].transpose(1, 0, 2).reshape(256, TOK), g['rows_k'], g['rows_r']], axis=0).T
    out = (y_prompt, y_sample, p_gdn, cp[None, None, :, :1536], p_ssm, cp[None, None, :, 1536:], rows[None, None, :T],
           s_gdn, cs[None, :, :, :1536], s_ssm, cs[None, :, :, 1536:], rows[None, T:, None])
    return tuple(np.ascontiguousarray(o) for o in out)
```

```python
import numpy as np
import concourse.bass as bass
from concourse import mybir
from contextlib import ExitStack

F32, F32R = mybir.dt.float32, mybir.dt.float32r
ACT = mybir.ActivationFunctionType
ALU = mybir.AluOpType
AX = mybir.AxisListType

T, NS = 512, 8
TOK = T + NS
HALF = TOK // 2
D, DFF = 1024, 2816
KD, KF = D // 128, DFF // 128
EPS = 1e-6
GH, SH, SG = 4, 8, 2
NCH = T // 128
NDEC = GH + SH
NGATE = NDEC + GH
NCONV = 20
LV = 6
MH, NOPE, RD, QH, VH = 16, 64, 32, 96, 64
NPG, NPOOL = 8, 80
PROW = 256 + 3 * 128
PSCALE = QH ** -0.5
NEG = -1e30
SLOT = KD * 128

TQ, TK, TV, TX, TB, TC, TZ, TSZ = 0, 4, 8, 12, 16, 18, 20, 24

R_L2, R_MIX, R_CQ, R_KV, R_KEY, R_HEAD = 1, 9, 17, 18, 19, 20
R_NORM = (0, 15, 16, R_HEAD + MH)
STAGES = [('proj', 7, 28), ('outa', 2, 8), ('gu0', 11, 44), ('dn0', 6, 8), ('inc', 2, 14), ('uq', 4, 0),
          ('outc', 2, 8), ('gu1', 11, 44), ('dn1', 6, 8)]
TURNS = {n: g for n, g, _ in STAGES}
GBASE = {n: sum(g for _, g, _ in STAGES[:k]) for k, (n, _, _) in enumerate(STAGES)}
TBASE = {n: sum(t for _, _, t in STAGES[:k]) // 2 for k, (n, _, _) in enumerate(STAGES)}

UPDATES = [(0,), (1,), (2,), (3,), (4,), (5,), (6, 7), ()]
INV_BANKS = ((3, 4, 5), (6, 7, 2))
FBASE = {'proj': 0, 'gu0': 28, 'dn0': 72, 'gu1': 96, 'dn1': 140}
NBASE = {0: 0, 1: 8, 3: 16}
DOWN = [8, 8, 6]
LN_EXP = 'natural_log_exp_and_others'

CONSTS = ['ident', 'triu', 'decaymask', 'causal', 'ones', 'ones_d', 'ones_128', 'ones_256', 'ones_512',
          'ones_96', 'rot96', 'rot32', 'headsel'] + [f'inv{l}' for l in range(LV + 1)]
C_GDN, C_D, C_SSM, C_QA, C_KVA, C_QN, C_KR, C_KN, C_EPS, NSMALL = 0, 1, 5, 9, 13, 15, 16, 17, 18, 19
SMALLS = ['w_gate', 'gains', 'convw', 'convb', 'small', 'gatec', 'prev']


class Steps:

    def __init__(self, eng, own):
        self.eng, self.own, self.count, self.shift, self.last = eng, own, {}, {}, None

    def __call__(self, ins, sem=None):
        sem = sem or self.own
        ins.then_inc(sem, 1)
        self.count[sem.name] = self.count.get(sem.name, 0) + 1
        self.last = sem

    def sync(self):
        self.eng.wait_ge(self.last, self.shift.get(self.last.name, 0) + self.count[self.last.name])

    def loop(self, first, last, body, per):
        before = dict(self.count)
        with self.eng.Fori(first, last) as i:
            self.shift = {s.name: (i - first) * n for s, n in per}
            body(i)
        for s, n in per:
            made = self.count.get(s.name, 0) - before.get(s.name, 0)
            assert made == n, (s.name, made, n)
            self.count[s.name] = before.get(s.name, 0) + (last - first) * n
        looped = [s.name for s, _ in per]
        assert all(k in looped or v == before.get(k, 0) for k, v in self.count.items()), self.count
        self.shift = {}


def build(nc, A, O):
    ctx = ExitStack()
    with ctx:
        def sb(name, *shape):
            return ctx.enter_context(nc.sbuf_tensor(name, list(shape), F32))

        def sem(name):
            return ctx.enter_context(nc.semaphore(name))

        def by3(ap):
            return ap.rearrange("p (a t) -> p a t", t=TOK)

        PS = ctx.enter_context(nc.psum_tensor("PS", [128, 8, 512], F32))
        xres = sb("xres", 128, KD, TOK)
        WORK = 12480
        base = nc.sbuf_base
        arena = sb("arena", 128, (2 * KD + 28) * TOK + WORK)
        xn = by3(arena[:, 0:KD * TOK])
        mix = by3(arena[:, KD * TOK:2 * KD * TOK])
        hid = by3(arena[:, 2 * KD * TOK:(2 * KD + 28) * TOK])
        work = arena[:, (2 * KD + 28) * TOK:]

        def split(name, first, tiles):
            return nc.alloc_sbuf_tensor_at(name, [128, tiles, TOK], F32R, offset=base + 4 * first * TOK)

        xraw = hid[:, 20:28]
        xnh, xnl = split("xnh", 0, KD), split("xnl", KD, KD)
        hidh, hidl = split("hidh", 2 * KD, KF), split("hidl", 2 * KD + KF, KF)
        tail = (2 * KD + 2 * KF) * TOK
        spots = [nc.alloc_sbuf_tensor_at(f"wsplit{e}", [128, SLOT], F32R, offset=base + 4 * (tail + e * SLOT)) for e in range(3)]
        stream = nc.sbuf_base
        ring_words = sb("ring_words", 128, 5 * SLOT)
        wring = [nc.alloc_sbuf_tensor_at(f"wring{u}", [128, SLOT], F32, offset=stream + 4 * u * SLOT) for u in range(4)]
        spots.append(nc.alloc_sbuf_tensor_at("wsplit3", [128, SLOT], F32R, offset=stream + 16 * SLOT))
        whi, wlo = spots[0:2], spots[2:4]
        cst = sb("cst", 128, len(CONSTS), 128)
        rinv, sqsum, sq = sb("rinv", 128, 2, TOK), sb("sqsum", 128, TOK), sb("sq", 128, 2, TOK)
        gains, convw, convb = sb("gains", 128, 4, KD), sb("convw", 128, NCONV, 4), sb("convb", 128, NCONV)
        small, gatec = sb("small", 128, NSMALL), sb("gatec", 128, NGATE + NDEC)
        prev, convout_p, convout_s = sb("prev", 128, NCONV, 3, NS), sb("convout_p", 128, NCONV, 3), sb("convout_s", 128, NCONV, NS)
        wgate = sb("wgate", 128, KD, NGATE)
        graw, gabs, gexp, gone, grec, gln, gsp = (sb(n, 128, 5, NGATE) for n in
                                                  ("graw", "gabs", "gexp", "gone", "grec", "gln", "gsp"))
        la, nega = sb("la", 128, 5, NDEC), sb("nega", 128, NDEC)
        cumt, ecumt, bec = sb("cumt", 128, NCH, NDEC), sb("ecumt", 128, NCH, NDEC), sb("bec", 128, NCH, GH)
        beta, gdt = grec[:, :, NDEC:NGATE], gsp[:, :, GH:NDEC]
        ptab = ctx.enter_context(nc.sbuf_tensor("ptab", [1, NS * NPG], mybir.dt.int32))
        at = [0]

        def take(*shape, rows=128):
            n = int(np.prod(shape))
            v = work[0:rows, at[0]:at[0] + n]
            at[0] += n
            assert at[0] <= WORK, at[0]
            if len(shape) == 2:
                return v.rearrange("p (a b) -> p a b", b=shape[1])
            if len(shape) == 3:
                return v.rearrange("p (a b c) -> p a b c", b=shape[1], c=shape[2])
            return v

        def const(name):
            return cst[:, CONSTS.index(name), :]

        def two(ap):
            return ap.rearrange("p (a t) -> p a t", a=2)

        def bank2(b, rows=128):
            return PS[0:rows, b:b + 2, 0:HALF]

        def by(ap, n):
            return ap.rearrange("p (h x) -> p h x", h=n)

        def over(ap, n):
            return ap.unsqueeze(2).broadcast_to([ap.shape[0], ap.shape[1], n])

        def across(ap, n):
            return ap.unsqueeze(1).broadcast_to([ap.shape[0], n, ap.shape[1]])

        ident = const('ident')

        raw = take(2, 3 + TOK)
        cacc = take(2, TOK)
        at[0] = 0
        arg, dect = xn[:, 0:3, 0:512], xn[:, 3:6, 0:512]
        bm, lt = xn[:, 6, 0:512], xn[:, 7, 0:512]
        xdt, xde = sq[:, 0, 0:512], sq[:, 1, 0:512]
        ecum = take(3, 512)
        attnt, kbe, kdec, vb, xinv, xinvt, yinv, wt, vnew, qe = (take(512) for _ in range(10))
        mt = take(LV + 1, 512)
        scoret = take(2, 512)
        sgdn, hssd = work[:, WORK - 1024:WORK - 512], work[:, WORK - 512:]
        ce = (rinv[:, 0, 0:512], sqsum[:, 0:512])
        btm, kd, kdarg = rinv[:, 1, 0:256], take(NDEC), take(NDEC)
        at[0] = 0
        s0, h0 = take(GH, NS, 128), take(NS, 512)
        vals, valx, valb, ab = take(24), take(24, NS), take(24, NS), take(NDEC, NS)
        rhs2, vnt, qkp, vrow = take(GH * NS, 2), take(GH, NS), take(GH, NS), take(512)
        kb8, bcp, apx = take(GH, NS), take(SG, NS), take(4, 2, NS)
        xds, ysm, yt2, xrow, supd = take(4, NS), take(4, NS), take(4, NS), take(512), take(2, 512)
        sgate = nc.alloc_sbuf_tensor_at("sgate", [128, 2, TOK], F32, offset=base + 4 * ((2 * KD + 28) * TOK + WORK - 2 * TOK))
        at[0] = 0
        krrot, invr, cosg, qs = take(TOK, rows=32), take(TOK, rows=16), take(TOK), take(MH, NS)
        wkr, rotg, rotk = take(KD, RD), take(QH), take(RD, rows=32)
        vol = at[0]
        krraw, krg, krsq, krt = (work[0:32, vol + i * TOK:vol + (i + 1) * TOK] for i in range(4))
        qraw, qsq, qt1, qt2 = (take(TOK) for _ in range(4))
        qhd, khd, pm, ptsb, otm = take(2, TOK), take(2, T), take(4, 512), take(1280), take(4, 128)
        invm = take(2, T, rows=16)
        mx, nb, den, rden = (take(4) for _ in range(4))
        cqn, clat, knope, rope = hid[:, 0:4], hid[:, 4:6], hid[:, 6:14], hid[:, 14:18]
        hflat = hid[:, 18:28].rearrange("p a t -> p (a t)")
        wuv = hflat[:, 0:2048].rearrange("p (k n) -> p k n", k=2)
        wukt = hflat[:, 2048:4096].rearrange("p (h c) -> p h c", h=8)
        vtok = xn[:, :, :].rearrange("p a t -> p (a t)")[:, 0:4096].rearrange("p (a n) -> p a n", a=4)
        hs = [4096]

        def htake(a, b, rows=128):
            v = hflat[0:rows, hs[0]:hs[0] + a * b].rearrange("p (a b) -> p a b", b=b)
            hs[0] += a * b
            assert hs[0] <= 5200
            return v

        qkn = htake(8, 2 * NS).rearrange("p m (e b) -> p m e b", e=2)
        qa = hflat[:, hs[0]:hs[0] + 256].rearrange("p (k h b) -> p k h b", k=2, b=NS); hs[0] += 256
        ctxt = hflat[:, hs[0]:hs[0] + 256].rearrange("p (k h b) -> p k h b", k=2, b=NS); hs[0] += 256
        qr, snew, pnd, pnn = htake(MH, NS, rows=32), htake(1, NS, rows=16)[:, 0, :], htake(MH, NS, rows=16), htake(1, NS, rows=16)[:, 0, :]
        m16, nb16, den16, pn16, rden16 = (htake(1, 2, rows=16)[:, 0, :] for _ in range(5))
        pagebuf = [flat[:, 0:NPG * PROW].rearrange("p (g r) -> p g r", g=NPG)
                   for flat in (hid[:, 6:18].rearrange("p a t -> p (a t)"), ring_words, work[:, vol:], work[:, vol + NPG * PROW:])]
        values = xn.rearrange("p a t -> p (a t)")
        prob = values[0:16, 0:2048].rearrange("p (a n) -> p a n", a=2)
        spt = values[:, 2048:2304].rearrange("p (a n) -> p a n", a=2)
        ctxn = values[0:16, 2304:2816].rearrange("p (a n) -> p a n", a=2)
        qseq = values[:, 2816:2912].rearrange("p (a k h) -> p a k h", a=2, k=3)

        x_loaded, c_loaded, g_loaded = sem("x_loaded"), sem("c_loaded"), sem("g_loaded")
        w_loaded = [sem(f"w_loaded{u}") for u in range(4)]
        gemm_ready = [sem(f"gemm_ready{p}") for p in range(2)]
        tile_taken = [sem(f"tile_taken{p}") for p in range(2)]
        pages_loaded = [sem(f"pages_loaded{p}") for p in range(4)]

        names = """sq_ready sq_added sq_zeroed ssq_mm xn_ready gates_mm gprep_ready gact_ready la_ready 
            cumt_ready ecumt_ready raw_ready zeroed conv_done silu_done l2sq_ready l2_mm l2_done
            cumB_mm arg_ready ecum_ready dect_ready kd_ready betaB_mm bm_ready kk_mm qk_mm ktm_mm vtm_mm
            lt_ready attn_ready kvs_ready mt_ready xinit_mm xinit_ready y_mm y_ready p_mm pt_mm x_ready vnew_mm
            w_mm w_ready qe_ready vnew_ready ot_mm ot_taken kv_mm s_ready bc_mm xtm_mm btm_mm score_ready
            xdt_ready btm_ready ce_ready yt_mm yt_taken hup_mm h_ready rec_stored st_loaded
            sprep_ready spread_mm valb_ready spread_ready rhs2_ready sv_mm vnt_ready qks_mm row_mm row_ready
            sel_mm sel_taken y0_mm xds_ready hsel_mm hsel_taken s_decayed osq_ready osq_mm
            mix_ready dve_own kr_mm kr_raw krsq_ready cq_sq cq_mm cq_ready rot_ready krot_ready
            kn_sq kn_mm h0_loaded ln_ready rinv_ready v_mm v_ready q_mm qsq_ready qss_mm qrot_mm qh_ready
            invm_ready invb_mm k_ready s_mm nb_ready p_ready pt2_mm pt2_taken o_mm otm_ready ott_mm omix_ready
            gk_ready sample_mm qa_ready snew_ready sc_mm smx_ready 
            sp_ready ctx_mm ctx_ready so_ready big_stored out_stored
            w_hi w_split part_done xn_raw xn_hi hid_hi hid_ready sc_taken spt_mm
            spt_taken ctt_mm rden_ready ctxn_ready qseq_ready""".split()
        sems = {n: sem(n) for n in names}

        def s(name):
            return sems[name]

        def slot_freed(stage, i, u):
            tb = TBASE[stage]
            if stage in FBASE:
                return s('w_split'), i * 4 + (FBASE[stage] + u + 1)
            if stage == 'uq':
                return s('q_mm'), i * 4 + (u + 1)
            if stage == 'inc':
                return gemm_ready[u % 2], tb + (u // 2 + 1 if i == 0 else 3 if u < 2 else 7)
            return gemm_ready[u % 2], tb + i * 2 + (u // 2 + 1)

        block = ctx.enter_context(nc.Block())

        @block.sync
        def _(sp_):
            for k in range(2):
                sp_.dma_start(xres[:, 4 * k:4 * k + 4], A['x'][:, 4 * k:4 * k + 4]).then_inc(x_loaded, 16)
            sp_.dma_start(ptab[:, :], A['page_table']).then_inc(x_loaded, 16)

            def load(stage, i, u):
                if stage in ('dn0', 'dn1'):
                    tile, part = divmod(i * 4 + u, 3)
                    first, n = sum(DOWN[:part]) * 128, DOWN[part] * 128
                    src = A['w_' + stage][tile, :, first:first + n]
                else:
                    n, src = 4 * QH if stage == 'uq' else SLOT, A['w_' + stage][i * 4 + u]
                sp_.dma_start(wring[u][:, 0:n], src).then_inc(w_loaded[u], 16)

            def pages():
                sp_.wait_ge(x_loaded, 48)

                for b in range(NS):
                    if b >= 4:
                        sp_.wait_ge(s('ctx_mm'), b - 3)
                    elif b == 0:
                        sp_.wait_ge(s('qh_ready'), MH)
                        sp_.wait_ge(s('k_ready'), MH)
                    elif b == 1:
                        sp_.wait_ge(s('q_mm'), MH)
                    else:
                        sp_.wait_ge(s('omix_ready'), MH // 2)
                    for g in range(NPG):
                        page = sp_.value_load(ptab[0:1, b * NPG + g:b * NPG + g + 1], min_val=0, max_val=NPOOL - 1)
                        sp_.dma_start(pagebuf[b % 4][:, g], A['pages'][bass.ds(page, 1)].rearrange("a p r -> p (a r)"))\
                            .then_inc(pages_loaded[b % 4], 16)

            before = None
            for stage, turns, _ in STAGES:
                for u in range(4):
                    if before == 'uq':
                        sp_.wait_ge(s('ctx_mm'), 6)
                    elif before:
                        sp_.wait_ge(*slot_freed(before, TURNS[before] - 1, u))
                    load(stage, 0, u)
                if stage in ('inc', 'dn0', 'dn1'):
                    for i in range(1, turns):
                        for u in range(4):
                            sp_.wait_ge(*slot_freed(stage, i - 1, u))
                            load(stage, i, u)
                else:
                    with sp_.Fori(1, turns) as i:
                        for u in range(4):
                            sp_.wait_ge(*slot_freed(stage, i - 1, u))
                            load(stage, i, u)
                before = stage
                if stage == 'uq':
                    pages()
            for k in range(0, KD, 2):
                for p in range(2):
                    sp_.wait_ge(tile_taken[p], TBASE['dn1'] + k // 2 + 1)
                sp_.dma_start(O['y'][:, k:k + 2], xres[:, k:k + 2, :]).then_inc(s('big_stored'), 16)
            sp_.wait_ge(s('big_stored'), 32 + 16 * (KD // 2))

        @block.gpsimd
        def _(pool):
            pool.dma_start(cst[:, :, :], A['consts']).then_inc(c_loaded, 16)
            for dst, src in zip((wgate, gains, convw, convb, small, gatec, prev), SMALLS):
                pool.dma_start(dst[:], A[src]).then_inc(g_loaded, 16)

            def sum_squares(n):
                pool.wait_ge(s('ssq_mm'), n)
                pool.memset(sqsum[:, :], 0.0).then_inc(s('sq_zeroed'), 1)
                pool.wait_ge(s('sq_zeroed'), n)
                for k in range(KD - 1):
                    pool.wait_ge(s('sq_ready'), KD * n + k + 1)
                    pool.wait_ge(s('sq_added'), (KD - 1) * n + k)
                    pool.tensor_tensor(sqsum[:, :], sqsum[:, :], sq[:, k % 2, :], ALU.add).then_inc(s('sq_added'), 1)

            pool.memset(raw[:, 0, 0:3], 0.0)
            pool.memset(raw[:, 1, 0:3], 0.0).then_inc(s('zeroed'), 1)
            pool.wait_ge(s('silu_done'), NCONV)
            pool.memset(sgdn, 0.0)
            pool.memset(hssd, 0.0).then_inc(s('zeroed'), 1)
            for c in range(NCH):
                pool.wait_ge(s('lt_ready'), c + 1)
                if c:
                    pool.wait_ge(s('x_ready'), 2 * LV * c)
                for l in range(LV + 1):
                    pool.tensor_tensor(by(mt[:, l], GH), by(lt, GH), across(const(f'inv{l}'), GH), ALU.mult)\
                        .then_inc(s('mt_ready'), 1)
            pool.wait_ge(s('s_ready'), NCH)
            pool.wait_ge(s('h_ready'), NCH)
            pool.wait_ge(s('ot_taken'), NCH)
            pool.wait_ge(s('yt_taken'), NCH)
            pool.dma_start(s0, A['s_gdn']).then_inc(s('st_loaded'), 16)
            pool.dma_start(h0, A['s_ssm']).then_inc(s('h0_loaded'), 16)
            pool.dma_start(O['p_gdn'], sgdn).then_inc(s('rec_stored'), 16)
            pool.dma_start(O['p_ssm'], hssd).then_inc(s('rec_stored'), 16)
            pool.dma_start(O['conv_p'], convout_p[:, :, :]).then_inc(s('out_stored'), 16)
            pool.wait_ge(s('spread_ready'), 1)
            pool.wait_ge(s('sv_mm'), 1)
            pool.wait_ge(s('y0_mm'), 1)
            for h in range(GH):
                pool.tensor_tensor(s0[:, h], s0[:, h], over(ab[:, h], 128), ALU.mult).then_inc(s('s_decayed'), 1)
            for b in range(NS):
                pool.tensor_tensor(by(h0[:, b], SH), by(h0[:, b], SH), over(ab[:, GH:, b], 64), ALU.mult)\
                    .then_inc(s('s_decayed'), 1)
            pool.dma_start(O['conv_s'][:, :, 2], convout_s[:, :, :]).then_inc(s('out_stored'), 16)
            pool.dma_start(O['conv_s'][:, :, 0:2], prev[:, :, 1:3]).then_inc(s('out_stored'), 16)
            sum_squares(1)
            sum_squares(2)
            pool.wait_ge(s('sq_ready'), 3 * KD)
            pool.wait_ge(s('out_stored'), 48)
            pool.wait_ge(s('big_stored'), 32)
            for dst, src in ((wkr, 'w_kr'), (rope, 'rope'), (wuv, 'w_uv'), (wukt, 'w_ukt')):
                pool.dma_start(dst, A[src]).then_inc(g_loaded, 16)
            pool.wait_ge(s('cq_ready'), 2)
            pool.dma_start(O['rows_c'], clat).then_inc(s('out_stored'), 16)
            pool.wait_ge(s('krot_ready'), 1)
            pool.dma_start(O['rows_k'], krrot).then_inc(s('out_stored'), 16)
            pool.wait_ge(s('rinv_ready'), R_KEY + 1)
            pool.dma_start(O['rows_r'], invr).then_inc(s('out_stored'), 16)
            pool.wait_ge(s('qa_ready'), 1)
            pool.wait_ge(s('gk_ready'), 1)
            pool.wait_ge(s('omix_ready'), MH // 2)

            def queries(i, p, first=False):
                b = i * 2 + p
                at_ = slice(b, b + 1) if isinstance(b, int) else bass.ds(b, 1)
                if not first:
                    pool.wait_ge(s('sc_mm'), b - 1)
                pool.tensor_copy(qseq[:, p, 0:2, :].unsqueeze(3), qa[:, :, :, at_])
                pool.tensor_copy(qseq[0:32, p, 2, :].unsqueeze(2), qr[:, :, at_]).then_inc(s('qseq_ready'), 1)
            for p in range(2):
                queries(0, p, first=True)
            with pool.Fori(1, NS // 2) as i:
                for p in range(2):
                    queries(i, p)
            sum_squares(3)
            pool.wait_ge(s('out_stored'), 96)

        @block.tensor
        def _(pe):
            def mm(out, lhsT, rhs, start=True, stop=True):
                return pe.matmul(out, lhsT, rhs, start=start, stop=stop)

            def both(b, lhsT, rhs, start=True, stop=True):
                for h in range(2):
                    last = mm(PS[0:lhsT.shape[1], b + h, 0:HALF], lhsT, rhs[:, h * HALF:(h + 1) * HALF], start, stop)
                return last

            def split_gemm(stage, high, low, begin=0, end=None, norm=None, after=None):
                def piece(p, u, chunks, k0, last, done, norm=None):
                    for k in range(chunks):
                        if norm is not None:
                            pe.wait_ge(s('xn_ready'), KD * norm + k + 1)
                        wh, wl = (w[u % 2][:, k * 128:(k + 1) * 128] for w in (whi, wlo))
                        both(2 * p, wh, high[:, k0 + k, :], k0 + k == 0, False)
                        both(2 * p, wh, low[:, k0 + k, :], False, False)
                        ins = both(2 * p, wl, high[:, k0 + k, :], False, last and k == chunks - 1)
                    ins.then_inc(done, 1)

                def up(i, norm=None):
                    for u in range(4):
                        p = u % 2
                        if stage != 'proj' or not isinstance(i, int) or i * 2 + u // 2 > 0:
                            pe.wait_ge(tile_taken[p], i * 2 + (TBASE[stage] + u // 2))
                        pe.wait_ge(s('w_split'), i * 4 + (FBASE[stage] + u + 1))
                        piece(p, u, KD, 0, True, gemm_ready[p], norm if u == 0 else None)
                        if after:
                            after(i, u)

                def down(i):
                    for e in range(12):
                        tile, part = divmod(e, 3)
                        p = tile % 2
                        if part == 0:
                            pe.wait_ge(tile_taken[p], i * 2 + (TBASE[stage] + tile // 2))
                        pe.wait_ge(s('w_split'), i * 12 + (FBASE[stage] + e + 1))
                        if e == 2:
                            pe.wait_ge(s('hid_ready'), KF if stage == 'dn0' else 2 * KF)
                        piece(p, e, DOWN[part], sum(DOWN[:part]), part == 2, gemm_ready[p] if part == 2 else s('part_done'))
                if norm is not None:
                    up(0, norm)
                    begin = 1
                end = end or (2 if stage in ('dn0', 'dn1') else TURNS[stage])
                if stage == 'proj' and end == begin + 1:
                    up(begin)
                elif end > begin:
                    with pe.Fori(begin, end) as i:
                        down(i) if stage in ('dn0', 'dn1') else up(i)

            def gemm_turn(stage, rhs, i, after=None, ready=None):
                for u in range(4):
                    p = u % 2
                    pe.wait_ge(w_loaded[u], i * 16 + 16 * (GBASE[stage] + 1))
                    pe.wait_ge(tile_taken[p], i * 2 + (TBASE[stage] + u // 2))
                    for k in range(KD):
                        if ready and u == 0:
                            pe.wait_ge(ready, k + 1)
                        ins = both(2 * p, wring[u][:, k * 128:(k + 1) * 128], rhs(k), k == 0, k == KD - 1)
                    ins.then_inc(gemm_ready[p], 1)
                    if after:
                        after(i * 4 + u)

            def norm_sum(n):
                pe.wait_ge(s('sq_added'), (KD - 1) * (n + 1))
                both(4, const('ones_d'), sqsum, True, False)
                pe.wait_ge(s('sq_ready'), KD * (n + 1))
                both(4, const('ones_d'), sq[:, 1, :], False, True).then_inc(s('ssq_mm'), 1)

            pe.wait_ge(c_loaded, 16)
            norm_sum(0)
            split_gemm('proj', xnh, xnl, 0, 1, norm=0)
            pe.wait_ge(g_loaded, 16 * len(SMALLS))
            for t in range(5):
                for k in range(KD):
                    toks = slice(t * 128, min((t + 1) * 128, TOK))
                    ins = mm(PS[0:toks.stop - toks.start, 6, t * NGATE:(t + 1) * NGATE], xraw[:, k, toks], wgate[:, k, :],
                             k == 0, k == KD - 1)
            ins.then_inc(s('gates_mm'), 1)
            split_gemm('proj', xnh, xnl, 1, 5)
            pe.wait_ge(s('la_ready'), 1)
            for c in range(NCH):
                ins = mm(PS[:, 7, c * NDEC:(c + 1) * NDEC], const('triu'), la[:, c, :])
            ins.then_inc(s('gates_mm'), 1)
            def length(j):
                pe.wait_ge(s('l2sq_ready'), j + 1)
                if j >= 2:
                    pe.wait_ge(s('ln_ready'), R_L2 + j - 1)
                if j == 1:
                    pe.wait_ge(s('cumt_ready'), 1)
                both(4 + 2 * (j % 2), const('ones'), sq[:, j % 2, :]).then_inc(s('l2_mm'), 1)

            def lengths(i, u):
                z = (i - 5) * 4 + u
                if 1 <= z <= 4:
                    length(2 * z - 2)
                    length(2 * z - 1)
            for i in (5, 6):
                split_gemm('proj', xnh, xnl, i, i + 1, after=lengths)

            pe.wait_ge(s('cumt_ready'), 1)
            pe.wait_ge(s('l2_done'), 8)
            pe.wait_ge(s('silu_done'), NCONV)
            for p in range(2):
                pe.wait_ge(tile_taken[p], 14)
            pe.wait_ge(s('ln_ready'), R_L2 + 8)
            for c in range(NCH):
                ts = slice(c * 128, (c + 1) * 128)
                if c:
                    pe.wait_ge(s('yt_taken'), c)
                    pe.wait_ge(s('h_ready'), c)
                    pe.wait_ge(s('ot_taken'), c)
                for h in range(NDEC):
                    ins = mm(PS[:, h // 4, (h % 4) * 128:(h % 4 + 1) * 128],
                             la[:, c, h:h + 1].broadcast_to([128, 128]), const('triu'))
                ins.then_inc(s('cumB_mm'), 1)
                if c:
                    pe.wait_ge(s('w_ready'), c)
                for h in range(GH):
                    ins = mm(PS[:, 3, h * 128:(h + 1) * 128], beta[:, c, h:h + 1].broadcast_to([128, 128]), ident)
                ins.then_inc(s('betaB_mm'), 1)
                if c:
                    pe.wait_ge(s('x_ready'), 2 * LV * c)
                for h in range(GH):
                    ins = mm(PS[:, 4, h * 128:(h + 1) * 128], hid[:, TK + h, ts], hid[:, TK + h, ts])
                ins.then_inc(s('kk_mm'), 1)
                for h in range(GH):
                    ins = mm(PS[:, 5, h * 128:(h + 1) * 128], hid[:, TK + h, ts], hid[:, TQ + h, ts])
                ins.then_inc(s('qk_mm'), 1)
                if c:
                    pe.wait_ge(s('vnew_ready'), c)
                for h in range(GH):
                    ins = pe.transpose(PS[:, 6, h * 128:(h + 1) * 128], hid[:, TK + h, ts], ident)
                ins.then_inc(s('ktm_mm'), 1)
                if c:
                    pe.wait_ge(s('s_ready'), c)
                for h in range(GH):
                    ins = pe.transpose(PS[:, 7, h * 128:(h + 1) * 128], hid[:, TV + h, ts], ident)
                ins.then_inc(s('vtm_mm'), 1)
                pe.wait_ge(s('ecum_ready'), 2 * c + 2)
                pe.wait_ge(s('arg_ready'), 2 * c + 2)
                for g in range(SG):
                    ins = mm(PS[:, 0, g * 128:(g + 1) * 128], hid[:, TB + g, ts], hid[:, TC + g, ts])
                ins.then_inc(s('bc_mm'), 1)
                for m in range(4):
                    ins = pe.transpose(PS[:, 1, m * 128:(m + 1) * 128], hid[:, TX + m, ts], ident)
                ins.then_inc(s('xtm_mm'), 1)
                for g in range(SG):
                    ins = pe.transpose(PS[:, 2, g * 128:(g + 1) * 128], hid[:, TB + g, ts], ident)
                ins.then_inc(s('btm_mm'), 1)
                pe.wait_ge(s('mt_ready'), (LV + 1) * c + 1)
                pe.wait_ge(s('bm_ready'), c + 1)
                for h in range(GH):
                    ins = mm(PS[:, 3, h * 128:(h + 1) * 128], mt[:, 0, h * 128:(h + 1) * 128], ident)
                ins.then_inc(s('xinit_mm'), 1)
                pe.wait_ge(s('xinit_ready'), c + 1)
                for l in range(LV):
                    pe.wait_ge(s('mt_ready'), (LV + 1) * c + l + 2)
                    for half, (by_, bp, bpt) in enumerate(INV_BANKS):
                        n = 2 * (LV * c + l) + half
                        if l:
                            pe.wait_ge(s('x_ready'), n - 1)
                        elif half:
                            pe.wait_ge(s('kvs_ready'), c + 1)
                            pe.wait_ge(s('btm_ready'), c + 1)
                        for h in (2 * half, 2 * half + 1):
                            hs_ = slice(h * 128, (h + 1) * 128)
                            ins = mm(PS[:, by_, hs_], mt[:, l + 1, hs_], xinv[:, hs_])
                        ins.then_inc(s('y_mm'), 1)
                    if l == 0:
                        pe.wait_ge(s('lt_ready'), c + 1)
                        pe.wait_ge(s('attn_ready'), c + 1)
                    for half, (by_, bp, bpt) in enumerate(INV_BANKS):
                        pe.wait_ge(s('y_ready'), 2 * (LV * c + l) + half + 1)
                        if l < LV - 1:
                            for h in (2 * half, 2 * half + 1):
                                hs_ = slice(h * 128, (h + 1) * 128)
                                ins = mm(PS[:, bp, hs_], xinvt[:, hs_], yinv[:, hs_])
                            ins.then_inc(s('p_mm'), 1)
                        for h in (2 * half, 2 * half + 1):
                            hs_ = slice(h * 128, (h + 1) * 128)
                            ins = mm(PS[:, bpt, hs_], yinv[:, hs_], xinvt[:, hs_])
                        ins.then_inc(s('pt_mm'), 1)
                    if l == 1:
                        pe.wait_ge(s('score_ready'), c + 1)
                        pe.wait_ge(s('xdt_ready'), c + 1)
                        pe.wait_ge(s('ce_ready'), c + 1)
                        if c == 0:
                            pe.wait_ge(s('zeroed'), 2)
                        for h in range(SH):
                            o = PS[64 * (h % 2):64 * (h % 2) + 64, 0, (h // 2) * 128:(h // 2 + 1) * 128]
                            gs = slice((h % 4) * 128, (h % 4 + 1) * 128)
                            mm(o, xdt[:, h * 64:(h + 1) * 64], scoret[:, h // 4, gs], True, False)
                            ins = mm(o, hssd[:, h * 64:(h + 1) * 64], ce[h // 4][:, gs], False, True)
                        ins.then_inc(s('yt_mm'), 1)
                    if l == 2:
                        pe.wait_ge(s('btm_ready'), c + 1)
                        for g in range(SG):
                            ins = mm(PS[:, 1, g * 256:(g + 1) * 256], btm[:, g * 128:(g + 1) * 128],
                                     xde[:, g * 256:(g + 1) * 256])
                        ins.then_inc(s('hup_mm'), 1)
                pe.wait_ge(s('x_ready'), 2 * LV * (c + 1))
                pe.wait_ge(s('kvs_ready'), c + 1)
                for h in range(GH):
                    hs_ = slice(h * 128, (h + 1) * 128)
                    ins = mm(PS[:, 3, hs_], kbe[:, hs_], xinvt[:, hs_])
                ins.then_inc(s('w_mm'), 1)
                pe.wait_ge(s('w_ready'), c + 1)
                for h in range(GH):
                    hs_ = slice(h * 128, (h + 1) * 128)
                    mm(PS[:, 6, hs_], xinvt[:, hs_], vb[:, hs_], True, False)
                    ins = mm(PS[:, 6, hs_], wt[:, hs_], sgdn[:, hs_], False, True)
                ins.then_inc(s('vnew_mm'), 1)
                pe.wait_ge(s('vnew_ready'), c + 1)
                pe.wait_ge(s('qe_ready'), c + 1)
                pe.wait_ge(s('attn_ready'), c + 1)
                for h in range(GH):
                    hs_ = slice(h * 128, (h + 1) * 128)
                    mm(PS[:, 2, hs_], sgdn[:, hs_], qe[:, hs_], True, False)
                    ins = mm(PS[:, 2, hs_], vnew[:, hs_], attnt[:, hs_], False, True)
                ins.then_inc(s('ot_mm'), 1)
                for h in range(GH):
                    hs_ = slice(h * 128, (h + 1) * 128)
                    ins = mm(PS[:, 7, hs_], kdec[:, hs_], vnew[:, hs_])
                ins.then_inc(s('kv_mm'), 1)

            pe.wait_ge(s('sprep_ready'), 1)
            pe.wait_ge(s('yt_taken'), NCH)
            mm(PS[:, 0, 0:192], const('ones')[0:8, :], valx[0:8].rearrange("p a b -> p (a b)")).then_inc(s('spread_mm'), 1)
            pe.wait_ge(s('x_ready'), 2 * LV * NCH)
            for m in range(4):
                for e in range(2):
                    lhsT = supd[0:8, e, m * 128:(m + 1) * 128]
                    ins = mm(PS[:, 4, (m * 2 + e) * NS:(m * 2 + e + 1) * NS], lhsT, ident[0:8, 0:8])
            ins.then_inc(s('spread_mm'), 1)
            pe.wait_ge(s('sprep_ready'), 2)
            pe.wait_ge(s('ot_taken'), NCH)
            mm(PS[:, 2, 0:GH * NS], const('ones'), qkp.rearrange("p a b -> p (a b)")).then_inc(s('qks_mm'), 1)
            pe.wait_ge(s('sprep_ready'), 3)
            mm(PS[:, 5, 0:SG * NS], const('ones'), bcp.rearrange("p a b -> p (a b)")).then_inc(s('qks_mm'), 1)
            pe.wait_ge(s('st_loaded'), 16)
            pe.wait_ge(s('rhs2_ready'), 1)
            pe.wait_ge(s('h_ready'), NCH)
            for h in range(GH):
                for b in range(NS):
                    e = h * NS + b
                    ins = mm(PS[:, 1, 2 * e:2 * e + 2], s0[:, h, b, :], rhs2[:, e, :])
            ins.then_inc(s('sv_mm'), 1)
            pe.wait_ge(s('vnew_ready'), NCH)
            pe.wait_ge(s('h0_loaded'), 16)
            for b in range(NS):
                for m in range(4):
                    ins = mm(PS[:, 6, m * NS + b:m * NS + b + 1], h0[:, b, m * 128:(m + 1) * 128],
                             hid[:, TC + m // 2, T + b:T + b + 1])
            ins.then_inc(s('y0_mm'), 1)
            pe.wait_ge(s('vnt_ready'), 1)
            for h in range(GH):
                ins = pe.transpose(PS[0:8, 3, h * 128:(h + 1) * 128], vnt[:, h, :], ident)
            ins.then_inc(s('row_mm'), 1)
            pe.wait_ge(s('xds_ready'), 1)
            pe.wait_ge(s('s_ready'), NCH)
            for m in range(4):
                ins = pe.transpose(PS[0:8, 7, m * 128:(m + 1) * 128], xds[:, m, :], ident)
            ins.then_inc(s('row_mm'), 1)
            for j in range(8):
                e = j if j < 4 else 4 + (j - 4) // 2
                pe.wait_ge(s('osq_ready'), j + 1)
                if e >= 2 and (j < 4 or j % 2 == 0):
                    pe.wait_ge(s('ln_ready'), R_MIX + e - 1)
                both(4 + 2 * (e % 2), const('ones_128' if j < 4 else 'ones_256'), sq[:, j % 2, :],
                     j < 4 or j % 2 == 0, j < 4 or j % 2 == 1).then_inc(s('osq_mm'), 1)

            def spread_rows(k):
                for b in UPDATES[k]:
                    if b == 0:
                        pe.wait_ge(s('ln_ready'), R_MIX + 6)
                        pe.wait_ge(s('row_ready'), 2)
                    pe.wait_ge(s('sel_taken'), b)
                    mm(PS[:, 6, :], ident[0:8, b:b + 1].broadcast_to([8, 128]), vrow[0:8, :]).then_inc(s('sel_mm'), 1)
                    pe.wait_ge(s('hsel_taken'), b)
                    mm(PS[:, 7, :], ident[0:8, b:b + 1].broadcast_to([8, 128]), xrow[0:8, :]).then_inc(s('hsel_mm'), 1)
            for i in range(2):
                gemm_turn('outa', lambda k: mix[:, k, :], i, spread_rows, ready=s('mix_ready') if i == 0 else None)
            norm_sum(1)
            split_gemm('gu0', xnh, xnl, norm=1)
            pe.wait_ge(s('hid_ready'), sum(DOWN[:2]))
            split_gemm('dn0', hidh, hidl)
            norm_sum(2)

            tb = TBASE['inc']

            def mean_square(j):
                pe.wait_ge(s('cq_sq'), j + 1)
                if j == 4:
                    pe.wait_ge(tile_taken[0], tb + 3)
                both(6 if j < 4 else 0, const('ones_512' if j < 4 else 'ones_256'), sq[:, j % 2, :],
                     j in (0, 4), j in (3, 5)).then_inc(s('cq_mm'), 1)
            for j in range(6):
                pe.wait_ge(w_loaded[j % 4], 16 * (GBASE['inc'] + j // 4 + 1))
                pe.wait_ge(tile_taken[j % 2], tb + j // 2)
                for k in range(KD):
                    if j == 0:
                        pe.wait_ge(s('xn_ready'), KD * 2 + k + 1)
                    ins = both(2 * (j % 2), wring[j % 4][:, k * 128:(k + 1) * 128], xn[:, k, :], k == 0, k == KD - 1)
                ins.then_inc(gemm_ready[j % 2], 1)
                if 1 <= j <= 4:
                    mean_square(j - 1)
            pe.wait_ge(g_loaded, 16 * (len(SMALLS) + 4))
            for k in range(KD):
                ins = both(4, wkr[:, k, :], xn[:, k, :], k == 0, k == KD - 1)
            ins.then_inc(s('kr_mm'), 1)
            mean_square(4)
            mean_square(5)
            pe.wait_ge(s('kr_raw'), 1)
            pe.wait_ge(s('rot_ready'), 1)
            both(4, rotk, krraw).then_inc(s('kr_mm'), 1)
            pe.wait_ge(s('cq_ready'), 2)
            for m in range(8):
                p = m % 2
                if m < 2:
                    pe.wait_ge(w_loaded[2 + m], 16 * (GBASE['inc'] + 2))
                    pe.wait_ge(w_loaded[3], 16 * (GBASE['inc'] + 2))
                pe.wait_ge(tile_taken[p], tb + 3 + m // 2)
                for k in range(2):
                    ins = both(2 * p, wring[2 + k][:, m * 128:(m + 1) * 128], clat[:, k, :], k == 0, k == 1)
                ins.then_inc(gemm_ready[p], 1)
                if m:
                    pe.wait_ge(s('kn_sq'), m)
                    both(6, const('headsel')[:, (m - 1) * 16:m * 16], sq[:, (m - 1) % 2, :], m == 1, False).then_inc(s('kn_mm'), 1)
            pe.wait_ge(s('kn_sq'), 8)
            both(6, const('headsel')[:, 112:128], sq[:, 1, :], False, False).then_inc(s('kn_mm'), 1)
            pe.wait_ge(s('krsq_ready'), 1)
            both(6, const('ones_96')[0:32, 0:16], krsq, False, True).then_inc(s('kn_mm'), 1)
            pe.wait_ge(s('krot_ready'), 1)
            for n in range(8):
                if n >= 2:
                    pe.wait_ge(s('v_ready'), n - 1)
                for k in range(2):
                    ins = mm(PS[:, 4 + n % 2, :], clat[:, k, (n // 2) * 128:(n // 2 + 1) * 128],
                             wuv[:, k, (n % 2) * 512:(n % 2 + 1) * 512], k == 0, k == 1)
                ins.then_inc(s('v_mm'), 1)

            def key_scale(n, b):
                pe.wait_ge(s('ln_ready'), n + (R_HEAD + 1))
                pe.wait_ge(s('invm_ready'), n + 1)
                mm(PS[0:QH, 2, :], const('ones')[0:16, 0:QH], invm[:, b, :]).then_inc(s('invb_mm'), 1)

            def pair_out(h):
                pe.wait_ge(s('otm_ready'), h)
                for q in range(4):
                    ins = pe.transpose(PS[:, 3, q * 128:(q + 1) * 128], otm[:, q, :], ident)
                ins.then_inc(s('ott_mm'), 1)

            def step(i, u, first=False, last=False):
                h = i * 4 + u
                b = u % 2
                pe.wait_ge(s('qh_ready'), h + 1)
                pe.wait_ge(s('k_ready'), h + 1)
                pe.wait_ge(s('pt2_taken'), h)
                for q in (3, 0, 1, 2):
                    if q == 2:
                        pe.wait_ge(s('otm_ready'), h)
                    ins = mm(PS[:, 4 + q, 0:(q + 1) * 128], qhd[0:QH, b, q * 128:(q + 1) * 128],
                             khd[0:QH, b, 0:(q + 1) * 128])
                ins.then_inc(s('s_mm'), 1)
                if b == 0 and not (first and u == 0):
                    pe.wait_ge(s('ln_ready'), h + (R_HEAD + 1))
                    pair_out(h)
                if not last:
                    g = i if u < 3 else i + 1
                    pe.wait_ge(w_loaded[(u + 1) % 4], g * 16 + 16 * (GBASE['uq'] + 1))
                    for k in range(4):
                        ins = both(0, wring[(u + 1) % 4][:, k * QH:(k + 1) * QH], cqn[:, k, :], k == 0, k == 3)
                    ins.then_inc(s('q_mm'), 1)
                else:
                    pe.wait_ge(s('gk_ready'), 1)
                    for m in range(MH // 2):
                        for k in range(2):
                            e = (k * 8 + m) * 2 * NS
                            ins = mm(PS[:, 0, e:e + 2 * NS], wukt[:, m, k * 128:(k + 1) * 128], qkn[:, m].rearrange("p e b -> p (e b)"))
                    ins.then_inc(s('sample_mm'), 1)
                pe.wait_ge(s('p_ready'), h + 1)
                n = 0
                for kb in range(4):
                    for q in range(kb, 4):
                        ins = pe.transpose(PS[:, 4 + n // 4, (n % 4) * 128:(n % 4 + 1) * 128],
                                           pm[:, q, kb * 128:(kb + 1) * 128], ident)
                        n += 1
                ins.then_inc(s('pt2_mm'), 1)
                if not last:
                    pe.wait_ge(s('qsq_ready'), h + 2)
                    pe.wait_ge(s('omix_ready'), i * 2 + u // 2)
                    both(2, const('ones_96')[0:QH, 0:QH], qsq[0:QH, :]).then_inc(s('qss_mm'), 1)
                    both(0, rotg[0:QH, :], qraw[0:QH, :]).then_inc(s('qrot_mm'), 1)
                pe.wait_ge(s('pt2_taken'), h + 1)
                start = [0, 4, 7, 9]
                for q in range(4):
                    if q == 3 and not last:
                        key_scale(h + 1, 1 - b)
                    for kb in range(q + 1):
                        n = start[kb] + q - kb
                        ins = mm(PS[:, 6, 256 + q * VH:256 + (q + 1) * VH], ptsb[:, n * 128:(n + 1) * 128],
                                 vtok[:, kb, bass.ds(h * VH, VH)] if not isinstance(h, int) else vtok[:, kb, h * VH:(h + 1) * VH],
                                 kb == 0, kb == q)
                ins.then_inc(s('o_mm'), 1)

            for p in range(2):
                pe.wait_ge(tile_taken[p], tb + 7)
            pe.wait_ge(w_loaded[0], 16 * (GBASE['uq'] + 1))
            for k in range(4):
                ins = both(0, wring[0][:, k * QH:(k + 1) * QH], cqn[:, k, :], k == 0, k == 3)
            ins.then_inc(s('q_mm'), 1)
            pe.wait_ge(s('qsq_ready'), 1)
            both(2, const('ones_96')[0:QH, 0:QH], qsq[0:QH, :]).then_inc(s('qss_mm'), 1)
            both(0, rotg[0:QH, :], qraw[0:QH, :]).then_inc(s('qrot_mm'), 1)
            key_scale(0, 0)
            pe.wait_ge(s('v_ready'), 8)
            pe.wait_ge(s('rinv_ready'), R_KEY + 1)
            for u in range(4):
                step(0, u, first=True)
            with pe.Fori(1, MH // 4 - 1) as i:
                for u in range(4):
                    step(i, u)
            for u in range(4):
                step(MH // 4 - 1, u, last=u == 3)
            pair_out(MH)

            pe.wait_ge(s('qa_ready'), 1)
            for b in range(NS):
                for k in range(2):
                    mm(PS[0:16, 4, b:b + 1], qa[:, k, :, b], clat[:, k, T + b:T + b + 1], k == 0, False)
                ins = mm(PS[0:16, 4, b:b + 1], qr[:, :, b], krrot[:, T + b:T + b + 1], False, True)
            ins.then_inc(s('sample_mm'), 1)

            def scores(b):
                p, buf = b % 2, pagebuf[b % 4]
                pe.wait_ge(pages_loaded[b % 4], 16 * NPG * (b // 4 + 1))
                pe.wait_ge(s('qseq_ready'), b + 1)
                if b >= 2:
                    pe.wait_ge(s('sc_taken'), b - 1)
                for half in range(2):
                    o, gs = PS[0:16, 2 * p + half, :], slice(4 * half, 4 * half + 4)
                    for k in range(2):
                        mm(o, qseq[:, p, k, :], buf[:, gs, 256 + k * 128:384 + k * 128], k == 0, False)
                    ins = mm(o, qseq[0:32, p, 2, :], buf[0:32, gs, 512:640], False, True)
                ins.then_inc(s('sc_mm'), 1)

            def context_turned(p):
                for k in range(2):
                    ins = mm(PS[:, 7, k * 16:(k + 1) * 16], ctxn[:, p, k * 128:(k + 1) * 128], ident[0:16, 0:16])
                ins.then_inc(s('ctt_mm'), 1)

            pe.wait_ge(s('omix_ready'), MH // 2)
            scores(0)
            for b in range(NS):
                p = b % 2
                if b + 1 < NS:
                    scores(b + 1)
                pe.wait_ge(s('sp_ready'), b + 1)
                if b >= 2:
                    pe.wait_ge(s('spt_taken'), b - 1)
                for g in range(NPG):
                    ins = pe.transpose(PS[:, 4 + p, g * 16:(g + 1) * 16], prob[:, p, g * 128:(g + 1) * 128], ident[0:16, 0:16])
                ins.then_inc(s('spt_mm'), 1)
                if b:
                    if b >= 2:
                        pe.wait_ge(s('ctx_ready'), b - 1)
                    pe.wait_ge(s('ctxn_ready'), b)
                    context_turned(1 - p)
                pe.wait_ge(s('spt_taken'), b + 1)
                for g in range(NPG):
                    ins = mm(PS[0:16, 6, 0:256], spt[:, p, g * 16:(g + 1) * 16], pagebuf[b % 4][:, g, 0:256], g == 0, g == NPG - 1)
                ins.then_inc(s('ctx_mm'), 1)
            pe.wait_ge(s('ctx_ready'), NS - 1)
            pe.wait_ge(s('ctxn_ready'), NS)
            context_turned(1)
            pe.wait_ge(s('snew_ready'), 2)
            pe.wait_ge(s('spt_taken'), NS)
            mm(PS[:, 5, 0:MH * NS], const('ones')[0:16, :], pnd.rearrange("p h b -> p (h b)")).then_inc(s('sample_mm'), 1)
            pe.wait_ge(s('snew_ready'), 3)
            for m in range(MH // 2):
                for k in range(2):
                    ins = mm(PS[:, 7, m * 16:(m + 1) * 16], wuv[:, k, m * 128:(m + 1) * 128],
                             ctxt[:, k, 2 * m:2 * m + 2, :].rearrange("p h b -> p (h b)"), k == 0, k == 1)
            ins.then_inc(s('sample_mm'), 1)
            pe.wait_ge(s('so_ready'), 1)
            with pe.Fori(0, TURNS['outc']) as i:
                gemm_turn('outc', lambda k: mix[:, k, :], i)
            norm_sum(3)
            split_gemm('gu1', xnh, xnl, norm=3)
            pe.wait_ge(s('hid_ready'), KF + sum(DOWN[:2]))
            split_gemm('dn1', hidh, hidl)

        @block.scalar
        def _(act):
            act.preload_act_table_set(LN_EXP)

            def square(n, k, ready):
                act.wait_ge(*ready)
                if k >= 2:
                    act.wait_ge(s('sq_added'), (KD - 1) * n + k - 1)
                act.activation(sq[:, k % 2, :], xres[:, k, :], ACT.Square).then_inc(s('sq_ready'), 1)

            def rsqrt(r, out, mean):
                act.activation(out, mean, ACT.Ln, bias=small[0:out.shape[0], C_EPS:C_EPS + 1]).then_inc(s('ln_ready'), 1)
                act.wait_ge(s('ln_ready'), r + 1)
                act.activation(out, out, ACT.Exp, scale=-0.5).then_inc(s('rinv_ready'), 1)

            def norm_root(n):
                act.wait_ge(s('ssq_mm'), n + 1)
                rsqrt(R_NORM[n], two(rinv[:, R_NORM[n] % 2, :]), bank2(4))

            def high(stage, i, u):
                w = DOWN[(i * 4 + u) % 3] * 128 if stage in ('dn0', 'dn1') else SLOT
                act.wait_ge(w_loaded[u], i * 16 + 16 * (GBASE[stage] + 1))
                act.activation(whi[u % 2][:, 0:w], wring[u][:, 0:w], ACT.Copy).then_inc(s('w_hi'), 1)

            def ffn(l, n, before):
                gu, dn = f'gu{l}', f'dn{l}'
                for k in range(KD):
                    if k == KD - 1:
                        if l == 0:
                            act.wait_ge(s('sel_taken'), NS)
                            act.dma_start(O['s_gdn'], s0).then_inc(s('big_stored'), 16)
                            act.wait_ge(s('hsel_taken'), NS)
                            act.dma_start(O['s_ssm'], h0).then_inc(s('big_stored'), 16)
                        for u in range(2):
                            high(gu, 0, u)
                    square(n, k, (tile_taken[k % 2], TBASE[before] + k // 2 + 1))
                norm_root(n)
                for k in range(KD):
                    act.wait_ge(s('xn_raw'), NBASE[n] + k + 1)
                    act.activation(xnh[:, k, :], sgate[:, k % 2, :], ACT.Copy).then_inc(s('xn_hi'), 1)
                act.wait_ge(*((s('big_stored'), 32) if l == 0 else (s('out_stored'), 96)))

                def turn(i, first=False, last=False):
                    for u in range(4):
                        q, j = u // 2, i * 2 + u // 2
                        act.wait_ge(gemm_ready[u % 2], j + (TBASE[gu] + 1))
                        if u < 2:
                            high(gu, i, u + 2)
                        elif last:
                            high(dn, 0, u - 2)
                        else:
                            high(gu, i + 1, u - 2)
                        if u % 2 == 0:
                            if not (l == 0 and first):
                                act.wait_ge(s('hid_ready'), j + (KF * l - 1))
                            act.activation(two(sgate[:, q, :]), bank2(0), ACT.Silu).then_inc(tile_taken[0], 1)
                        else:
                            act.wait_ge(tile_taken[1], j + (TBASE[gu] + 1))
                            hq = hidh[:, j, :]
                            act.activation(hq, sgate[:, q, :], ACT.Copy).then_inc(s('hid_hi'), 1)
                turn(0, first=True)
                with act.Fori(1, TURNS[gu] - 1) as i:
                    turn(i)
                turn(TURNS[gu] - 1, last=True)
                if l == 0:
                    act.preload_act_table_set(LN_EXP)
                for e in range(3 * KD):
                    tile, part = divmod(e, 3)
                    if part < 2:
                        act.wait_ge(s('part_done'), 2 * KD * l + 2 * tile + part + 1)
                    else:
                        act.wait_ge(gemm_ready[tile % 2], TBASE[dn] + tile // 2 + 1)
                    if e + 2 < 3 * KD:
                        high(dn, (e + 2) // 4, (e + 2) % 4)
                    if part == 2 and l == 0:
                        square(2, tile, (tile_taken[tile % 2], TBASE[dn] + tile // 2 + 1))
                if l == 0:
                    norm_root(2)

            for k in range(KD):
                square(0, k, (x_loaded, 48))
            for u in range(2):
                high('proj', 0, u)
            act.wait_ge(g_loaded, 16 * len(SMALLS))
            norm_root(0)
            for k in range(KD):
                act.wait_ge(s('xn_raw'), k + 1)
                act.activation(xnh[:, k, :], xraw[:, k, :], ACT.Copy).then_inc(s('xn_hi'), 1)
            act.wait_ge(s('zeroed'), 1)

            def conv_turn(i, first):
                def take_tile(u):
                    p = u % 2
                    act.wait_ge(gemm_ready[p], i * 2 + (u // 2 + 1))
                    high('proj', i if u < 2 else i + 1, (u + 2) % 4)
                    if not (first and u < 2):
                        act.wait_ge(s('conv_done'), i * 4 + (u - 1))
                    act.activation(two(raw[:, p, 3:3 + TOK]), bank2(2 * p), ACT.Copy).then_inc(s('raw_ready'), 1)
                    act.activation(convout_p[:, i * 4 + u, :], PS[:, 2 * p + 1, T - 3 - HALF:T - HALF], ACT.Copy)
                    act.activation(convout_s[:, i * 4 + u, :], PS[:, 2 * p + 1, T - HALF:HALF], ACT.Copy)\
                        .then_inc(tile_taken[p], 1)

                def silu(u):
                    act.wait_ge(s('conv_done'), i * 4 + (u + 1))
                    bias = convb[:, bass.ds(i * 4 + u, 1)] if not isinstance(i, int) else convb[:, i * 4 + u:i * 4 + u + 1]
                    act.activation(hid[:, i * 4 + u, :], cacc[:, u % 2, :], ACT.Silu, bias=bias)\
                        .then_inc(s('silu_done'), 1)
                take_tile(0)
                for u in range(1, 4):
                    take_tile(u)
                    silu(u - 1)
                silu(3)
            conv_turn(0, True)
            act.preload_act_table_set(LN_EXP)
            act.activation(nega[:, :], gatec[:, NGATE:], ACT.Exp).then_inc(s('gact_ready'), 1)
            act.wait_ge(s('gprep_ready'), 1)
            act.activation(gexp[:, :, 0:NDEC], gabs[:, :, 0:NDEC], ACT.Exp, scale=-1.0)
            act.activation(gexp[:, :, NDEC:], graw[:, :, NDEC:], ACT.Exp, scale=-1.0).then_inc(s('gact_ready'), 1)
            act.wait_ge(s('gprep_ready'), 2)
            act.activation(gln[:, :, 0:NDEC], gone[:, :, 0:NDEC], ACT.Ln).then_inc(s('gact_ready'), 1)
            with act.Fori(1, 5) as i:
                conv_turn(i, False)

            act.preload_act_table_set(LN_EXP)

            def l2_root(j):
                act.wait_ge(s('l2_mm'), j + 1)
                if j >= 2:
                    act.wait_ge(s('l2_done'), j - 1)
                rsqrt(R_L2 + j, two(rinv[:, (R_L2 + j) % 2, :]), bank2(4 + 2 * (j % 2)))
            act.wait_ge(s('silu_done'), 8)
            for z in range(8):
                p = z % 2
                act.wait_ge(gemm_ready[p], 10 + z // 2 + 1)
                if z < 6:
                    high('proj', 5 + (z + 2) // 4, (z + 2) % 4)
                act.activation(two(hid[:, TZ + z, :]), bank2(2 * p), ACT.Copy).then_inc(tile_taken[p], 1)
                if 1 <= z <= 4:
                    l2_root(2 * z - 2)
                    l2_root(2 * z - 1)
                if z < 4:
                    for j in (2 * z, 2 * z + 1):
                        if j >= 2:
                            act.wait_ge(s('l2_mm'), j - 1)
                        act.activation(sq[:, j % 2, :], hid[:, j, :], ACT.Square).then_inc(s('l2sq_ready'), 1)
                if z == 5:
                    act.wait_ge(s('cumt_ready'), 1)
                    act.activation(ecumt[:, :, :], cumt[:, :, :], ACT.Exp).then_inc(s('ecumt_ready'), 1)
            for p in range(2):
                act.wait_ge(tile_taken[p], 14)
            act.activation(hid[:, TZ:TZ + 8, :], hid[:, TZ:TZ + 8, :], ACT.Silu).then_inc(s('silu_done'), 1)
            act.preload_act_table_set(LN_EXP)

            for c in range(NCH):
                act.wait_ge(s('cumB_mm'), c + 1)
                if c:
                    act.wait_ge(s('s_ready'), c)
                    act.wait_ge(s('h_ready'), c)
                act.activation(ecum[:, 0], PS[:, 0, :], ACT.Exp).then_inc(s('ecum_ready'), 1)
                act.activation(ecum[:, 1:3], PS[:, 1:3, :], ACT.Exp).then_inc(s('ecum_ready'), 1)
                act.wait_ge(s('arg_ready'), 2 * c + 1)
                act.activation(dect[:, 0], arg[:, 0], ACT.Exp).then_inc(s('dect_ready'), 1)
                act.wait_ge(s('arg_ready'), 2 * c + 2)
                act.activation(kd, kdarg, ACT.Exp).then_inc(s('kd_ready'), 1)
                act.activation(dect[:, 1:3], arg[:, 1:3], ACT.Exp).then_inc(s('dect_ready'), 1)
                act.wait_ge(s('btm_mm'), c + 1)
                act.activation(btm, PS[:, 2, 0:256], ACT.Copy).then_inc(s('btm_ready'), 1)
                for l in range(LV):
                    for half, (by_, _, _) in enumerate(INV_BANKS):
                        hs_ = slice(half * 256, (half + 1) * 256)
                        act.wait_ge(s('y_mm'), 2 * (LV * c + l) + half + 1)
                        act.activation(yinv[:, hs_], PS[:, by_, hs_], ACT.Copy).then_inc(s('y_ready'), 1)
                act.wait_ge(s('w_mm'), c + 1)
                act.activation(wt, PS[:, 3, :], ACT.Copy, scale=-1.0).then_inc(s('w_ready'), 1)
                act.wait_ge(s('vnew_mm'), c + 1)
                act.activation(vnew, PS[:, 6, :], ACT.Copy).then_inc(s('vnew_ready'), 1)
                act.wait_ge(s('ot_mm'), c + 1)
                act.activation(mix[:, 0:4, c * 128:(c + 1) * 128], by(PS[:, 2, :], GH), ACT.Copy).then_inc(s('ot_taken'), 1)

            act.wait_ge(s('spread_mm'), 1)
            act.activation(ab, PS[:, 0, 0:NDEC * NS].rearrange("p (a b) -> p a b", b=NS), ACT.Exp).then_inc(s('spread_ready'), 1)
            act.wait_ge(s('spread_mm'), 2)
            apx_ps = PS[:, 4, 0:64].rearrange("p (m e b) -> p m e b", e=2, b=NS)
            act.activation(apx[:, :, 0, :], apx_ps[:, :, 0, :], ACT.Exp)
            act.activation(apx[:, :, 1, :], apx_ps[:, :, 1, :], ACT.Copy).then_inc(s('spread_ready'), 1)
            act.wait_ge(s('row_mm'), 1)
            act.activation(vrow[0:8, :], PS[0:8, 3, :], ACT.Copy).then_inc(s('row_ready'), 1)
            act.wait_ge(s('row_mm'), 2)
            act.activation(xrow[0:8, :], PS[0:8, 7, :], ACT.Copy).then_inc(s('row_ready'), 1)
            act.wait_ge(s('xds_ready'), 2)

            def mix_root(e):
                act.wait_ge(s('osq_mm'), e + 1 if e < 4 else 4 + 2 * (e - 3))
                if e >= 2:
                    act.wait_ge(s('mix_ready'), e - 1)
                rsqrt(R_MIX + e, two(rinv[:, (R_MIX + e) % 2, :]), bank2(4 + 2 * (e % 2)))
            for j in range(8):
                if j >= 2:
                    act.wait_ge(s('osq_mm'), j - 1)
                act.activation(sq[:, j % 2, :], mix[:, j, :], ACT.Square).then_inc(s('osq_ready'), 1)
                if 1 <= j <= 4:
                    mix_root(j - 1)
                elif j == 6:
                    mix_root(4)
            mix_root(5)
            ffn(0, 1, 'outa')

            tb = TBASE['inc']
            for j in range(6):
                act.wait_ge(gemm_ready[j % 2], tb + j // 2 + 1)
                if j >= 2:
                    act.wait_ge(s('cq_mm'), j - 1)
                act.activation(two(sq[:, j % 2, :]), bank2(2 * (j % 2)), ACT.Square).then_inc(s('cq_sq'), 1)
                act.activation(two(hid[:, j, :]), bank2(2 * (j % 2)), ACT.Copy).then_inc(tile_taken[j % 2], 1)
            for r, b, n in ((R_CQ, 6, 4), (R_KV, 0, 6)):
                act.wait_ge(s('cq_mm'), n)
                rsqrt(r, two(rinv[:, r % 2, :]), bank2(b))
            act.wait_ge(s('kr_mm'), 1)
            act.activation(two(krsq), bank2(4, 32), ACT.Square).then_inc(s('krsq_ready'), 1)
            act.activation(two(krraw), bank2(4, 32), ACT.Copy).then_inc(s('kr_raw'), 1)
            for m in range(8):
                p = m % 2
                act.wait_ge(gemm_ready[p], tb + 3 + m // 2 + 1)
                if m >= 2:
                    act.wait_ge(s('kn_mm'), m - 1)
                act.activation(two(sq[:, p, :]), bank2(2 * p), ACT.Square).then_inc(s('kn_sq'), 1)
                act.activation(two(knope[:, m, :]), bank2(2 * p), ACT.Copy, scale=small[:, C_KN:C_KN + 1])\
                    .then_inc(tile_taken[p], 1)
            act.wait_ge(s('kn_mm'), 9)
            rsqrt(R_KEY, two(invr), bank2(6, 16))
            for n in range(8):
                act.wait_ge(s('v_mm'), n + 1)
                act.activation(vtok[:, n // 2, (n % 2) * 512:(n % 2 + 1) * 512], PS[:, 4 + n % 2, :], ACT.Copy)\
                    .then_inc(s('v_ready'), 1)

            def query(h, first=False):
                act.wait_ge(s('q_mm'), h + 1)
                if not first:
                    act.wait_ge(s('qrot_mm'), h)
                    act.wait_ge(s('qh_ready'), h)
                act.activation(two(qraw[0:QH, :]), bank2(0, QH), ACT.Copy)
                act.activation(two(qsq[0:QH, :]), bank2(0, QH), ACT.Square).then_inc(s('qsq_ready'), 1)

            def query_root(h, b):
                act.wait_ge(s('qss_mm'), h + 1)
                rsqrt(h + R_HEAD, two(rinv[0:QH, b, :]), bank2(2, QH))

            def pair_out(n):
                act.wait_ge(s('ott_mm'), n + 1)
                act.activation(mix[:, n, 0:T], PS[:, 3, :], ACT.Copy).then_inc(s('omix_ready'), 1)

            def step(i, u, first=False, last=False):
                h = i * 4 + u
                if u % 2 == 0 and not (first and u == 0):
                    pair_out(i * 2 + (u // 2 - 1))
                act.wait_ge(s('nb_ready'), h + 1)
                act.wait_ge(s('pt2_mm'), h)
                act.wait_ge(s('otm_ready'), h)
                for q in range(4):
                    ins = act.activation(pm[:, q, 0:(q + 1) * 128], PS[:, 4 + q, 0:(q + 1) * 128], ACT.Exp,
                                         bias=nb[:, q:q + 1], scale=PSCALE, accum_out=den[:, q:q + 1])
                ins.then_inc(s('p_ready'), 1)
                if not last:
                    query(h + 1)
                act.wait_ge(s('pt2_mm'), h + 1)
                act.wait_ge(s('o_mm'), h)
                act.activation(ptsb[:, 0:1024].rearrange("p (a n) -> p a n", a=2), PS[:, 4:6, :], ACT.Copy)
                act.activation(ptsb[:, 1024:1280], PS[:, 6, 0:256], ACT.Copy).then_inc(s('pt2_taken'), 1)
                if not last:
                    query_root(h + 1, (u + 1) % 2)
            query(0, True)
            query_root(0, 0)
            for u in range(4):
                step(0, u, first=True)
            with act.Fori(1, MH // 4 - 1) as i:
                for u in range(4):
                    step(i, u)
            for u in range(4):
                step(MH // 4 - 1, u, last=u == 3)
            pair_out(MH // 2 - 1)

            act.wait_ge(s('sample_mm'), 1)
            act.activation(qa[:, :, :, :], PS[:, 0, 0:256].rearrange("p (k h b) -> p k h b", k=2, b=NS), ACT.Copy).then_inc(s('qa_ready'), 1)

            def context_out(b, last):
                act.wait_ge(s('ctt_mm'), last)
                out = ctxt[:, :, :, b] if isinstance(b, int) else ctxt[:, :, :, bass.ds(b, 1)].rearrange("p k h b -> p k (h b)")
                act.activation(out, PS[:, 7, 0:32].rearrange("p (k h) -> p k h", k=2), ACT.Copy).then_inc(s('ctx_ready'), 1)

            def sequence(i, p, first=False):
                b = i * 2 + p
                sn = snew[:, b:b + 1] if isinstance(b, int) else snew[:, bass.ds(b, 1)]
                act.wait_ge(s('smx_ready'), b + 1)
                if not first:
                    act.wait_ge(s('rden_ready'), b - 1)
                act.activation(pn16[:, p:p + 1], sn, ACT.Exp, bias=nb16[:, p:p + 1], scale=PSCALE)
                act.activation(prob[:, p], prob[:, p], ACT.Exp, bias=nb16[:, p:p + 1], scale=PSCALE, accum_out=den16[:, p:p + 1])\
                    .then_inc(s('sp_ready'), 1)
                act.wait_ge(s('spt_mm'), b + 1)
                if not first:
                    act.wait_ge(s('ctx_mm'), b - 1)
                act.activation(spt[:, p], PS[:, 4 + p, 0:128], ACT.Copy).then_inc(s('spt_taken'), 1)
                if not (first and p == 0):
                    context_out(b - 1, b)
                act.wait_ge(s('ctx_mm'), b + 1)
                act.wait_ge(s('rden_ready'), b + 1)
                act.activation(ctxn[:, p], PS[0:16, 6, 0:256], ACT.Copy, scale=rden16[:, p:p + 1]).then_inc(s('ctxn_ready'), 1)
            for p in range(2):
                sequence(0, p, first=True)
            with act.Fori(1, NS // 2) as i:
                for p in range(2):
                    sequence(i, p)
            context_out(NS - 1, NS)
            act.wait_ge(s('sample_mm'), 4)
            for e in range(2):
                so = PS[64 * e:64 * e + 64, 7, 0:MH * NS].rearrange("p (m e b) -> p m e b", e=2, b=NS)
                ins = act.activation(mix[64 * e:64 * e + 64, :, T:TOK], so[:, :, e, :], ACT.Copy)
            ins.then_inc(s('so_ready'), 1)
            ffn(1, 3, 'outc')

        @block.vector
        def _(dve):
            st = Steps(dve, s('dve_own'))
            own = s('dve_own')
            tt, ts_, stt = dve.tensor_tensor, dve.tensor_scalar, dve.scalar_tensor_tensor
            for k in range(KD - 1):
                dve.wait_ge(s('sq_ready'), k + 1)
                if k == 0:
                    st(dve.tensor_copy(sqsum[:, :], sq[:, 0, :]), s('sq_added'))
                else:
                    dve.wait_ge(s('sq_added'), k)
                    st(tt(sqsum[:, :], sqsum[:, :], sq[:, k % 2, :], ALU.add), s('sq_added'))
            dve.wait_ge(c_loaded, 16)
            dve.wait_ge(g_loaded, 16 * len(SMALLS))

            def normalise(n):
                dve.wait_ge(s('rinv_ready'), R_NORM[n] + 1)
                for k in range(KD):
                    st(stt(out=xn[:, k, :], in0=xres[:, k, :], scalar=gains[:, n, k:k + 1], in1=rinv[:, R_NORM[n] % 2, :],
                           op0=ALU.mult, op1=ALU.mult), s('xn_ready'))

            def residual(stage, l, after=None):
                for k in range(KD):
                    p = k % 2
                    if k == KD - 1:
                        for u in range(2):
                            low(f'gu{l}', 0, u)
                    dve.wait_ge(gemm_ready[p], TBASE[stage] + k // 2 + 1)
                    st(tt(two(xres[:, k, :]), two(xres[:, k, :]), bank2(2 * p), ALU.add), tile_taken[p])
                    if after:
                        after(k)

            def low(stage, i, u):
                w = DOWN[(i * 4 + u) % 3] * 128 if stage in ('dn0', 'dn1') else SLOT
                dve.wait_ge(s('w_hi'), i * 4 + (FBASE[stage] + u + 1))
                tt(wlo[u % 2][:, 0:w], wring[u][:, 0:w], whi[u % 2][:, 0:w].bitcast(F32), ALU.subtract).then_inc(s('w_split'), 1)

            def ffn(l, n):
                gu, dn = f'gu{l}', f'dn{l}'
                dve.wait_ge(s('rinv_ready'), R_NORM[n] + 1)
                if l == 0:
                    dve.wait_ge(s('rec_stored'), 32)

                def raw_tile(k):
                    st(stt(out=sgate[:, k % 2, :], in0=xres[:, k, :], scalar=gains[:, n, k:k + 1], in1=rinv[:, R_NORM[n] % 2, :],
                           op0=ALU.mult, op1=ALU.mult), s('xn_raw'))
                raw_tile(0)
                for k in range(KD):
                    if k + 1 < KD:
                        if k:
                            dve.wait_ge(s('xn_ready'), KD * n + k)
                        raw_tile(k + 1)
                    dve.wait_ge(s('xn_hi'), NBASE[n] + k + 1)
                    st(tt(xnl[:, k, :], sgate[:, k % 2, :], xnh[:, k, :].bitcast(F32), ALU.subtract), s('xn_ready'))
                dve.wait_ge(*((s('big_stored'), 32) if l == 0 else (s('out_stored'), 96)))

                def turn(i, last=False):
                    for u in range(4):
                        q, j = u // 2, i * 2 + u // 2
                        dve.wait_ge(gemm_ready[u % 2], j + (TBASE[gu] + 1))
                        if u % 2:
                            dve.wait_ge(tile_taken[0], j + (TBASE[gu] + 1))
                            tt(two(sgate[:, q, :]), two(sgate[:, q, :]), bank2(2), ALU.mult).then_inc(tile_taken[1], 1)
                        if u < 2:
                            low(gu, i, u + 2)
                        elif last:
                            low(dn, 0, u - 2)
                        else:
                            low(gu, i + 1, u - 2)
                        if u % 2:
                            dve.wait_ge(s('hid_hi'), j + (KF * l + 1))
                            hh, hl = hidh[:, j, :], hidl[:, j, :]
                            tt(hl, sgate[:, q, :], hh.bitcast(F32), ALU.subtract).then_inc(s('hid_ready'), 1)
                with dve.Fori(0, TURNS[gu] - 1) as i:
                    turn(i)
                turn(TURNS[gu] - 1, last=True)
                for e in range(3 * KD):
                    tile, part = divmod(e, 3)
                    p = tile % 2
                    if part == 2:
                        dve.wait_ge(gemm_ready[p], TBASE[dn] + tile // 2 + 1)
                        st(tt(two(xres[:, tile, :]), two(xres[:, tile, :]), bank2(2 * p), ALU.add), tile_taken[p])
                    if e + 2 < 3 * KD:
                        low(dn, (e + 2) // 4, (e + 2) % 4)

            for u in range(2):
                low('proj', 0, u)
            dve.wait_ge(s('rinv_ready'), 1)
            for k in range(KD + 1):
                if k < KD:
                    st(stt(out=xraw[:, k, :], in0=xres[:, k, :], scalar=gains[:, 0, k:k + 1], in1=rinv[:, 0, :],
                           op0=ALU.mult, op1=ALU.mult), s('xn_raw'))
                if k:
                    dve.wait_ge(s('xn_hi'), k)
                    st(tt(xnl[:, k - 1, :], xraw[:, k - 1, :], xnh[:, k - 1, :].bitcast(F32), ALU.subtract), s('xn_ready'))
            def conv_turn(i, first):
                for u in range(4):
                    p, j = u % 2, i * 4 + u

                    def w(t):
                        return convw[:, j, t:t + 1]
                    low('proj', i if u < 2 else i + 1, (u + 2) % 4)
                    dve.wait_ge(s('raw_ready'), j + 1)
                    if not (first and u < 2):
                        dve.wait_ge(s('silu_done'), i * 4 + (u - 1))
                    st(ts_(cacc[:, p, :], raw[:, p, 3:3 + TOK], w(3), None, ALU.mult))
                    for t in range(3):
                        st.sync()
                        st(stt(out=cacc[:, p, T:TOK], in0=prev[:, j, t, :], scalar=w(t), in1=cacc[:, p, T:TOK],
                               op0=ALU.mult, op1=ALU.add))
                        st(stt(out=cacc[:, p, 0:T], in0=raw[:, p, t:t + T], scalar=w(t), in1=cacc[:, p, 0:T],
                               op0=ALU.mult, op1=ALU.add), s('conv_done') if t == 2 else None)
            dve.wait_ge(s('zeroed'), 1)
            conv_turn(0, True)
            dve.wait_ge(s('gates_mm'), 1)
            st(dve.memset(graw[:, :, :], 0.0))
            st.sync()
            st(tt(graw[:, 0:4, :], PS[:, 6, 0:4 * NGATE].rearrange("p (t n) -> p t n", n=NGATE), across(gatec[:, 0:NGATE], 4), ALU.add))
            st(tt(graw[0:NS, 4, :], PS[0:NS, 6, 4 * NGATE:5 * NGATE], gatec[0:NS, 0:NGATE], ALU.add))
            st.sync()
            st(stt(out=gabs[:, :, :], in0=graw[:, :, :], scalar=-1.0, in1=graw[:, :, :], op0=ALU.mult, op1=ALU.max), s('gprep_ready'))
            dve.wait_ge(s('gact_ready'), 2)
            st(ts_(gone[:, :, :], gexp[:, :, :], 1.0, None, ALU.add), s('gprep_ready'))
            st.sync()
            st(dve.reciprocal(grec[:, :, :], gone[:, :, :]))
            dc = slice(0, NDEC)
            st(ts_(gabs[:, :, dc], gone[:, :, dc], -1.0, None, ALU.add))
            st.sync()
            st(tt(gabs[:, :, dc], gexp[:, :, dc], gabs[:, :, dc], ALU.subtract))
            st.sync()
            st(tt(gabs[:, :, dc], gabs[:, :, dc], grec[:, :, dc], ALU.mult))
            dve.wait_ge(s('gact_ready'), 3)
            st.sync()
            st(tt(gabs[:, :, dc], gabs[:, :, dc], gln[:, :, dc], ALU.add))
            st.sync()
            st(stt(out=gsp[:, :, dc], in0=graw[:, :, dc], scalar=0.0, in1=gabs[:, :, dc], op0=ALU.max, op1=ALU.add))
            dve.wait_ge(s('gact_ready'), 1)
            st.sync()
            st(stt(out=la[:, :, :], in0=gsp[:, :, dc], scalar=-1.0, in1=across(nega[:, :], 5), op0=ALU.mult, op1=ALU.mult), s('la_ready'))

            st.loop(1, 5, lambda i: conv_turn(i, False), [(own, 24), (s('conv_done'), 4)])

            dve.wait_ge(s('gates_mm'), 2)
            st(dve.tensor_copy(cumt[:, :, :], PS[:, 7, 0:NCH * NDEC].rearrange("p (c n) -> p c n", n=NDEC)), s('cumt_ready'))
            for z in range(6):
                low('proj', (22 + z) // 4, (22 + z) % 4)
                for j in (2 * z - 2, 2 * z - 1) if 1 <= z <= 4 else ():
                    dve.wait_ge(s('rinv_ready'), R_L2 + j + 1)
                    st(stt(out=hid[:, j, :], in0=hid[:, j, :], scalar=128 ** -0.5 if j < 4 else 1.0, in1=rinv[:, (R_L2 + j) % 2, :],
                           op0=ALU.mult, op1=ALU.mult), s('l2_done'))
            dve.wait_ge(s('ecumt_ready'), 1)
            st(tt(bec[:, :, :], beta[:, 0:NCH], ecumt[:, :, 0:GH], ALU.mult))
            st.sync()

            ident4 = across(ident, GH)
            for c in range(NCH):
                tc_ = slice(c * 128, (c + 1) * 128)
                dve.wait_ge(s('cumB_mm'), c + 1)
                dve.wait_ge(s('ecum_ready'), 2 * c + 1)
                if c == 0:
                    dve.wait_ge(gemm_ready[1], 14)
                    dve.wait_ge(s('silu_done'), NCONV)
                for h in range(NDEC):
                    if h == GH:
                        dve.wait_ge(s('ecum_ready'), 2 * c + 2)
                        st(tt(kdarg.rearrange("p (a b) -> p a b", b=4), PS[:, 0:3, 127:512:128],
                              cumt[:, c, :].rearrange("p (a b) -> p a b", b=4), ALU.subtract))
                    hs_ = slice((h % 4) * 128, (h % 4 + 1) * 128)
                    st(stt(out=arg[:, h // 4, hs_], in0=PS[:, h // 4, hs_], scalar=cumt[:, c, h:h + 1],
                           in1=const('decaymask'), op0=ALU.subtract, op1=ALU.min),
                       s('arg_ready') if h in (GH - 1, NDEC - 1) else None)
                dve.wait_ge(s('dect_ready'), 2 * c + 1)
                dve.wait_ge(s('betaB_mm'), c + 1)
                st(tt(bm, dect[:, 0, :], PS[:, 3, :], ALU.mult), s('bm_ready'))
                dve.wait_ge(s('kk_mm'), c + 1)
                st.sync()
                st(tt(lt, PS[:, 4, :], bm, ALU.mult), s('lt_ready'))
                dve.wait_ge(s('qk_mm'), c + 1)
                st(tt(attnt, PS[:, 5, :], dect[:, 0, :], ALU.mult), s('attn_ready'))
                dve.wait_ge(s('mt_ready'), (LV + 1) * c + 1)
                st(tt(by(xinvt, GH), ident4, by(mt[:, 0], GH), ALU.subtract))
                dve.wait_ge(s('xinit_mm'), c + 1)
                st(tt(by(xinv, GH), ident4, by(PS[:, 3, :], GH), ALU.subtract), s('xinit_ready'))
                dve.wait_ge(s('kd_ready'), c + 1)
                dve.wait_ge(s('ktm_mm'), c + 1)
                st(tt(by(kbe, GH), by(PS[:, 6, :], GH), over(bec[:, c, :], 128), ALU.mult))
                st(tt(by(kdec, GH), by(PS[:, 6, :], GH), over(kd[:, 0:GH], 128), ALU.mult))
                dve.wait_ge(s('vtm_mm'), c + 1)
                st(tt(by(vb, GH), by(PS[:, 7, :], GH), over(beta[:, c, :], 128), ALU.mult), s('kvs_ready'))
                fill = []

                def ssd_scores():
                    dve.wait_ge(s('bc_mm'), c + 1)
                    dve.wait_ge(s('dect_ready'), 2 * c + 2)
                    for g in range(SG):
                        st(tt(by(scoret[:, g], 4), by(dect[:, 1 + g, :], 4), across(PS[:, 0, g * 128:(g + 1) * 128], 4), ALU.mult),
                           s('score_ready') if g else None)
                    dve.wait_ge(s('xtm_mm'), c + 1)
                    st(tt(by(xdt, SH), by(PS[:, 1, :], SH), over(gdt[:, c, :], 64), ALU.mult))
                    st.sync()
                    st(tt(by(xde, SH), by(xdt, SH), over(kd[:, GH:], 64), ALU.mult), s('xdt_ready'))
                    for g in range(SG):
                        st(tt(by(ce[g], 4), across(hid[:, TC + g, tc_], 4), by(ecum[:, 1 + g], 4), ALU.mult),
                           s('ce_ready') if g else None)

                def ssd_out():
                    dve.wait_ge(s('yt_mm'), c + 1)
                    if c == 0:
                        dve.wait_ge(s('silu_done'), NCONV + 1)
                    for m in range(4):
                        st(stt(out=mix[:, 4 + m, tc_], in0=hid[:, TX + m, tc_], scalar=small[:, C_D + m:C_D + m + 1],
                               in1=PS[:, 0, m * 128:(m + 1) * 128], op0=ALU.mult, op1=ALU.add))
                    st.sync()
                    st(tt(mix[:, 4:8, tc_], mix[:, 4:8, tc_], hid[:, TSZ:TSZ + 4, tc_], ALU.mult), s('yt_taken'))
                    last = ecum[:, 1:3, 127:512:128].rearrange("p a b -> p a b")
                    st(tt(hssd.rearrange("p (a b x) -> p a b x", a=2, b=4), hssd.rearrange("p (a b x) -> p a b x", a=2, b=4),
                          last.unsqueeze(3).broadcast_to([128, 2, 4, 64]), ALU.mult))

                def queries():
                    st(tt(by(qe, GH), hid[:, TQ:TQ + 4, tc_], by(ecum[:, 0], GH), ALU.mult), s('qe_ready'))
                fill = {0: ssd_scores, 2: ssd_out, 3: queries}
                for l in range(LV):
                    for half, (_, bp, bpt) in enumerate(INV_BANKS):
                        hs_ = slice(half * 256, (half + 1) * 256)
                        if l < LV - 1:
                            dve.wait_ge(s('p_mm'), 2 * ((LV - 1) * c + l) + half + 1)
                            st(tt(xinv[:, hs_], xinv[:, hs_], PS[:, bp, hs_], ALU.subtract))
                        dve.wait_ge(s('pt_mm'), 2 * (LV * c + l) + half + 1)
                        st(tt(xinvt[:, hs_], xinvt[:, hs_], PS[:, bpt, hs_], ALU.subtract), s('x_ready'))
                    if l in fill:
                        fill[l]()
                dve.wait_ge(s('hup_mm'), c + 1)
                st.sync()
                st(tt(hssd, hssd, PS[:, 1, :], ALU.add), s('h_ready'))
                dve.wait_ge(s('kv_mm'), c + 1)
                for h in range(GH):
                    hs_ = slice(h * 128, (h + 1) * 128)
                    st(stt(out=sgdn[:, hs_], in0=sgdn[:, hs_], scalar=ecum[:, 0, h * 128 + 127:h * 128 + 128],
                           in1=PS[:, 7, hs_], op0=ALU.mult, op1=ALU.add), s('s_ready') if h == GH - 1 else None)

            dve.wait_ge(s('ot_taken'), NCH)
            sc = slice(T, TOK)
            st(dve.tensor_copy(vals[0:8, 0:12], la[0:8, 4, :]))
            st(dve.tensor_copy(vals[0:8, 12:16], beta[0:8, 4, :]))
            st(dve.tensor_copy(vals[0:8, 16:24], gdt[0:8, 4, :]))
            st.sync()
            for e, col in ((0, GH), (1, 16)):
                st(dve.tensor_copy(by(supd[0:8, e], SH), over(vals[0:8, col:col + SH], 64)))
            st(tt(valx[0:8], over(vals[0:8, :], NS), across(ident[0:8, 0:8], 24), ALU.mult), s('sprep_ready'))
            st(tt(qkp, hid[:, TQ:TQ + 4, sc], hid[:, TK:TK + 4, sc], ALU.mult), s('sprep_ready'))
            st(tt(bcp, hid[:, TB:TB + 2, sc], hid[:, TC:TC + 2, sc], ALU.mult), s('sprep_ready'))
            dve.wait_ge(s('spread_mm'), 1)
            dve.wait_ge(s('spread_ready'), 1)
            st(dve.tensor_copy(valb, PS[:, 0, 0:192].rearrange("p (a b) -> p a b", b=NS)), s('valb_ready'))
            st.sync()
            st(tt(kb8, hid[:, TK:TK + 4, sc], valb[:, 12:16], ALU.mult))
            dve.wait_ge(s('spread_ready'), 1)
            st.sync()
            r2 = rhs2.rearrange("p (h b) e -> p h b e", b=NS)
            st(tt(r2[:, :, :, 0], kb8, ab[:, 0:GH], ALU.mult))
            st(tt(r2[:, :, :, 1], hid[:, TQ:TQ + 4, sc], ab[:, 0:GH], ALU.mult), s('rhs2_ready'))
            st(tt(vnt, hid[:, TV:TV + 4, sc], valb[:, 12:16], ALU.mult))
            dve.wait_ge(s('sv_mm'), 1)
            st.sync()
            sv = PS[:, 1, 0:2 * GH * NS].rearrange("p (h b e) -> p h b e", b=NS, e=2)
            st(tt(vnt, vnt, sv[:, :, :, 0], ALU.subtract), s('vnt_ready'))
            dve.wait_ge(s('qks_mm'), 1)
            st.sync()
            st(tt(kb8, vnt, PS[:, 2, 0:GH * NS].rearrange("p (h b) -> p h b", b=NS), ALU.mult))
            st.sync()
            st(tt(mix[:, 0:4, sc], kb8, sv[:, :, :, 1], ALU.add))
            dve.wait_ge(s('spread_ready'), 2)
            st(tt(xds, hid[:, TX:TX + 4, sc], apx[:, :, 1, :], ALU.mult), s('xds_ready'))
            dve.wait_ge(s('y0_mm'), 1)
            st(tt(ysm, PS[:, 6, 0:32].rearrange("p (m b) -> p m b", b=NS), apx[:, :, 0, :], ALU.mult))
            dve.wait_ge(s('qks_mm'), 2)
            st.sync()
            st(tt(yt2.rearrange("p (g m) b -> p g m b", g=2), xds.rearrange("p (g m) b -> p g m b", g=2),
                  PS[:, 5, 0:16].rearrange("p (g b) -> p g b", b=NS).unsqueeze(2).broadcast_to([128, 2, 2, NS]), ALU.mult))
            st.sync()
            st(tt(ysm, ysm, yt2, ALU.add))
            st.sync()
            st(tt(yt2, hid[:, TX:TX + 4, sc], over(small[:, C_D:C_D + 4], NS), ALU.mult))
            st.sync()
            st(tt(ysm, ysm, yt2, ALU.add))
            st.sync()
            st(tt(mix[:, 4:8, sc], ysm, hid[:, TSZ:TSZ + 4, sc], ALU.mult), s('xds_ready'))
            for e in range(6):
                dve.wait_ge(s('rinv_ready'), R_MIX + e + 1)
                root = rinv[:, (R_MIX + e) % 2, :]
                if e < 4:
                    st(stt(out=mix[:, e, :], in0=mix[:, e, :], scalar=small[:, C_GDN:C_GDN + 1], in1=root, op0=ALU.mult, op1=ALU.mult))
                    st.sync()
                    st(tt(mix[:, e, :], mix[:, e, :], hid[:, TZ + e, :], ALU.mult), s('mix_ready'))
                else:
                    for m in (2 * e - 4, 2 * e - 3):
                        st(stt(out=mix[:, m, :], in0=mix[:, m, :], scalar=small[:, C_SSM + m - 4:C_SSM + m - 3], in1=root,
                               op0=ALU.mult, op1=ALU.mult), s('mix_ready'))
            def update(b):
                dve.wait_ge(s('sel_mm'), b + 1)
                if b:
                    dve.wait_ge(s('sel_taken'), b)
                st(tt(by(supd[:, 0], GH), by(PS[:, 6, :], GH), over(hid[:, TK:TK + 4, T + b], 128), ALU.mult))
                st.sync()
                if b == 0:
                    dve.wait_ge(s('s_decayed'), GH)
                st(tt(s0[:, :, b, :], s0[:, :, b, :], by(supd[:, 0], GH), ALU.add), s('sel_taken'))
                dve.wait_ge(s('hsel_mm'), b + 1)
                if b:
                    dve.wait_ge(s('hsel_taken'), b)
                st(tt(by(supd[:, 1], 2), by(PS[:, 7, :], 2), over(hid[:, TB:TB + 2, T + b], 256), ALU.mult))
                st.sync()
                dve.wait_ge(s('s_decayed'), GH + b + 1)
                st(tt(h0[:, b], h0[:, b], supd[:, 1], ALU.add), s('hsel_taken'))
            residual('outa', 0, lambda k: [update(b) for b in UPDATES[k]])
            ffn(0, 1)
            normalise(2)

            dve.wait_ge(g_loaded, 16 * (len(SMALLS) + 4))
            st(ts_(cosg[0:QH, :], rope[0:QH, 0, :], small[0:QH, C_QN:C_QN + 1], None, ALU.mult))
            st(ts_(rotg[0:QH, :], const('rot96')[0:QH, 0:QH], small[0:QH, C_QN:C_QN + 1], None, ALU.mult))
            st(ts_(rotk, const('rot32')[0:32, 0:32], small[0:32, C_KR:C_KR + 1], None, ALU.mult), s('rot_ready'))
            dve.wait_ge(s('rinv_ready'), R_CQ + 1)
            dve.wait_ge(tile_taken[1], TBASE['inc'] + 2)
            for j in range(4):
                st(stt(out=cqn[:, j, :], in0=cqn[:, j, :], scalar=small[:, C_QA + j:C_QA + j + 1], in1=rinv[:, R_CQ % 2, :],
                       op0=ALU.mult, op1=ALU.mult), s('cq_ready') if j == 3 else None)
            dve.wait_ge(s('rinv_ready'), R_KV + 1)
            dve.wait_ge(tile_taken[1], TBASE['inc'] + 3)
            for j in range(2):
                st(stt(out=clat[:, j, :], in0=clat[:, j, :], scalar=small[:, C_KVA + j:C_KVA + j + 1], in1=rinv[:, R_KV % 2, :],
                       op0=ALU.mult, op1=ALU.mult), s('cq_ready') if j == 1 else None)
            dve.wait_ge(s('kr_raw'), 1)
            st(ts_(krg, krraw, small[0:32, C_KR:C_KR + 1], None, ALU.mult))
            st.sync()
            st(tt(krg, krg, rope[0:32, 2, :], ALU.mult))
            dve.wait_ge(s('kr_mm'), 2)
            st(tt(two(krt), bank2(4, 32), two(rope[0:32, 3, :]), ALU.mult))
            st.sync()
            st(tt(krrot, krg, krt, ALU.add), s('krot_ready'))
            dve.wait_ge(s('rinv_ready'), R_KEY + 1)
            dve.wait_ge(tile_taken[0], TBASE['outc'])
            dve.wait_ge(tile_taken[1], TBASE['outc'])

            def key_mask(h, b):
                col = ident[0:16, h:h + 1] if isinstance(h, int) else ident[0:16, bass.ds(h, 1)]
                st(ts_(invm[:, b, :], invr[:, 0:T], col, None, ALU.mult), s('invm_ready'))

            def query(h, pair, b):
                dve.wait_ge(s('qsq_ready'), h + 1)
                st(tt(qt1[0:QH, :], qraw[0:QH, :], cosg[0:QH, :], ALU.mult))
                dve.wait_ge(s('qrot_mm'), h + 1)
                st(tt(two(qt2[0:QH, :]), bank2(0, QH), two(rope[0:QH, 1, :]), ALU.mult))
                st.sync()
                st(tt(qt1[0:QH, :], qt1[0:QH, :], qt2[0:QH, :], ALU.add))
                st.sync()
                dve.wait_ge(s('rinv_ready'), h + (R_HEAD + 1))
                st(tt(qhd[0:QH, b, :], qt1[0:QH, :], rinv[0:QH, b, :], ALU.mult), s('qh_ready'))
                st.sync()
                st(dve.tensor_copy(qs[0:QH, h, :], qhd[0:QH, b, T:TOK]))
                dve.wait_ge(s('invb_mm'), h + 1)
                st(tt(khd[0:64, b, :], knope[64 * b:64 * b + 64, pair, 0:T], PS[0:64, 2, :], ALU.mult))
                st(tt(khd[64:96, b, :], krrot[:, 0:T], PS[0:32, 2, :], ALU.mult), s('k_ready'))

            def step(i, u, last=False):
                h, b = i * 4 + u, u % 2
                if not last:
                    key_mask(h + 1, 1 - b)
                else:
                    st.sync()
                    st(dve.memset(qkn[:, :, :, :], 0.0))
                    st.sync()
                    for p in range(2):
                        src = qs[0:64, :, :].rearrange("p (m e) b -> p m e b", e=2)[:, :, p, :]
                        st(ts_(qkn[64 * p:64 * p + 64, :, p, :], src, small[0:64, C_KN:C_KN + 1], None, ALU.mult))
                    st(dve.tensor_copy(qr, qs[64:96]), s('gk_ready'))
                dve.wait_ge(s('s_mm'), h + 1)
                for q in range(4):
                    blk = PS[:, 4 + q, q * 128:(q + 1) * 128]
                    st(tt(blk, blk, const('causal'), ALU.add))
                st.sync()
                for q in range(4):
                    st(dve.tensor_reduce(mx[:, q:q + 1], PS[:, 4 + q, 0:(q + 1) * 128], AX.X, ALU.max))
                st.sync()
                dve.wait_ge(s('p_ready'), h)
                st(ts_(nb, mx, -PSCALE, None, ALU.mult), s('nb_ready'))
                if not last:
                    query(h + 1, i * 2 + (u + 1) // 2, 1 - b)
                dve.wait_ge(s('o_mm'), h + 1)
                if b == 0:
                    dve.wait_ge(s('ott_mm'), i * 2 + u // 2)
                st(dve.reciprocal(rden, den))
                st.sync()
                st(tt(otm[:, :, b * VH:(b + 1) * VH], PS[:, 6, 256:512].rearrange("p (q v) -> p q v", v=VH), over(rden, VH), ALU.mult),
                   s('otm_ready'))
            key_mask(0, 0)
            query(0, 0, 0)
            per = [(own, 4 * (8 + 6)), (s('invm_ready'), 4), (s('nb_ready'), 4), (s('qh_ready'), 4),
                   (s('k_ready'), 4), (s('otm_ready'), 4)]
            for u in range(4):
                step(0, u)
            st.loop(1, MH // 4 - 1, lambda i: [step(i, u) for u in range(4)], per)
            for u in range(4):
                step(MH // 4 - 1, u, last=u == 3)

            dve.wait_ge(s('sample_mm'), 2)
            st(tt(snew, PS[0:16, 4, 0:NS], invr[:, T:TOK], ALU.mult), s('snew_ready'))

            for b in range(NS):
                p, here = b % 2, slice(b, b + 1)
                m_, nb_, dn_, pn_, rd_ = (v[:, p:p + 1] for v in (m16, nb16, den16, pn16, rden16))
                dve.wait_ge(s('sc_mm'), b + 1)
                if b >= 2:
                    dve.wait_ge(s('spt_mm'), b - 1)
                st(tt(prob[:, p].rearrange("p (g s) -> p g s", g=NPG), PS[0:16, 2 * p:2 * p + 2, :].rearrange("p a (g s) -> p (a g) s", s=128),
                      pagebuf[b % 4][32:48, :, 512:640], ALU.mult), s('sc_taken'))
                st.sync()
                st(dve.tensor_reduce(m_, prob[:, p], AX.X, ALU.max))
                st.sync()
                st(tt(m_, m_, snew[:, here], ALU.max))
                st.sync()
                st(ts_(nb_, m_, -PSCALE, None, ALU.mult), s('smx_ready'))
                dve.wait_ge(s('sp_ready'), b + 1)
                if b >= 2:
                    dve.wait_ge(s('ctxn_ready'), b - 1)
                st(tt(dn_, dn_, pn_, ALU.add))
                st.sync()
                st(dve.reciprocal(rd_, dn_))
                st.sync()
                st(tt(pnn[:, here], pn_, rd_, ALU.mult), s('rden_ready'))
            st.sync()
            st(tt(pnd, over(ident[0:16, 0:16], NS), across(pnn, MH), ALU.mult), s('snew_ready'))
            dve.wait_ge(s('sample_mm'), 3)
            dve.wait_ge(s('ctx_ready'), NS)
            new = spt[:, :, :].rearrange("p a (h b) -> p a h b", b=NS)
            for k in range(2):
                st(tt(new[:, k], PS[:, 5, 0:MH * NS].rearrange("p (h b) -> p h b", b=NS), across(clat[:, k, T:TOK], MH), ALU.mult))
            st.sync()
            st(tt(ctxt[:, :, :, :], ctxt[:, :, :, :], new, ALU.add), s('snew_ready'))
            residual('outc', 1)
            ffn(1, 3)


def _constants():
    r = np.arange(128)
    row, col = r[:, None], r[None, :]
    m = {'ident': row == col, 'triu': row <= col, 'ones': np.ones((128, 128)),
         'decaymask': np.where(col >= row, 0.0, NEG), 'causal': np.where(col <= row, 0.0, NEG)}
    for n, v in (('ones_d', D), ('ones_128', 128), ('ones_256', 256), ('ones_512', 512), ('ones_96', 96)):
        m[n] = np.full((128, 128), 1.0 / v)
    half = RD // 2
    for n, base in (('rot96', NOPE), ('rot32', 0)):
        z = np.zeros((128, 128))
        for e in range(half):
            z[base + half + e, base + e] = -1.0
            z[base + e, base + half + e] = 1.0
        m[n] = z
    z = np.zeros((128, 8, 16))
    for t in range(8):
        for p in range(128):
            z[p, t, 2 * t + p // 64] = 1.0 / QH
    m['headsel'] = z.reshape(128, 128)
    for l in range(LV + 1):
        b = 2 ** l
        m[f'inv{l}'] = (row // (2 * b) == col // (2 * b)) & ((col // b) % 2 == 1) & ((row // b) % 2 == 0)
    return np.stack([np.asarray(m[n], np.float32) for n in CONSTS], axis=1)


def _rope_tables():
    f32 = np.float32
    half = RD // 2
    freq = (f32(10000.0) ** (-np.arange(half, dtype=f32) / f32(half))).astype(f32)
    pos = np.concatenate([np.arange(T, dtype=f32), np.full(NS, NPG * 128, f32)])
    ang = (pos[:, None] * freq[None, :]).astype(f32)
    cos, sin = np.cos(ang).T.astype(f32), np.sin(ang).T.astype(f32)
    cos, sin = np.concatenate([cos, cos]), np.concatenate([sin, sin])
    t = np.zeros((128, 4, TOK), f32)
    t[0:NOPE, 0] = 1.0
    t[NOPE:QH, 0], t[NOPE:QH, 1] = cos, sin
    t[0:RD, 2], t[0:RD, 3] = cos, sin
    return t


def _cols(v, n):
    return np.ascontiguousarray(np.asarray(v).reshape(n, 128).T)


def _tiles(w, m=128):
    k, n = w.shape
    return np.ascontiguousarray(w.reshape(k // 128, 128, n // m, m).transpose(2, 1, 0, 3)).reshape(n // m, 128, -1)


def kernel(**inputs):
    import concourse.bacc as _bacc
    from concourse.bass_utils import run_bass_kernel_spmd as _run
    I = {k: np.asarray(v) for k, v in inputs.items()}
    f = {}
    x = np.concatenate([I['x_prompt'][0], I['x_sample'][:, 0]], axis=0)
    f['x'] = np.ascontiguousarray(x.T.reshape(KD, 128, TOK).transpose(1, 0, 2))
    w = I['w_in_a'][0]
    c = np.cumsum([0, 1536, 512, 4, 4, 512, 1024, 8])
    qkv, gz, ga, gb, sz, xbc, dt = (w[:, c[i]:c[i + 1]] for i in range(7))
    f['w_proj'] = _tiles(np.concatenate([qkv, xbc, gz, sz], axis=1))
    f['w_gate'] = np.ascontiguousarray(np.concatenate([ga, dt, gb], axis=1).reshape(KD, 128, NGATE).transpose(1, 0, 2))
    f['w_outa'], f['w_outc'] = _tiles(I['w_out_a'][0]), _tiles(I['w_out_c'][0])
    for l in range(2):
        gu = I['w_gate_up'][l].reshape(D, 2, KF, 128).transpose(0, 2, 1, 3).reshape(D, 2 * DFF)
        f[f'w_gu{l}'] = _tiles(gu)
        f[f'w_dn{l}'] = np.ascontiguousarray(I['w_down'][l].reshape(KF, 128, KD, 128).transpose(2, 1, 0, 3)).reshape(KD, 128, KF * 128)
    wc = I['w_in_c'][0]
    uk = I['w_uk'][0]
    f['w_inc'] = np.concatenate([_tiles(wc[:, 0:768]), uk.reshape(2, 128, 1024)], axis=0)
    f['w_kr'] = np.ascontiguousarray(wc[:, 768:800].reshape(KD, 128, RD).transpose(1, 0, 2))
    f['w_uq'] = _tiles(I['w_uq'][0], QH)
    f['w_uv'] = np.ascontiguousarray(I['w_uv'][0].reshape(2, 128, 1024).transpose(1, 0, 2))
    f['w_ukt'] = np.ascontiguousarray(uk.transpose(1, 2, 0).reshape(8, 128, 256).transpose(1, 0, 2))
    f['consts'] = _constants()
    f['rope'] = _rope_tables()
    f['gains'] = np.stack([_cols(v, KD) for v in (I['norm_mix_a'][0], I['norm_ffn'][0], I['norm_mix_c'][0], I['norm_ffn'][1])], axis=1)
    cw = np.concatenate([I['conv_gdn_w'][0], I['conv_ssm_w'][0]], axis=1)
    f['convw'] = np.ascontiguousarray(cw.reshape(4, NCONV, 128).transpose(2, 1, 0))
    f['convb'] = _cols(np.concatenate([np.zeros(1536, np.float32), I['conv_ssm_b'][0]]), NCONV)
    sm = np.zeros((128, NSMALL), np.float32)
    sm[:, C_GDN] = I['gdn_norm'][0]
    sm[:, C_D:C_D + 4] = _cols(np.repeat(I['ssm_D'][0], 64), 4)
    sm[:, C_SSM:C_SSM + 4] = _cols(I['ssm_norm'][0], 4)
    sm[:, C_QA:C_QA + 4] = _cols(I['q_a_norm'][0], 4)
    sm[:, C_KVA:C_KVA + 2] = _cols(I['kv_a_norm'][0], 2)
    sm[0:QH, C_QN] = I['q_norm'][0]
    sm[0:RD, C_KR] = I['k_norm'][0][NOPE:]
    sm[:, C_EPS] = EPS
    sm[:, C_KN] = np.tile(I['k_norm'][0][:NOPE], 2)
    f['small'] = sm
    gc = np.concatenate([I['gdn_dt_bias'][0], I['ssm_dt_bias'][0], np.zeros(GH, np.float32), I['gdn_A_log'][0], I['ssm_A_log'][0]])
    f['gatec'] = np.ascontiguousarray(np.broadcast_to(gc, (128, NGATE + NDEC)))
    pv = np.concatenate([I['state_gdn_conv'][0], I['state_ssm_conv'][0]], axis=2)
    f['prev'] = np.ascontiguousarray(pv.reshape(NS, 3, NCONV, 128).transpose(3, 2, 1, 0))
    f['s_gdn'] = np.ascontiguousarray(I['state_gdn'][0].transpose(2, 1, 0, 3))
    f['s_ssm'] = np.ascontiguousarray(I['state_ssm'][0].transpose(3, 0, 1, 2)).reshape(128, NS, 512)
    f['page_table'] = np.ascontiguousarray(I['page_table'].reshape(1, NS * NPG))
    cm = I['cache_mla'][0]
    pages = np.zeros((NPOOL, 128, PROW), np.float32)
    pages[:, :, 0:256] = cm[:, :, 0:256]
    pages[:, :, 256:512] = cm[:, :, 0:256].reshape(NPOOL, 128, 2, 128).transpose(0, 3, 2, 1).reshape(NPOOL, 128, 256)
    pages[:, 0:48, 512:640] = cm[:, :, 256:304].transpose(0, 2, 1)
    f['pages'] = pages

    nc = _bacc.Bacc("TRN2", target_bir_lowering=False, num_devices=1)
    arrays, A, O = {}, {}, {}
    for n, a in f.items():
        arrays[f"in_{n}"] = a
        A[n] = nc.dram_tensor(f"in_{n}", a.shape, mybir.dt.from_np(a.dtype), kind="ExternalInput").ap()
    outs = {'y': (128, KD, TOK), 'p_gdn': (128, 512), 'p_ssm': (128, 512), 'conv_p': (128, NCONV, 3), 'conv_s': (128, NCONV, 3, NS),
            's_gdn': (128, GH, NS, 128), 's_ssm': (128, NS, 512), 'rows_c': (128, 2, TOK), 'rows_k': (RD, TOK), 'rows_r': (16, TOK)}
    for n, shape in outs.items():
        O[n] = nc.dram_tensor(f"out_{n}", shape, F32, kind="ExternalOutput").ap()
    build(nc, A, O)
    r = _run(nc, [arrays], core_ids=[0]).results[0]
    g = {n: np.asarray(r[f"out_{n}"]) for n in outs}
    y = g['y'].transpose(1, 0, 2).reshape(D, TOK).T
    y_prompt, y_sample = y[None, :T], y[T:, None]
    p_gdn = g['p_gdn'].reshape(128, GH, 128).transpose(1, 0, 2)[None, None]
    s_gdn = g['s_gdn'].transpose(2, 1, 0, 3)[None]
    p_ssm = g['p_ssm'].reshape(128, SH, 64).transpose(1, 2, 0)[None, None]
    s_ssm = g['s_ssm'].reshape(128, NS, SH, 64).transpose(1, 2, 3, 0)[None]
    cp = g['conv_p'].transpose(2, 1, 0).reshape(3, NCONV * 128)
    cs = g['conv_s'].transpose(3, 2, 1, 0).reshape(NS, 3, NCONV * 128)
    rows = np.concatenate([g['rows_c'].transpose(1, 0, 2).reshape(256, TOK), g['rows_k'], g['rows_r']], axis=0).T
    out = (y_prompt, y_sample, p_gdn, cp[None, None, :, :1536], p_ssm, cp[None, None, :, 1536:], rows[None, None, :T],
           s_gdn, cs[None, :, :, :1536], s_ssm, cs[None, :, :, 1536:], rows[None, T:, None])
    return tuple(np.ascontiguousarray(o) for o in out)
```
